# Optimizing a Trainium2 kernel written in Bass

```python
import math
import jax, jax.numpy as jnp
from jax import lax
import numpy as np

D_MODEL = 1024
BATCH = 1
SEQ = 256
DEPTH = 1
DEC_BATCH = 1
DEC_SEQ = 512
PAST_LEN = 128

GRID_W = 64
N_HEADS = 16
N_KV_HEADS = 4
HEAD_DIM = 64
ATTN_Q_WIDTH = N_HEADS * HEAD_DIM
ATTN_KV_WIDTH = N_KV_HEADS * HEAD_DIM
ROPE_THETA = 10000.0
Q_BLOCK = 128
SG_WIDTH = 1024
SG_GROUPS = 8
SG_GROUP_DIM = SG_WIDTH // SG_GROUPS
SG_CHUNK = 128
N_BRANCHES = 2
IN_SPLITS = (ATTN_Q_WIDTH,
             ATTN_Q_WIDTH + ATTN_KV_WIDTH,
             ATTN_Q_WIDTH + 2 * ATTN_KV_WIDTH,
             ATTN_Q_WIDTH + 2 * ATTN_KV_WIDTH + 2 * SG_WIDTH)
IN_WIDTH = ATTN_Q_WIDTH + 2 * ATTN_KV_WIDTH + 2 * SG_WIDTH + N_BRANCHES * D_MODEL
N_MEM = 256
XA_HEADS = 4
XA_HEAD_DIM = D_MODEL // XA_HEADS
PEER_HEADS = 8
PEER_N_KEYS = 128
PEER_N_EXPERTS = PEER_N_KEYS * PEER_N_KEYS
PEER_D_KEY = 256
PEER_HALF = PEER_D_KEY // 2
PEER_TOPK = 16
PEER_TOKEN_BLOCK = 128
EPS = 1e-6

kernel_name = 'hybrid_gqa_sgu_peer_encoder'

def rmsnorm(x, g):
    x32 = x.astype(jnp.float32)
    y = x32 * lax.rsqrt(jnp.mean(x32 * x32, axis=-1, keepdims=True) + EPS)
    return (y * g.astype(jnp.float32)).astype(x.dtype)

def axial_rope_tables(n_tokens):
    rows = n_tokens // GRID_W
    row_pos = jnp.repeat(jnp.arange(rows, dtype=jnp.float32), GRID_W)
    col_pos = jnp.tile(jnp.arange(GRID_W, dtype=jnp.float32), rows)
    n_freq = HEAD_DIM // 4
    inv_freq = ROPE_THETA ** (-jnp.arange(n_freq, dtype=jnp.float32) / n_freq)
    ang_r = row_pos[:, None] * inv_freq[None, :]
    ang_c = col_pos[:, None] * inv_freq[None, :]
    return jnp.cos(ang_r), jnp.sin(ang_r), jnp.cos(ang_c), jnp.sin(ang_c)

def _rotate(x, cos, sin):
    x1, x2 = jnp.split(x, 2, axis=-1)
    c = cos[None, :, None, :]
    s = sin[None, :, None, :]
    return jnp.concatenate([x1 * c - x2 * s, x2 * c + x1 * s], axis=-1)

def apply_axial_rope(x, cos_r, sin_r, cos_c, sin_c):
    x32 = x.astype(jnp.float32)
    xr, xc = jnp.split(x32, 2, axis=-1)
    out = jnp.concatenate([_rotate(xr, cos_r, sin_r), _rotate(xc, cos_c, sin_c)], axis=-1)
    return out.astype(x.dtype)

def block_attention(q, k, v):
    B, S = q.shape[0], q.shape[1]
    n_blk = S // Q_BLOCK
    grp = N_HEADS // N_KV_HEADS
    scale = 1.0 / math.sqrt(HEAD_DIM)
    qb = q.reshape(B, n_blk, Q_BLOCK, N_KV_HEADS, grp, HEAD_DIM).transpose(1, 0, 3, 4, 2, 5)

    def one_block(q_blk):
        s = jnp.einsum('bkgqd,bskd->bkgqs', q_blk, k).astype(jnp.float32) * scale
        p = jax.nn.softmax(s, axis=-1).astype(v.dtype)
        return jnp.einsum('bkgqs,bskd->bkgqd', p, v)

    o = lax.map(one_block, qb)
    return o.transpose(1, 0, 4, 2, 3, 5).reshape(B, S, ATTN_Q_WIDTH)

def spatial_gating(z, norm_g, w_s, b_s):
    B, S = z.shape[0], z.shape[1]
    u, v = jnp.split(z, 2, axis=-1)
    v = rmsnorm(v, norm_g)
    vc = v.reshape(B, S // SG_CHUNK, SG_CHUNK, SG_GROUPS, SG_GROUP_DIM)
    sv = jnp.einsum('gpq,bnqgc->bnpgc', w_s, vc) + b_s.T[:, :, None]
    return u * sv.reshape(B, S, SG_WIDTH)

def cross_attention(h, mem_n, wq, wkv, wo):
    B, S = h.shape[0], h.shape[1]
    M = mem_n.shape[1]
    q = (h @ wq).reshape(B, S, XA_HEADS, XA_HEAD_DIM)
    k, v = jnp.split(mem_n @ wkv, 2, axis=-1)
    k = k.reshape(B, M, XA_HEADS, XA_HEAD_DIM)
    v = v.reshape(B, M, XA_HEADS, XA_HEAD_DIM)
    s = jnp.einsum('bshd,bmhd->bhsm', q, k).astype(jnp.float32) * (1.0 / math.sqrt(XA_HEAD_DIM))
    p = jax.nn.softmax(s, axis=-1).astype(v.dtype)
    o = jnp.einsum('bhsm,bmhd->bshd', p, v).reshape(B, S, D_MODEL)
    return o @ wo

def peer_ffn(h, w_q, sub_k1, sub_k2, e_down, e_up):
    B, S, D = h.shape
    n_tok = B * S
    hb = h.reshape(n_tok // PEER_TOKEN_BLOCK, PEER_TOKEN_BLOCK, D)

    def one_block(xb):
        n = xb.shape[0]
        q = (xb @ w_q).reshape(n, PEER_HEADS, PEER_D_KEY)
        q1, q2 = jnp.split(q, 2, axis=-1)
        s1 = jnp.einsum('nhd,hkd->nhk', q1, sub_k1).astype(jnp.float32)
        s2 = jnp.einsum('nhd,hkd->nhk', q2, sub_k2).astype(jnp.float32)
        v1, i1 = lax.top_k(s1, PEER_TOPK)
        v2, i2 = lax.top_k(s2, PEER_TOPK)
        cand = (v1[..., :, None] + v2[..., None, :]).reshape(n, PEER_HEADS, PEER_TOPK * PEER_TOPK)
        top_s, top_c = lax.top_k(cand, PEER_TOPK)
        e1 = jnp.take_along_axis(i1, top_c // PEER_TOPK, axis=-1)
        e2 = jnp.take_along_axis(i2, top_c % PEER_TOPK, axis=-1)
        idx = e1 * PEER_N_KEYS + e2
        g = jax.nn.softmax(top_s, axis=-1).astype(xb.dtype)
        act = jax.nn.gelu(jnp.einsum('nhkd,nd->nhk', e_down[idx], xb))
        return jnp.einsum('nhk,nhkd->nd', g * act, e_up[idx])

    return lax.map(one_block, hb).reshape(B, S, D)

def encoder_layer(x, mem, norm_mix_g, w_in, q_norm_g, k_norm_g, sg_norm_g, sg_w, sg_b,
                  w_attn_o, w_sg_o, w_out, norm_xa_g, norm_mem_g, wq_xa, wkv_xa, wo_xa,
                  norm_ffn_g, w_peer_q, peer_k1, peer_k2, expert_down, expert_up):
    B, S = x.shape[0], x.shape[1]
    h = rmsnorm(x, norm_mix_g)
    proj = h @ w_in
    q, k, v, z_sg, gate_logits = jnp.split(proj, IN_SPLITS, axis=-1)
    q = rmsnorm(q.reshape(B, S, N_HEADS, HEAD_DIM), q_norm_g)
    k = rmsnorm(k.reshape(B, S, N_KV_HEADS, HEAD_DIM), k_norm_g)
    v = v.reshape(B, S, N_KV_HEADS, HEAD_DIM)
    cos_r, sin_r, cos_c, sin_c = axial_rope_tables(S)
    q = apply_axial_rope(q, cos_r, sin_r, cos_c, sin_c)
    k = apply_axial_rope(k, cos_r, sin_r, cos_c, sin_c)
    attn_branch = block_attention(q, k, v) @ w_attn_o
    sg_branch = spatial_gating(jax.nn.gelu(z_sg), sg_norm_g, sg_w, sg_b) @ w_sg_o
    g_attn, g_sg = jnp.split(jax.nn.sigmoid(gate_logits), N_BRANCHES, axis=-1)
    x = x + (g_attn * attn_branch + g_sg * sg_branch) @ w_out
    x = x + cross_attention(rmsnorm(x, norm_xa_g), rmsnorm(mem, norm_mem_g), wq_xa, wkv_xa, wo_xa)
    x = x + peer_ffn(rmsnorm(x, norm_ffn_g), w_peer_q, peer_k1, peer_k2, expert_down, expert_up)
    return x

def setup_inputs(seed: int = 0) -> dict:
    key = jax.random.key(seed)
    ks = jax.random.split(key, 32)
    f32 = jnp.float32

    def nrm(k, shape, scale):
        return jax.random.normal(k, shape, dtype=f32) * scale

    def gain(k, shape):
        return 1.0 + 0.02 * jax.random.normal(k, shape, dtype=f32)

    return {
        'x_prompt': nrm(ks[0], (BATCH, SEQ, D_MODEL), 1.0),
        'x_sample': nrm(ks[1], (DEC_BATCH, DEC_SEQ, D_MODEL), 1.0),
        'mem_prompt': nrm(ks[2], (BATCH, N_MEM, D_MODEL), 1.0),
        'mem_sample': nrm(ks[3], (DEC_BATCH, N_MEM, D_MODEL), 1.0),
        'norm_mix_g': gain(ks[4], (DEPTH, D_MODEL)),
        'w_in': nrm(ks[5], (DEPTH, D_MODEL, IN_WIDTH), D_MODEL ** -0.5),
        'q_norm_g': gain(ks[6], (DEPTH, HEAD_DIM)),
        'k_norm_g': gain(ks[7], (DEPTH, HEAD_DIM)),
        'sg_norm_g': gain(ks[8], (DEPTH, SG_WIDTH)),
        'sg_w': nrm(ks[9], (DEPTH, SG_GROUPS, SG_CHUNK, SG_CHUNK), 0.5 * SG_CHUNK ** -0.5),
        'sg_b': 1.0 + nrm(ks[10], (DEPTH, SG_GROUPS, SG_CHUNK), 0.1),
        'w_attn_o': nrm(ks[11], (DEPTH, ATTN_Q_WIDTH, D_MODEL), ATTN_Q_WIDTH ** -0.5),
        'w_sg_o': nrm(ks[12], (DEPTH, SG_WIDTH, D_MODEL), SG_WIDTH ** -0.5),
        'w_out': nrm(ks[13], (DEPTH, D_MODEL, D_MODEL), D_MODEL ** -0.5),
        'norm_xa_g': gain(ks[14], (DEPTH, D_MODEL)),
        'norm_mem_g': gain(ks[15], (DEPTH, D_MODEL)),
        'wq_xa': nrm(ks[16], (DEPTH, D_MODEL, D_MODEL), D_MODEL ** -0.5),
        'wkv_xa': nrm(ks[17], (DEPTH, D_MODEL, 2 * D_MODEL), D_MODEL ** -0.5),
        'wo_xa': nrm(ks[18], (DEPTH, D_MODEL, D_MODEL), D_MODEL ** -0.5),
        'norm_ffn_g': gain(ks[19], (DEPTH, D_MODEL)),
        'w_peer_q': nrm(ks[20], (DEPTH, D_MODEL, PEER_HEADS * PEER_D_KEY), D_MODEL ** -0.5),
        'peer_k1': nrm(ks[21], (DEPTH, PEER_HEADS, PEER_N_KEYS, PEER_HALF), PEER_HALF ** -0.5),
        'peer_k2': nrm(ks[22], (DEPTH, PEER_HEADS, PEER_N_KEYS, PEER_HALF), PEER_HALF ** -0.5),
        'expert_down': nrm(ks[23], (DEPTH, PEER_N_EXPERTS, D_MODEL), D_MODEL ** -0.5),
        'expert_up': nrm(ks[24], (DEPTH, PEER_N_EXPERTS, D_MODEL), 0.5),
        'final_norm_g': gain(ks[25], (D_MODEL,)),
    }

def reference(x_prompt, x_sample, mem_prompt, mem_sample, norm_mix_g, w_in, q_norm_g, k_norm_g,
              sg_norm_g, sg_w, sg_b, w_attn_o, w_sg_o, w_out, norm_xa_g, norm_mem_g, wq_xa, wkv_xa,
              wo_xa, norm_ffn_g, w_peer_q, peer_k1, peer_k2, expert_down, expert_up, final_norm_g):
    xp = x_prompt
    xs = x_sample
    for l in range(DEPTH):
        params = (norm_mix_g[l], w_in[l], q_norm_g[l], k_norm_g[l], sg_norm_g[l], sg_w[l], sg_b[l],
                  w_attn_o[l], w_sg_o[l], w_out[l], norm_xa_g[l], norm_mem_g[l], wq_xa[l], wkv_xa[l],
                  wo_xa[l], norm_ffn_g[l], w_peer_q[l], peer_k1[l], peer_k2[l], expert_down[l],
                  expert_up[l])
        xp = encoder_layer(xp, mem_prompt, *params)
        xs = encoder_layer(xs, mem_sample, *params)
    y_prompt = rmsnorm(xp, final_norm_g)
    y_sample = rmsnorm(xs, final_norm_g)
    return (y_prompt, y_sample)


_drawn_inputs = setup_inputs


def setup_inputs(seed=0):
    import zlib

    import numpy as np

    out = dict(_drawn_inputs(seed))
    spreads = {}
    factors = {'q_norm_g': 5.885,
     'k_norm_g': 6.486,
     'sg_norm_g': 3.93,
     'norm_xa_g': 5.134,
     'norm_mem_g': 4.058,
     'final_norm_g': 7.861,
     'norm_ffn_g': 5.814}
    for name, (base, spread) in spreads.items():
        noise = np.random.default_rng([zlib.crc32(name.encode()), seed]).standard_normal(out[name].shape)
        drawn = base * np.exp(spread * noise) if base else spread * noise
        out[name] = __import__('jax').numpy.asarray(drawn.astype(out[name].dtype))
    for name, factor in factors.items():
        out[name] = (out[name] * factor).astype(out[name].dtype)
    return out
```

```python
from contextlib import ExitStack

import numpy as np

import concourse.bass as bass
from concourse import mybir

F32 = mybir.dt.float32
F32R = mybir.dt.float32r
I32 = mybir.dt.int32
U32 = mybir.dt.uint32
ALU = mybir.AluOpType
ACT = mybir.ActivationFunctionType
AX_X = mybir.AxisListType.X

P = 128
D = 1024
KB = D // P
CH = 512
HK = KB // 2
SAMPLE, PROMPT = 512, 256
SEQS = [(0, SAMPLE // P), (SAMPLE // P, PROMPT // P)]
NT = (SAMPLE + PROMPT) // P
TOK = NT * P
NH, NKV, HD = 16, 4, 64
MEM = 256
XH, XD = 4, 256
NSEQ = 2
NM = NSEQ * MEM // P
G_SG = 8
PH, NK, TOPK = 8, 128, 16
NE = PH * TOPK
EPS = 1e-6
LOWEST = -3.4e38
GATHERS = 16

W_KV, W_Q, W_U, W_VS, W_GA, W_GS = 0, 1, 3, 5, 7, 9
W_AO, W_SO, W_OUT, W_XKV, W_XQ, W_XO, W_PQ, W_END = 11, 13, 15, 17, 21, 23, 25, 29


class Pool:

    semaphores = None
    shared = {}

    @classmethod
    def begin(cls, ctx):
        cls.semaphores, cls.shared = ctx, {}

    def carried(self, name, increments):
        if name not in Pool.shared:
            Pool.shared[name] = [self.sem(name), 0]
        sem, base = Pool.shared[name]
        Pool.shared[name][1] = base + increments
        return sem, base

    def __init__(self, nc, ctx):
        self.nc, self.ctx = nc, ctx

    def sb(self, name, shape, dt=F32):
        return self.ctx.enter_context(self.nc.sbuf_tensor(name, shape, dt))

    def sem(self, name):
        return Pool.semaphores.enter_context(self.nc.semaphore(name))


class Stream:

    def __init__(self, nc, ctx, tag, wall, chunks):
        self.wall, self.chunks = wall, chunks
        self.n = 2 * len(chunks)
        m = Pool(nc, ctx)
        self.raw = m.sb(f"w_raw_{tag}", [P, 2, HK, CH])
        self.hi = m.sb(f"w_hi_{tag}", [P, 2, HK, CH], F32R)
        self.lo = m.sb(f"w_lo_{tag}", [P, 2, HK, CH], F32R)
        self.loaded = [m.carried(f"w_loaded{i}", 0)[0] for i in range(2)]
        self.hi_done, self.base = m.carried("w_hi_done", self.n)
        self.lo_done, _ = m.carried("w_lo_done", self.n)
        self.used, _ = m.carried("w_used", 0)

    def load(self, sp):
        for h in range(self.n):
            if h >= 2:
                sp.wait_ge(self.lo_done, self.base + h - 1)
            sp.dma_start(self.raw[:, h % 2], self.wall[self.chunks[h // 2], :, h % 2]).then_inc(
                self.loaded[h % 2], 16)

    def split_hi(self, act, h):
        if h >= self.n:
            return
        act.wait_ge(self.loaded[h % 2], 16 * ((self.base + h) // 2 + 1))
        if h >= 2 and h % 2 == 0:
            act.wait_ge(self.used, (self.base + h) // 2)
        act.activation(self.hi[:, h % 2], self.raw[:, h % 2], ACT.Copy).then_inc(self.hi_done, 1)

    def split_lo(self, dve, h):
        if h >= self.n:
            return
        dve.wait_ge(self.hi_done, self.base + h + 1)
        dve.tensor_tensor(self.lo[:, h % 2], self.raw[:, h % 2], self.hi[:, h % 2].bitcast(F32),
                          ALU.subtract).then_inc(self.lo_done, 1)


class Outputs:

    def __init__(self, nc, ctx, tag):
        m = Pool(nc, ctx)
        self.ready = m.sem(f"{tag}_ready")
        self.freed = m.sem(f"{tag}_freed")


def three(pe, out, lhs, rhs, start, stop):
    pe.matmul(out, lhs[0], rhs[0], start=start, stop=False, skip_group_check=True)
    pe.matmul(out, lhs[0], rhs[1], start=False, stop=False, skip_group_check=True)
    return pe.matmul(out, lhs[1], rhs[0], start=False, stop=stop, skip_group_check=True)


def project_tokens(pe, st, h0, nchunks, T, tiles, lin, o, between=None):
    n = len(tiles)
    for c in range(nchunks):
        for half in range(2):
            h = h0 + 2 * c + half
            pe.wait_ge(st.lo_done, st.base + h + 1)
            for i, t in enumerate(tiles):
                if half == 0 and c > 0:
                    pe.wait_ge(o.freed, n * (c - 1) + i + 1)
                for k in range(HK):
                    cols = slice(t * P, (t + 1) * P)
                    kk = half * HK + k
                    last = three(pe, lin[:, i, :], (T[0][:, kk, cols], T[1][:, kk, cols]),
                                 (st.hi[:, h % 2, k, :], st.lo[:, h % 2, k, :]),
                                 start=(kk == 0), stop=(kk == KB - 1))
                if half == 1:
                    last.then_inc(o.ready, 1)
                elif i == n - 1:
                    last.then_inc(st.used, 1)
                if half == 0 and between is not None:
                    between(c, i)


def project_features(pe, st, h0, nchunks, T, groups, lin, o, per, between=None):
    n = len(groups)
    for c in range(nchunks):
        for half in range(2):
            h = h0 + 2 * c + half
            pe.wait_ge(st.lo_done, st.base + h + 1)
            for i, (bank, col, first, cb, cols, need) in enumerate(groups):
                if half == 0 and c > 0:
                    pe.wait_ge(o.freed, n * (c - 1) + need)
                for k in range(HK):
                    kk = half * HK + k
                    fs = slice(cb * P, (cb + 1) * P)
                    last = three(pe, lin[:, bank, col:col + cols.stop - cols.start],
                                 (st.hi[:, h % 2, k, fs], st.lo[:, h % 2, k, fs]),
                                 (T[0][:, kk, cols], T[1][:, kk, cols]),
                                 start=(kk == 0 and first), stop=(kk == KB - 1))
                if half == 1:
                    last.then_inc(o.ready, 1)
                elif i == n - 1:
                    last.then_inc(st.used, 1)
                if between is not None:
                    between(c, half, i)


FEATURES = [(cb, 0, True, cb, slice(0, SAMPLE), cb + 1) for cb in range(4)] + [
    (4 + cb // 2, (cb % 2) * PROMPT, cb % 2 == 0, cb, slice(SAMPLE, TOK), 6 if cb < 2 else 8)
    for cb in range(4)]


class Turn:

    def __init__(self, nc, ctx, tag, src, T, lin, ident, gain, tiles):
        m = Pool(nc, ctx)
        self.src, self.T, self.lin, self.ident, self.gain = src, T, lin, ident, gain
        self.steps = [(k, t0, min(4, tiles - t0)) for k in range(KB) for t0 in range(0, tiles, 4)]
        (self.turned, self.base), (self.hi, _), (self.lo, _) = (
            m.carried(x, len(self.steps)) for x in ("turned", "turn_hi", "turn_lo"))

    def pe(self, pe):
        for n, (k, t0, nt) in enumerate(self.steps):
            if n >= 6:
                pe.wait_ge(self.lo, self.base + n - 5)
            for t in range(nt):
                last = pe.transpose(self.lin[:, n % 6, t * P:(t + 1) * P],
                                    self.src[:, t0 + t, k * P:(k + 1) * P], self.ident[:])
            last.then_inc(self.turned, 1)

    def act(self, act):
        for n, (k, t0, nt) in enumerate(self.steps):
            act.wait_ge(self.turned, self.base + n + 1)
            scale = 1.0 if self.gain is None else self.gain[:, k:k + 1]
            act.activation(self.T[0][:, k, t0 * P:(t0 + nt) * P], self.lin[:, n % 6, 0:nt * P], ACT.Copy,
                           scale=scale).then_inc(self.hi, 1)

    def dve(self, dve):
        for n, (k, t0, nt) in enumerate(self.steps):
            dve.wait_ge(self.hi, self.base + n + 1)
            scale = 1.0 if self.gain is None else self.gain[:, k:k + 1]
            cols = slice(t0 * P, (t0 + nt) * P)
            dve.scalar_tensor_tensor(out=self.T[1][:, k, cols], in0=self.lin[:, n % 6, 0:nt * P], scalar=scale,
                                     in1=self.T[0][:, k, cols].bitcast(F32), op0=ALU.mult,
                                     op1=ALU.subtract).then_inc(self.lo, 1)

    def wait(self, eng):
        eng.wait_ge(self.lo, self.base + len(self.steps))


class Norm:

    def __init__(self, nc, ctx, tag, src, tiles):
        m = Pool(nc, ctx)
        self.src, self.tiles = src, tiles
        self.junk = m.sb(f"{tag}_squares", [P, D])
        self.ss, self.ms, self.sd, self.rstd = (m.sb(f"{tag}_{x}", [P, tiles]) for x in ("ss", "ms", "sd", "rstd"))
        (self.summed, self.base), (self.scaled, _) = (m.carried(f"norm_{x}", tiles) for x in ("summed", "scaled"))
        (self.meaned, self.use), (self.rooted, _), (self.inverted, _) = (
            m.carried(f"norm_{x}", 1) for x in ("meaned", "rooted", "inverted"))

    def act(self, act, before=None):
        for t in range(self.tiles):
            if before is not None:
                before(t)
            if t > 0:
                act.wait_ge(self.summed, self.base + t)
            act.activation(self.junk[:], self.src[:, t, :], ACT.Square,
                           accum_out=self.ss[:, t:t + 1]).then_inc(self.summed, 1)
        act.wait_ge(self.meaned, self.use + 1)
        act.activation(self.sd[:], self.ms[:], ACT.Sqrt).then_inc(self.rooted, 1)

    def dve(self, dve, dst, row=None):
        dve.wait_ge(self.summed, self.base + self.tiles)
        dve.tensor_scalar(self.ms[:], self.ss[:], 1.0 / D, EPS, ALU.mult, ALU.add).then_inc(self.meaned, 1)
        dve.wait_ge(self.rooted, self.use + 1)
        dve.reciprocal(self.rstd[:], self.sd[:]).then_inc(self.inverted, 1)
        dve.wait_ge(self.inverted, self.use + 1)
        for t in range(self.tiles):
            if row is None:
                dve.tensor_scalar(dst[:, t, :], self.src[:, t, :], self.rstd[:, t:t + 1], None,
                                  ALU.mult).then_inc(self.scaled, 1)
            else:
                dve.scalar_tensor_tensor(out=dst[:, t, :], in0=self.src[:, t, :], scalar=self.rstd[:, t:t + 1],
                                         in1=row[:], op0=ALU.mult, op1=ALU.mult).then_inc(self.scaled, 1)

    def wait(self, eng):
        eng.wait_ge(self.scaled, self.base + self.tiles)


def mixer_inputs(nc, m, T, Y, qT, kT, v_sb, lin, tr, A, U, GA, GS, ident):
    with ExitStack() as ctx:
        mm = Pool(nc, ctx)
        st = Stream(nc, ctx, "in", A["wall"], list(range(W_KV, W_AO)))
        norm = Norm(nc, ctx, "mix", Y, NT)
        gains = mm.sb("mix_gain", [P, KB])
        turn = Turn(nc, ctx, "mix", Y, T, lin, ident, gains, NT)
        cos, sin = mm.sb("cos", [P, 4, HD]), mm.sb("sin", [P, 4, HD])
        qg, kg = mm.sb("qg", [P, HD]), mm.sb("kg", [P, HD])
        gcos, gsin = mm.sb("gcos", [P, 2, 4, HD]), mm.sb("gsin", [P, 2, 4, HD])
        sq = mm.sb("sq", [P, 2, CH])
        hss, hms, hsd, hr = (mm.sb(x, [P, 2, 8]) for x in ("hss", "hms", "hsd", "hr"))
        qn, ra, rb = mm.sb("qn", [P, CH]), mm.sb("ra", [P, CH]), mm.sb("rb", [P, CH])
        rope = mm.sb("rope", [P, 2, CH])
        STG = 4
        stage = mm.sb("stage", [P, STG, CH])
        x_in = [mm.sem(f"x_in{t}") for t in range(NT)]
        small_in, table_done = mm.sem("small_in"), mm.sem("table_done")
        o = Outputs(nc, ctx, "in")
        sq_done, hs_done, ms_done, sd_done, hr_done = (mm.sem(x) for x in ("sq_done", "hs_done", "hms_done", "hsd_done", "hr_done"))
        part, roped, turned, copied = (mm.sem(x) for x in ("rope_part", "roped", "qk_turned", "qk_copied"))
        spilled = [mm.sem(f"spilled{i}") for i in range(STG)]
        NQ = 3 * NT
        NALL = 11 * NT
        spills = [n for n in range(NQ, NALL) if not 5 * NT <= n < 7 * NT]

        def wait_odd(eng, h):
            if h >= 2 and h % 2 == 1 and h < st.n:
                eng.wait_ge(o.ready, NT * (h // 2))

        with nc.Block() as block:
            @block.sync
            def _(sp):
                for t in range(NT):
                    sp.dma_start(Y[:, t, :], A["x"][t * P:(t + 1) * P, :]).then_inc(x_in[t], 16)
                st.load(sp)

            @block.gpsimd
            def _(pool):
                for dst, src in ((ident[:], A["ident"]), (gains[:], A["gains"][:, 0, :]), (cos[:], A["cos"]),
                                 (sin[:], A["sin"]), (qg[:], A["qg"].broadcast_to((P, HD))),
                                 (kg[:], A["kg"].broadcast_to((P, HD)))):
                    pool.dma_start(dst, src).then_inc(small_in, 16)
                for i, n in enumerate(spills):
                    c, t = n // NT, n % NT
                    dst = U if c < 5 else GA if c < 9 else GS
                    pool.wait_ge(o.freed, n + 1)
                    pool.dma_start(dst[t, :, (c + 1) % 2 * CH:((c + 1) % 2 + 1) * CH], stage[:, i % STG, :]).then_inc(
                        spilled[i % STG], 16)
                for i in range(STG):
                    pool.wait_ge(spilled[i], 16 * len(spills[i::STG]))

            @block.tensor
            def _(pe):
                pe.wait_ge(small_in, 96)
                norm.wait(pe)
                turn.pe(pe)
                turn.wait(pe)

                def qk_turn(n):
                    pe.wait_ge(roped, n + 1)
                    if n >= 2:
                        pe.wait_ge(copied, n - 1)
                    for b in range(4):
                        last = pe.transpose(tr[:, n % 2, b * P:(b + 1) * P], rope[:, n % 2, b * P:(b + 1) * P], ident[:])
                    last.then_inc(turned, 1)

                def between(c, i):
                    if 1 <= c <= 3:
                        qk_turn((c - 1) * NT + i)

                project_tokens(pe, st, 0, 11, T, range(NT), lin, o, between)

            @block.scalar
            def _(act):
                norm.act(act, before=lambda t: act.wait_ge(x_in[t], 16))
                st.split_hi(act, 0)
                st.split_hi(act, 1)
                act.wait_ge(small_in, 96)
                turn.act(act)

                def root(n):
                    act.wait_ge(ms_done, n + 1)
                    act.activation(hsd[:, n % 2, :], hms[:, n % 2, :], ACT.Sqrt).then_inc(sd_done, 1)

                def copy(n):
                    c, t = n // NT, n % NT
                    act.wait_ge(turned, n + 1)
                    src = tr[:, n % 2, :].rearrange("p (b f) -> p b f", b=4)
                    dst = (kT[:, :, t * P:(t + 1) * P] if c == 0 else
                           qT[:, 4 * (c - 1):4 * c, t * P:(t + 1) * P])
                    act.activation(dst, src, ACT.Copy).then_inc(copied, 1)

                for c in range(11):
                    if 1 <= c <= 3:
                        for t in range(NT):
                            copy((c - 1) * NT + t)
                    st.split_hi(act, 2 * c + 2)
                    for t in range(NT):
                        n = c * NT + t
                        act.wait_ge(o.ready, n + 1)
                        if n == NQ:
                            act.wait_ge(o.freed, NQ)
                        if n < NQ:
                            w = CH // 2 if c == 0 else CH
                            if c == 0:
                                act.activation(v_sb[:, t, :], lin[:, t, CH // 2:CH], ACT.Copy)
                            act.activation(sq[:, n % 2, 0:w], lin[:, t, 0:w], ACT.Square).then_inc(sq_done, 1)
                            if t >= 1:
                                root(n - 1)
                            if t == NT - 1:
                                root(n)
                        elif 5 <= c < 7:
                            act.activation(Y[:, t, (c - 5) * CH:(c - 4) * CH], lin[:, t, :],
                                           ACT.Gelu_apprx_tanh).then_inc(o.freed, 1)
                        else:
                            i = spills.index(n)
                            if i >= STG:
                                act.wait_ge(spilled[i % STG], 16 * (i // STG))
                            act.activation(stage[:, i % STG, :], lin[:, t, :],
                                           ACT.Gelu_apprx_tanh if c < 5 else ACT.Sigmoid).then_inc(o.freed, 1)
                    wait_odd(act, 2 * c + 3)
                    st.split_hi(act, 2 * c + 3)

            @block.vector
            def _(dve):
                norm.dve(dve, Y)
                st.split_lo(dve, 0)
                st.split_lo(dve, 1)
                dve.wait_ge(small_in, 96)
                turn.dve(dve)
                for j, g in enumerate((kg, qg)):
                    gb = g[:].unsqueeze(1).broadcast_to((P, 4, HD))
                    dve.tensor_tensor(gcos[:, j], cos[:], gb, ALU.mult).then_inc(table_done, 1)
                    gv = g[:].rearrange("p (a b f) -> p a b f", a=2, b=2)
                    sv = sin[:].rearrange("p n (a b f) -> p n a b f", a=2, b=2)
                    ov = gsin[:, j].rearrange("p n (a b f) -> p n a b f", a=2, b=2)
                    for b in range(2):
                        for a in range(2):
                            dve.tensor_tensor(ov[:, :, a, b, :], sv[:, :, a, b, :],
                                              gv[:, a, 1 - b, :].unsqueeze(1).broadcast_to((P, 4, 16)),
                                              ALU.mult).then_inc(table_done, 1)
                dve.wait_ge(table_done, 10)
                nparts = 0

                def rotate(n):
                    nonlocal nparts
                    c, t = n // NT, n % NT
                    nh = 4 if c == 0 else 8
                    w = nh * HD
                    pos = t if t < 4 else t - 4
                    j = 0 if c == 0 else 1
                    dve.wait_ge(sd_done, n + 1)
                    dve.reciprocal(hr[:, n % 2, :], hsd[:, n % 2, :]).then_inc(hr_done, 1)
                    dve.wait_ge(hr_done, n + 1)
                    src = lin[:, t, 0:w].rearrange("p (h f) -> p h f", h=nh)
                    r = hr[:, n % 2, 0:nh].unsqueeze(2).broadcast_to((P, nh, HD))
                    q = qn[:, 0:w].rearrange("p (h f) -> p h f", h=nh)
                    dve.tensor_tensor(q, src, r, ALU.mult).then_inc(o.freed, 1)
                    dve.wait_ge(o.freed, n + 1)
                    cb = gcos[:, j, pos].unsqueeze(1).broadcast_to((P, nh, HD))
                    dve.tensor_tensor(ra[:, 0:w].rearrange("p (h f) -> p h f", h=nh), q, cb, ALU.mult).then_inc(part, 1)
                    qv = qn[:, 0:w].rearrange("p (h a b f) -> p h a b f", h=nh, a=2, b=2)
                    bv = rb[:, 0:w].rearrange("p (h a b f) -> p h a b f", h=nh, a=2, b=2)
                    gv = gsin[:, j, pos].rearrange("p (a b f) -> p a b f", a=2, b=2)
                    for b in range(2):
                        sb = gv[:, :, b, :].unsqueeze(1).broadcast_to((P, nh, 2, 16))
                        dve.tensor_tensor(bv[:, :, :, b, :], qv[:, :, :, 1 - b, :], sb, ALU.mult).then_inc(part, 1)
                    nparts += 3
                    dve.wait_ge(part, nparts)
                    if n >= 2:
                        dve.wait_ge(turned, n - 1)
                    if c == 0:
                        for dup in range(2):
                            dst = rope[:, n % 2, :].rearrange("p (h u f) -> p h u f", h=nh, u=2)[:, :, dup, :]
                            last = dve.tensor_tensor(dst, ra[:, 0:w].rearrange("p (h f) -> p h f", h=nh),
                                                     rb[:, 0:w].rearrange("p (h f) -> p h f", h=nh), ALU.add)
                    else:
                        last = dve.tensor_tensor(rope[:, n % 2, :], ra[:], rb[:], ALU.add)
                    last.then_inc(roped, 1)
                    dve.wait_ge(roped, n + 1)

                for c in range(11):
                    st.split_lo(dve, 2 * c + 2)
                    for t in range(NT):
                        n = c * NT + t
                        if n < NQ:
                            nh = 4 if c == 0 else 8
                            dve.wait_ge(sq_done, n + 1)
                            if n == 0:
                                dve.memset(hss[:], 1.0).then_inc(hs_done, 1)
                                dve.wait_ge(hs_done, 1)
                            dve.tensor_reduce(hss[:, n % 2, 0:nh],
                                              sq[:, n % 2, 0:nh * HD].rearrange("p (h f) -> p h f", h=nh),
                                              AX_X, ALU.add).then_inc(hs_done, 1)
                            dve.wait_ge(hs_done, n + 2)
                            dve.tensor_scalar(hms[:, n % 2, :], hss[:, n % 2, :], 1.0 / HD, EPS, ALU.mult,
                                              ALU.add).then_inc(ms_done, 1)
                            if t >= 1:
                                rotate(n - 1)
                            if t == NT - 1:
                                rotate(n)
                    st.split_lo(dve, 2 * c + 3)



def attention(nc, tag, T, ident, lin, tr, units, heads, outs, width_of, scores_of, scale):
    with ExitStack() as ctx:
        m = Pool(nc, ctx)
        KMAX = max(width_of(u) for u in units)
        probs = m.sb(f"{tag}_probs", [P, 3, KMAX])
        pT = m.sb(f"{tag}_probsT", [P, 2, KMAX // P, SAMPLE])
        mx, nmx, rs, rr = (m.sb(f"{tag}_{x}", [P, 3]) for x in ("mx", "nmx", "rs", "rr"))
        scored, maxed, negated, exped, inverted, normed, turned, copied, summed, out_hi, out_lo = (
            m.sem(f"{tag}_{x}") for x in ("scored", "maxed", "negated", "exped", "inverted", "normed", "turned",
                                          "copied", "summed", "out_hi", "out_lo"))
        N = len(units)
        head_of = {(s, h): i for i, (s, h) in enumerate(heads)}
        last_unit = [max(u for u, x in enumerate(units) if x[:2] == sh) for sh in heads]
        prods_to_head = [sum(p["head"] <= i for p in outs) for i in range(len(heads))]
        banks = [(n + 1, p) for n, p in enumerate(outs) if p["ends"]]
        bank_step = [last_unit[p["head"]] + 5 for _, p in banks]

        with nc.Block() as block:
            @block.tensor
            def _(pe):
                def scores(u):
                    if u >= 3:
                        pe.wait_ge(exped, u - 2)
                    pairs = scores_of(units[u])
                    for i, (a, b) in enumerate(pairs):
                        last = pe.matmul(lin[:, u % 3, 0:width_of(units[u])], a, b, start=(i == 0),
                                         stop=(i == len(pairs) - 1))
                    last.then_inc(scored, 1)

                def turn(u):
                    pe.wait_ge(normed, u + 1)
                    if u >= 3:
                        pe.wait_ge(copied, u - 2)
                    for kb in range(width_of(units[u]) // P):
                        last = pe.transpose(lin[:, 3 + u % 3, kb * P:(kb + 1) * P],
                                            probs[:, u % 3, kb * P:(kb + 1) * P], ident[:])
                    last.then_inc(turned, 1)

                def values(i):
                    pe.wait_ge(copied, last_unit[i] + 1)
                    for p in (p for p in outs if p["head"] == i):
                        if p["opens"] and p["bank"] >= 2:
                            pe.wait_ge(out_lo, p["bank"] - 1)
                        w = p["cols"].stop - p["cols"].start
                        for kb, v in enumerate(p["values"]):
                            last = pe.matmul(tr[p["rows"], p["bank"] % 2, 0:w], v, pT[:, i % 2, kb, 0:w],
                                             start=(kb == 0), stop=(kb == len(p["values"]) - 1))
                        last.then_inc(summed, 1)

                done = 0
                for step in range(N + 4):
                    if step < N:
                        scores(step)
                    if 2 <= step < N + 2:
                        turn(step - 2)
                    while done < len(heads) and last_unit[done] <= step - 3:
                        values(done)
                        done += 1

            @block.scalar
            def _(act):
                def exp(u):
                    w = width_of(units[u])
                    act.wait_ge(negated, u + 1)
                    if u >= 3:
                        act.wait_ge(turned, u - 2)
                    act.activation(probs[:, u % 3, 0:w], lin[:, u % 3, 0:w], ACT.Exp, bias=nmx[:, u % 3:u % 3 + 1],
                                   scale=scale, accum_out=rs[:, u % 3:u % 3 + 1]).then_inc(exped, 1)

                def copy(u):
                    s, h, t = units[u]
                    i = head_of[s, h]
                    kbs = width_of(units[u]) // P
                    act.wait_ge(turned, u + 1)
                    if i >= 2 and t == 0:
                        act.wait_ge(summed, prods_to_head[i - 2])
                    act.activation(pT[:, i % 2, 0:kbs, t * P:(t + 1) * P],
                                   lin[:, 3 + u % 3, 0:kbs * P].rearrange("p (k q) -> p k q", k=kbs),
                                   ACT.Copy).then_inc(copied, 1)

                for step in range(N + 6):
                    if step < N:
                        exp(step)
                    if 3 <= step < N + 3:
                        copy(step - 3)
                    for n, (prods, p) in enumerate(banks):
                        if bank_step[n] == step:
                            act.wait_ge(summed, prods)
                            act.activation(T[0][:, p["block"], p["cols"]],
                                           tr[:, n % 2, 0:p["cols"].stop - p["cols"].start], ACT.Copy).then_inc(out_hi, 1)

            @block.vector
            def _(dve):
                def norm(u):
                    w = width_of(units[u])
                    i = u % 3
                    dve.wait_ge(exped, u + 1)
                    dve.reciprocal(rr[:, i:i + 1], rs[:, i:i + 1]).then_inc(inverted, 1)
                    dve.wait_ge(inverted, u + 1)
                    dve.tensor_scalar(probs[:, i, 0:w], probs[:, i, 0:w], rr[:, i:i + 1], None,
                                      ALU.mult).then_inc(normed, 1)

                for step in range(N + 6):
                    if step < N:
                        w = width_of(units[step])
                        i = step % 3
                        dve.wait_ge(scored, step + 1)
                        dve.reduce_max(mx[:, i:i + 1], lin[:, i, 0:w], AX_X).then_inc(maxed, 1)
                        dve.wait_ge(maxed, step + 1)
                        dve.tensor_scalar(nmx[:, i:i + 1], mx[:, i:i + 1], -scale, None, ALU.mult).then_inc(negated, 1)
                    if 1 <= step < N + 1:
                        norm(step - 1)
                    for n, (prods, p) in enumerate(banks):
                        if bank_step[n] == step:
                            cols = p["cols"]
                            dve.wait_ge(out_hi, n + 1)
                            dve.tensor_tensor(T[1][:, p["block"], cols], tr[:, n % 2, 0:cols.stop - cols.start],
                                              T[0][:, p["block"], cols].bitcast(F32), ALU.subtract).then_inc(out_lo, 1)


def self_attention(nc, T, qT, kT, v_sb, ident, lin, tr):
    heads = [(s, h) for s in range(NSEQ) for h in range(NH)]
    units = [(s, h, t) for s, h in heads for t in range(SEQS[s][1])]
    span = lambda s: slice(SEQS[s][0] * P, sum(SEQS[s]) * P)
    kv_of = lambda h: h // (NH // NKV)

    def scores_of(u):
        s, h, t = u
        t0 = SEQS[s][0]
        rows = slice(h % 2 * HD, (h % 2 + 1) * HD)
        return [(qT[rows, h // 2, (t0 + t) * P:(t0 + t + 1) * P], kT[rows, kv_of(h), span(s)])]

    outs = [{"head": i, "bank": i // 2, "rows": slice(h % 2 * HD, (h % 2 + 1) * HD), "opens": h % 2 == 0,
             "ends": h % 2 == 1, "block": h // 2, "cols": span(s),
             "values": [v_sb[:, t, kv_of(h) * HD:(kv_of(h) + 1) * HD] for t in range(SEQS[s][0], sum(SEQS[s]))]}
            for i, (s, h) in enumerate(heads)]
    attention(nc, "att", T, ident, lin, tr, units, heads, outs, lambda u: SEQS[u[0]][1] * P, scores_of, HD ** -0.5)


def mixer_outputs(nc, T, Y, G, lin, A, U, GA, GS, ident):
    with ExitStack() as ctx:
        m = Pool(nc, ctx)
        st = Stream(nc, ctx, "out", A["wall"], list(range(W_AO, W_XKV)))
        norm = Norm(nc, ctx, "sg", Y, NT)
        sgn = m.sb("sg_gain", [P, D])
        sgw, sgb = m.sb("sgw", [P, G_SG, P]), m.sb("sgb", [P, G_SG])
        RING = 3
        side = m.sb("side", [P, RING, CH])
        ug = m.sb("ug", [P, 2, NT, P])
        tmp = m.sb("tmp", [P, CH])
        turn_s = Turn(nc, ctx, "sgt", Y, T, lin, ident, None, NT)
        turn_g = Turn(nc, ctx, "mixt", G, T, lin, ident, None, NT)
        small_in = m.sem("sg_small_in")
        side_in = [m.sem(f"side_in{i}") for i in range(RING)]
        side_used = m.sem("side_used")
        ug_in = [m.sem(f"ug_in{i}") for i in range(2)]
        o, o2, o3 = (Outputs(nc, ctx, x) for x in ("attn_o", "sg_o", "mix_o"))
        sg_ready, sg_done, tmp_done = m.sem("sg_ready"), m.sem("sg_done"), m.sem("sg_tmp")
        NO = 2 * NT
        SGP = [(g, t0, n) for g in range(G_SG) for t0, n in SEQS]

        with nc.Block() as block:
            @block.sync
            def _(sp):
                st.load(sp)

            @block.gpsimd
            def _(pool):
                for dst, src in ((sgn[:], A["sg_gain"].broadcast_to((P, D))), (sgw[:], A["sgw"]), (sgb[:], A["sgb"])):
                    pool.dma_start(dst, src).then_inc(small_in, 16)
                for g in range(2):
                    pool.dma_start(ug[:, g], U[:, :, g * P:(g + 1) * P].rearrange("t p f -> p t f")).then_inc(ug_in[g], 16)
                for n in range(3 * NO):
                    j, c, t = n // NO, n // NT % 2, n % NT
                    if j == 1 and n % NO == 0:
                        for g in range(2, G_SG):
                            pool.wait_ge(sg_done, 2 * g - 2)
                            pool.dma_start(ug[:, g % 2], U[:, :, g * P:(g + 1) * P].rearrange("t p f -> p t f")).then_inc(
                                ug_in[g % 2], 16)
                    if n >= RING:
                        r = n - RING
                        pool.wait_ge((o.freed, side_used, o3.freed)[r // NO], r % NO + 1)
                    src = (GA[t], GS[t], A["x"][t * P:(t + 1) * P, :])[j]
                    pool.dma_start(side[:, n % RING, :], src[:, c * CH:(c + 1) * CH]).then_inc(side_in[n % RING], 16)

            @block.tensor
            def _(pe):
                project_tokens(pe, st, 0, 2, T, range(NT), lin, o)
                norm.wait(pe)
                pe.wait_ge(small_in, 48)
                pe.wait_ge(o.freed, NO)
                for n, (g, t0, nt) in enumerate(SGP):
                    if n >= 6:
                        pe.wait_ge(sg_done, n - 5)
                    pe.matmul(lin[:, n % 6, 0:nt * P], sgw[:, g, :], Y[:, t0:t0 + nt, g * P:(g + 1) * P], start=True,
                              stop=True).then_inc(sg_ready, 1)
                pe.wait_ge(sg_done, len(SGP))
                turn_s.pe(pe)
                turn_s.wait(pe)
                project_tokens(pe, st, 4, 2, T, range(NT), lin, o2)
                pe.wait_ge(o2.freed, NO)
                turn_g.pe(pe)
                turn_g.wait(pe)
                project_tokens(pe, st, 8, 2, T, range(NT), lin, o3)

            @block.scalar
            def _(act):
                st.split_hi(act, 0)
                st.split_hi(act, 1)
                norm.act(act)
                for j, oo in enumerate((o, o2, o3)):
                    if j == 1:
                        turn_s.act(act)
                    if j == 2:
                        turn_g.act(act)
                    for c in range(2):
                        st.split_hi(act, 4 * j + 2 * c + 2)
                        act.wait_ge(oo.ready, NT * (c + 1))
                        st.split_hi(act, 4 * j + 2 * c + 3)

            @block.vector
            def _(dve):
                st.split_lo(dve, 0)
                st.split_lo(dve, 1)
                dve.wait_ge(small_in, 48)
                norm.dve(dve, Y, sgn)

                def each(j, oo, use):
                    for c in range(2):
                        st.split_lo(dve, 4 * j + 2 * c + 2)
                        for t in range(NT):
                            n = c * NT + t
                            dve.wait_ge(oo.ready, n + 1)
                            s = NO * j + n
                            dve.wait_ge(side_in[s % RING], 16 * (s // RING + 1))
                            use(oo, n, t, slice(c * CH, (c + 1) * CH), side[:, s % RING, :])
                        st.split_lo(dve, 4 * j + 2 * c + 3)

                def gated(oo, n, t, cols, s):
                    dve.tensor_tensor(G[:, t, cols], lin[:, t, :], s, ALU.mult).then_inc(oo.freed, 1)

                def added(oo, n, t, cols, s):
                    dve.tensor_tensor(tmp[:], lin[:, t, :], s, ALU.mult).then_inc(oo.freed, 1)
                    dve.wait_ge(oo.freed, n + 1)
                    dve.tensor_tensor(G[:, t, cols], G[:, t, cols], tmp[:], ALU.add).then_inc(side_used, 1)
                    dve.wait_ge(side_used, n + 1)

                def residual(oo, n, t, cols, s):
                    dve.tensor_tensor(Y[:, t, cols], lin[:, t, :], s, ALU.add).then_inc(oo.freed, 1)

                each(0, o, gated)
                for n, (g, t0, nt) in enumerate(SGP):
                    dve.wait_ge(sg_ready, n + 1)
                    dve.wait_ge(ug_in[g % 2], 16 * (g // 2 + 1))
                    dve.scalar_tensor_tensor(
                        out=Y[:, t0:t0 + nt, g * P:(g + 1) * P], in0=lin[:, n % 6, 0:nt * P].rearrange("p (t f) -> p t f", t=nt),
                        scalar=sgb[:, g:g + 1], in1=ug[:, g % 2, t0:t0 + nt, :], op0=ALU.add, op1=ALU.mult).then_inc(sg_done, 1)
                turn_s.dve(dve)
                each(1, o2, added)
                turn_g.dve(dve)
                each(2, o3, residual)


def cross_inputs(nc, T, Y, G, keysT, vals, lin, A, ident):
    with ExitStack() as ctx:
        m = Pool(nc, ctx)
        st = Stream(nc, ctx, "xin", A["wall"], list(range(W_XKV, W_XO)))
        M = G[:, 0:NM, :]
        norm_m, norm_x = Norm(nc, ctx, "mem", M, NM), Norm(nc, ctx, "xa", Y, NT)
        gains = m.sb("xa_gains", [P, 2, KB])
        turn_m = Turn(nc, ctx, "memt", M, T, lin, ident, gains[:, 1, :], NM)
        turn_x = Turn(nc, ctx, "xat", G, T, lin, ident, gains[:, 0, :], NT)
        qT = G[:].rearrange("p t d -> p (t d)").rearrange("p (b n) -> p b n", b=KB)
        small_in = m.sem("xa_small_in")
        m_in = [m.sem(f"m_in{t}") for t in range(NM)]
        o_k, o_v, o_q = (Outputs(nc, ctx, x) for x in ("xk", "xv", "xq"))
        MEMS = [(cb, 0, True, cb, slice(0, NM * P), cb + 1) for cb in range(4)]

        with nc.Block() as block:
            @block.sync
            def _(sp):
                for t in range(NM):
                    sp.dma_start(M[:, t, :], A["mem"][t * P:(t + 1) * P, :]).then_inc(m_in[t], 16)
                st.load(sp)

            @block.gpsimd
            def _(pool):
                pool.dma_start(gains[:], A["gains"][:, 1:3, :]).then_inc(small_in, 16)

            @block.tensor
            def _(pe):
                norm_m.wait(pe)
                turn_m.pe(pe)
                turn_m.wait(pe)
                project_features(pe, st, 0, 2, T, MEMS, lin, o_k, None)
                pe.wait_ge(o_k.freed, 8)
                project_tokens(pe, st, 4, 2, T, range(NM), lin, o_v)
                pe.wait_ge(o_v.freed, 2 * NM)
                norm_x.wait(pe)
                turn_x.pe(pe)
                turn_x.wait(pe)
                project_features(pe, st, 8, 2, T, FEATURES, lin, o_q, None)

            @block.scalar
            def _(act):
                norm_m.act(act, before=lambda t: act.wait_ge(m_in[t], 16))
                st.split_hi(act, 0)
                st.split_hi(act, 1)
                act.wait_ge(small_in, 16)
                turn_m.act(act)
                for c in range(4):
                    o = o_k if c < 2 else o_v
                    st.split_hi(act, 2 * c + 2)
                    for i in range(4):
                        act.wait_ge(o.ready, 4 * (c % 2) + i + 1)
                        dst = keysT[:, 4 * c + i, :] if c < 2 else vals[:, i, (c - 2) * CH:(c - 1) * CH]
                        act.activation(dst, lin[:, i, :], ACT.Copy).then_inc(o.freed, 1)
                    st.split_hi(act, 2 * c + 3)
                norm_x.act(act)
                turn_x.act(act)
                for c in range(2):
                    st.split_hi(act, 10 + 2 * c)
                    for bank, col, _, cb, cols, need in FEATURES:
                        act.wait_ge(o_q.ready, 8 * c + need)
                        act.activation(qT[:, 4 * c + cb, cols], lin[:, bank, col:col + cols.stop - cols.start],
                                       ACT.Copy).then_inc(o_q.freed, 1)
                    st.split_hi(act, 11 + 2 * c)

            @block.vector
            def _(dve):
                norm_m.dve(dve, M)
                st.split_lo(dve, 0)
                st.split_lo(dve, 1)
                dve.wait_ge(small_in, 16)
                turn_m.dve(dve)
                for h in range(2, 10):
                    st.split_lo(dve, h)
                norm_x.dve(dve, G)
                turn_x.dve(dve)
                for h in range(10, 12):
                    st.split_lo(dve, h)


def cross_attention(nc, T, G, keysT, vals, ident, lin, tr):
    heads = [(s, h) for s in range(NSEQ) for h in range(XH)]
    units = [(s, h, t) for s, h in heads for t in range(SEQS[s][1])]
    qT = G[:].rearrange("p t d -> p (t d)").rearrange("p (b n) -> p b n", b=KB)
    NB = XD // P

    def scores_of(u):
        s, h, t = u
        t += SEQS[s][0]
        return [(qT[:, NB * h + j, t * P:(t + 1) * P], keysT[:, NB * h + j, s * MEM:(s + 1) * MEM]) for j in range(NB)]

    outs = [{"head": i, "bank": NB * i + j, "rows": slice(0, P), "opens": True, "ends": True, "block": NB * h + j,
             "cols": slice(SEQS[s][0] * P, sum(SEQS[s]) * P),
             "values": [vals[:, s * (MEM // P) + kb, (NB * h + j) * P:(NB * h + j + 1) * P] for kb in range(MEM // P)]}
            for i, (s, h) in enumerate(heads) for j in range(NB)]
    attention(nc, "xatt", T, ident, lin, tr, units, heads, outs, lambda u: MEM, scores_of, XD ** -0.5)


def routing(nc, T, Y, G, IDX, GATE, lin, tr, A, ident):
    with ExitStack() as ctx:
        m = Pool(nc, ctx)
        st = Stream(nc, ctx, "rt", A["wall"], list(range(W_XO, W_END)))
        norm = Norm(nc, ctx, "ffn", Y, NT)
        gains, row = m.sb("ffn_gains", [P, KB]), m.sb("ffn_row", [P, D])
        turn = Turn(nc, ctx, "ffnt", G, T, lin, ident, gains, NT)
        qT = m.sb("peer_qT", [P, 4, TOK])
        subk = m.sb("subk", [P, 2 * PH, NK])
        iota = m.sb("iota", [P, TOPK])
        sc = m.sb("sc", [P, 2, 4, NK])
        left = m.sb("left", [P, 4, NK])
        best, ids = m.sb("best", [P, 4, TOPK]), m.sb("ids", [P, 4, TOPK], U32)
        idf = m.sb("idf", [P, 4, TOPK])
        cand, cleft = m.sb("cand", [P, 2, TOPK * TOPK]), m.sb("cleft", [P, 2, TOPK * TOPK])
        pos, part_u = m.sb("pos", [P, 2, TOPK], U32), m.sb("part_u", [P, 2, 2 * TOPK], U32)
        part_f = m.sb("part_f", [P, 2, 2 * TOPK])
        pick, e12 = m.sb("pick", [P, 2, 2 * TOPK, TOPK]), m.sb("e12", [P, 2, 2 * TOPK])
        gsum = m.sb("gsum", [P, NT * PH])
        small_in, chain = m.sem("rt_small_in"), m.sem("rt_chain")
        o_x, o_q = Outputs(nc, ctx, "xo"), Outputs(nc, ctx, "pq")
        s_ready, s_copied, s_used, g_shift, g_exp, h_done = (
            m.sem(x) for x in ("s_ready", "s_copied", "s_used", "g_shift", "g_exp", "h_done"))
        NPC = 4

        with nc.Block() as block:
            @block.sync
            def _(sp):
                st.load(sp)

            @block.gpsimd
            def _(pool):
                for dst, src in ((gains[:], A["gains"][:, 3, :]), (row[:], A["ffn_row"].broadcast_to((P, D))),
                                 (subk[:], A["subk"]), (iota[:], A["iota"])):
                    pool.dma_start(dst, src).then_inc(small_in, 16)

            @block.tensor
            def _(pe):
                project_tokens(pe, st, 0, 2, T, range(NT), lin, o_x)
                norm.wait(pe)
                turn.pe(pe)
                turn.wait(pe)
                pe.wait_ge(small_in, 64)

                def scores(c, t):
                    i = c * NT + t
                    pe.wait_ge(o_q.freed, 8 * (c + 1))
                    if i >= 2:
                        pe.wait_ge(s_copied, i - 1)
                    for j in range(4):
                        last = pe.matmul(tr[:, i % 2, j * NK:(j + 1) * NK], qT[:, j, t * P:(t + 1) * P],
                                         subk[:, 4 * c + j, :], start=True, stop=True)
                    last.then_inc(s_ready, 1)

                def between(c, half, i):
                    if c >= 1 and half == 0 and i < NT:
                        scores(c - 1, i)

                project_features(pe, st, 4, NPC, T, FEATURES, lin, o_q, None, between)
                for t in range(NT):
                    scores(NPC - 1, t)

            @block.scalar
            def _(act):
                st.split_hi(act, 0)
                st.split_hi(act, 1)
                for c in range(2):
                    st.split_hi(act, 2 * c + 2)
                    act.wait_ge(o_x.ready, NT * (c + 1))
                    st.split_hi(act, 2 * c + 3)
                act.wait_ge(o_x.freed, 2 * NT)
                norm.act(act)
                act.wait_ge(small_in, 64)
                turn.act(act)

                def copy(c):
                    for t in range(NT):
                        i = c * NT + t
                        act.wait_ge(s_ready, i + 1)
                        if i >= 2:
                            act.wait_ge(s_used, i - 1)
                        act.activation(sc[:, i % 2].rearrange("p j k -> p (j k)"), tr[:, i % 2, :], ACT.Copy).then_inc(
                            s_copied, 1)

                for c in range(NPC):
                    if c >= 1:
                        copy(c - 1)
                    st.split_hi(act, 6 + 2 * c)
                    for bank, col, _, cb, cols, need in FEATURES:
                        act.wait_ge(o_q.ready, 8 * c + need)
                        if c >= 1:
                            act.wait_ge(s_ready, NT * c)
                        act.activation(qT[:, cb, cols], lin[:, bank, col:col + cols.stop - cols.start],
                                       ACT.Copy).then_inc(o_q.freed, 1)
                    st.split_hi(act, 7 + 2 * c)
                copy(NPC - 1)
                act.wait_ge(g_shift, 1)
                act.activation(GATE[:], GATE[:], ACT.Exp).then_inc(g_exp, 1)

            @block.vector
            def _(dve):
                links = 0

                def link(*instructions):
                    nonlocal links
                    for x in instructions:
                        x.then_inc(chain, 1)
                        links += 1
                    dve.wait_ge(chain, links)

                st.split_lo(dve, 0)
                st.split_lo(dve, 1)
                for c in range(2):
                    st.split_lo(dve, 2 * c + 2)
                    for t in range(NT):
                        dve.wait_ge(o_x.ready, NT * c + t + 1)
                        cols = slice(c * CH, (c + 1) * CH)
                        dve.tensor_tensor(Y[:, t, cols], lin[:, t, :], Y[:, t, cols], ALU.add).then_inc(o_x.freed, 1)
                    st.split_lo(dve, 2 * c + 3)
                norm.dve(dve, G)
                dve.wait_ge(small_in, 64)
                turn.dve(dve)
                for t in range(NT):
                    last = dve.tensor_tensor(G[:, t, :], G[:, t, :], row[:], ALU.mult)
                last.then_inc(h_done, 1)

                def top16(v, i, src, rest):
                    n = len(v)
                    link(*[dve.max(v[j][:, 0:8], src[j]) for j in range(n)])
                    link(*[x for j in range(n) for x in (
                        dve.max_index(i[j][:, 0:8], v[j][:, 0:8], src[j]),
                        dve.match_replace(rest[j], v[j][:, 0:8], src[j], LOWEST))])
                    link(*[dve.max(v[j][:, 8:16], rest[j]) for j in range(n)])
                    link(*[dve.max_index(i[j][:, 8:16], v[j][:, 8:16], rest[j]) for j in range(n)])

                def pick_two(c, t):
                    i = c * NT + t
                    dve.wait_ge(s_copied, i + 1)
                    top16([best[:, j, :] for j in range(4)], [ids[:, j, :] for j in range(4)],
                          [sc[:, i % 2, j, :] for j in range(4)], [left[:, j, :] for j in range(4)])
                    adds = []
                    for h in range(2):
                        a = best[:, 2 * h, :].unsqueeze(2).broadcast_to((P, TOPK, TOPK))
                        b = best[:, 2 * h + 1, :].unsqueeze(1).broadcast_to((P, TOPK, TOPK))
                        adds.append(dve.tensor_tensor(cand[:, h].rearrange("p (a b) -> p a b", a=TOPK), a, b, ALU.add))
                    link(dve.tensor_copy(idf[:], ids[:]), *adds)
                    top = [GATE[:, t, (2 * c + h) * TOPK:(2 * c + h + 1) * TOPK] for h in range(2)]
                    top16(top, [pos[:, h, :] for h in range(2)], [cand[:, h, :] for h in range(2)],
                          [cleft[:, h, :] for h in range(2)])
                    link(dve.tensor_scalar(part_u[:, :, 0:TOPK], pos[:], 4, None, ALU.logical_shift_right),
                         dve.tensor_scalar(part_u[:, :, TOPK:], pos[:], TOPK - 1, None, ALU.bitwise_and))
                    link(dve.tensor_copy(part_f[:], part_u[:]))
                    n = 2 * 2 * TOPK
                    link(dve.tensor_tensor(pick[:].rearrange("p h j a -> p (h j) a"),
                                           part_f[:].rearrange("p h j -> p (h j)").unsqueeze(2).broadcast_to((P, n, TOPK)),
                                           iota[:].unsqueeze(1).broadcast_to((P, n, TOPK)), ALU.is_equal))
                    pv = pick[:].rearrange("p h (s j) a -> p (h s) j a", s=2)
                    link(dve.tensor_tensor(pv, pv, idf[:].unsqueeze(2).broadcast_to((P, 4, TOPK, TOPK)), ALU.mult))
                    link(dve.tensor_reduce(e12[:].rearrange("p h j -> p (h j)"), pick[:].rearrange("p h j a -> p (h j) a"),
                                           AX_X, ALU.add))
                    dst = IDX[:, t, 2 * c * TOPK:2 * (c + 1) * TOPK].rearrange("p (h j) -> p h j", h=2)
                    dve.scalar_tensor_tensor(out=dst, in0=e12[:, :, 0:TOPK], scalar=float(NK), in1=e12[:, :, TOPK:],
                                             op0=ALU.mult, op1=ALU.add).then_inc(s_used, 1)
                    dve.wait_ge(s_used, i + 1)

                for c in range(NPC):
                    if c >= 1:
                        for t in range(NT - 2):
                            pick_two(c - 1, t)
                    st.split_lo(dve, 6 + 2 * c)
                    if c >= 1:
                        for t in range(NT - 2, NT):
                            pick_two(c - 1, t)
                    st.split_lo(dve, 7 + 2 * c)
                for t in range(NT):
                    pick_two(NPC - 1, t)
                g = GATE[:].rearrange("p t (h j) -> p (t h) j", j=TOPK)
                dve.tensor_copy(gsum[:], g[:, :, 0]).then_inc(chain, 1)
                links += 1
                dve.wait_ge(chain, links)
                dve.tensor_tensor(g, g, gsum[:].unsqueeze(2).broadcast_to((P, NT * PH, TOPK)), ALU.subtract).then_inc(g_shift, 1)
                dve.wait_ge(g_exp, 1)
                link(dve.tensor_reduce(gsum[:], g, AX_X, ALU.add))
                link(dve.reciprocal(gsum[:], gsum[:]))
                link(dve.tensor_tensor(g, g, gsum[:].unsqueeze(2).broadcast_to((P, NT * PH, TOPK)), ALU.mult))
                dve.wait_ge(h_done, 1)


def experts(nc, Y, G, IDX, GATE, lin, A, ident, outs):
    with ExitStack() as ctx:
        m = Pool(nc, ctx)
        R = GATHERS // 2
        dn, up = m.sb("dn", [P, R, D]), m.sb("up", [P, R, D])
        dots, coef = m.sb("dots", [P, 2, NE]), m.sb("coef", [P, 2, NE])
        DG = 4
        diag = m.sb("diag", [P, DG, P])
        row = m.sb("final_row", [P, D])
        res = m.sb("res", [P, 2, D])
        ss, ms, sd, rstd = (m.sb(f"fin_{x}", [P, NT]) for x in ("ss", "ms", "sd", "rstd"))
        dn_in = [m.sem(f"dn_in{i}") for i in range(R)]
        up_in = [m.sem(f"up_in{i}") for i in range(R)]
        dn_used, up_used, gelued, weighted, diag_done = (
            m.sem(x) for x in ("dn_used", "up_used", "gelued", "weighted", "diag_done"))
        res_done, squared, meaned, rooted, inverted, normed, row_in = (
            m.sem(f"fin_{x}") for x in ("res", "squared", "meaned", "rooted", "inverted", "normed", "row_in"))
        stored = [m.sem(f"stored{i}") for i in range(2)]

        with nc.Block() as block:
            @block.gpsimd
            def _(pool):
                for t in range(NT + 1):
                    for s in range(NE):
                        for table, ring, tt, came, used, on in ((A["down"], dn, t, dn_in, dn_used, t < NT),
                                                                (A["up"], up, t - 1, up_in, up_used, t >= 1)):
                            if not on:
                                continue
                            n = tt * NE + s
                            if n >= R:
                                pool.wait_ge(used, n - R + 1)
                            pool.indirect_dma_start(ring[:, n % R, :], None, table, bass.IndirectOffsetOnAxis(
                                ap=IDX[:, tt, s:s + 1], axis=0)).then_inc(came[n % R], 16)

            @block.vector
            def _(dve):
                dve.wait_ge(row_in, 16)

                def finish(t):
                    dve.wait_ge(up_used, NE * (t + 1))
                    if t >= 2:
                        dve.wait_ge(stored[t % 2], 16 * (t // 2))
                    dve.tensor_tensor(res[:, t % 2, :], lin[:, 2 * (t % 2):2 * (t % 2) + 2, :].rearrange("p a b -> p (a b)"),
                                      Y[:, t, :], ALU.add).then_inc(res_done, 1)
                    dve.wait_ge(squared, t + 1)
                    dve.tensor_scalar(ms[:, t:t + 1], ss[:, t:t + 1], 1.0 / D, EPS, ALU.mult, ALU.add).then_inc(meaned, 1)
                    dve.wait_ge(rooted, t + 1)
                    dve.reciprocal(rstd[:, t:t + 1], sd[:, t:t + 1]).then_inc(inverted, 1)
                    dve.wait_ge(inverted, t + 1)
                    dve.scalar_tensor_tensor(out=res[:, t % 2, :], in0=res[:, t % 2, :], scalar=rstd[:, t:t + 1],
                                             in1=row[:], op0=ALU.mult, op1=ALU.mult).then_inc(normed, 1)

                for t in range(NT):
                    for s in range(NE):
                        n = t * NE + s
                        dve.wait_ge(dn_in[n % R], 16 * (n // R + 1))
                        dve.tensor_tensor_reduce(dn[:, n % R, :], dn[:, n % R, :], G[:, t, :], 1.0, 0.0, ALU.mult, ALU.add,
                                                 dots[:, t % 2, s:s + 1]).then_inc(dn_used, 1)
                    dve.wait_ge(gelued, t + 1)
                    dve.tensor_tensor(coef[:, t % 2, :], dots[:, t % 2, :], GATE[:, t, :], ALU.mult).then_inc(weighted, 1)
                    if t >= 1:
                        finish(t - 1)
                finish(NT - 1)

            @block.scalar
            def _(act):
                def squares(t):
                    act.wait_ge(res_done, t + 1)
                    act.activation(Y[:, t, :], res[:, t % 2, :], ACT.Square, accum_out=ss[:, t:t + 1]).then_inc(squared, 1)
                    act.wait_ge(meaned, t + 1)
                    act.activation(sd[:, t:t + 1], ms[:, t:t + 1], ACT.Sqrt).then_inc(rooted, 1)

                for t in range(NT + 1):
                    if t < NT:
                        pass
                    if t >= 1:
                        for s in range(NE):
                            n = (t - 1) * NE + s
                            if s == 0:
                                act.wait_ge(weighted, t)
                            if n >= DG:
                                act.wait_ge(up_used, n - DG + 1)
                            act.activation(diag[:, n % DG, :], ident[:], ACT.Copy,
                                           scale=coef[:, (t - 1) % 2, s:s + 1]).then_inc(diag_done, 1)
                    if t < NT:
                        act.wait_ge(dn_used, (t + 1) * NE)
                        act.activation(dots[:, t % 2, :], dots[:, t % 2, :], ACT.Gelu_apprx_tanh).then_inc(gelued, 1)
                    if t >= 1:
                        squares(t - 1)

            @block.tensor
            def _(pe):
                for t in range(NT):
                    if t >= 2:
                        pe.wait_ge(res_done, t - 1)
                    for s in range(NE):
                        n = t * NE + s
                        pe.wait_ge(diag_done, n + 1)
                        pe.wait_ge(up_in[n % R], 16 * (n // R + 1))
                        for half in range(2):
                            last = pe.matmul(lin[:, 2 * (t % 2) + half, :], diag[:, n % DG, :],
                                             up[:, n % R, half * CH:(half + 1) * CH], start=(s == 0), stop=(s == NE - 1))
                        last.then_inc(up_used, 1)

            @block.sync
            def _(sp):
                sp.dma_start(row[:], A["final_row"].broadcast_to((P, D))).then_inc(row_in, 16)
                for t in range(NT):
                    sp.wait_ge(normed, t + 1)
                    out, tt = (outs[0], t) if t < SEQS[1][0] else (outs[1], t - SEQS[1][0])
                    sp.dma_start(out[tt * P:(tt + 1) * P, :], res[:, t % 2, :]).then_inc(stored[t % 2], 16)
                for i in range(2):
                    sp.wait_ge(stored[i], 16 * (NT // 2))


def layer(nc, A, outs):
    U, GA, GS = (nc.dram_tensor(x, (NT, P, D), F32).ap() for x in ("u_rows", "attn_gate_rows", "sg_gate_rows"))
    with ExitStack() as ctx:
        Pool.begin(ctx)
        m = Pool(nc, ctx)
        lin = ctx.enter_context(nc.psum_tensor("lin", [P, 6, CH], F32))
        tr = ctx.enter_context(nc.psum_tensor("tr", [P, 2, CH], F32))
        ident = m.sb("ident", [P, P])
        Y = m.sb("Y", [P, NT, D])
        G = m.sb("G", [P, NT, D])
        IDX, GATE = m.sb("IDX", [P, NT, NE], I32), m.sb("GATE", [P, NT, NE])
        with ExitStack() as c1:
            n = Pool(nc, c1)
            T = n.sb("T_hi", [P, KB, TOK], F32R), n.sb("T_lo", [P, KB, TOK], F32R)
            with ExitStack() as c2:
                k = Pool(nc, c2)
                qT = G[:].rearrange("p t d -> p (t d)").rearrange("p (b n) -> p b n", b=KB)
                kT, v_sb = k.sb("kT", [P, NKV, TOK]), k.sb("v_sb", [P, NT, NKV * HD])
                mixer_inputs(nc, m, T, Y, qT, kT, v_sb, lin, tr, A, U, GA, GS, ident)
                self_attention(nc, T, qT, kT, v_sb, ident, lin, tr)
            mixer_outputs(nc, T, Y, G, lin, A, U, GA, GS, ident)
            with ExitStack() as c2:
                k = Pool(nc, c2)
                keysT, vals = k.sb("keysT", [P, KB, NM * P]), k.sb("vals", [P, NM, D])
                cross_inputs(nc, T, Y, G, keysT, vals, lin, A, ident)
                cross_attention(nc, T, G, keysT, vals, ident, lin, tr)
            routing(nc, T, Y, G, IDX, GATE, lin, tr, A, ident)
        experts(nc, Y, G, IDX, GATE, lin, A, ident, outs)


def rope_tables():
    nf = HD // 4
    pos = np.arange(SAMPLE)
    inv = (np.float32(10000.0) ** (-np.arange(nf, dtype=np.float32) / np.float32(nf))).astype(np.float32)
    ar = (pos // 64).astype(np.float32)[:, None] * inv
    ac = (pos % 64).astype(np.float32)[:, None] * inv
    cos = np.concatenate([np.cos(ar), np.cos(ar), np.cos(ac), np.cos(ac)], 1)
    sin = np.concatenate([-np.sin(ar), np.sin(ar), -np.sin(ac), np.sin(ac)], 1)
    return [np.ascontiguousarray(a.reshape(4, P, HD).transpose(1, 0, 2)).astype(np.float32) for a in (cos, sin)]


def chunks_of(w):
    return w.reshape(2, HK, P, -1, CH).transpose(3, 2, 0, 1, 4)


def kernel(**inputs):
    import concourse.bacc as bacc
    from concourse.bass_utils import run_bass_kernel_spmd as run

    a = {k: np.asarray(v) for k, v in inputs.items()}
    w_in = chunks_of(a["w_in"][0])
    wall = np.concatenate([w_in[2:3], w_in[0:2], w_in[3:]] + [chunks_of(a[x][0]) for x in (
        "w_attn_o", "w_sg_o", "w_out", "wkv_xa", "wq_xa", "wo_xa", "w_peer_q")])
    assert wall.shape[0] == W_END
    cos, sin = rope_tables()
    arrays = {
        "x": np.concatenate([a["x_sample"][0], a["x_prompt"][0]]),
        "mem": np.concatenate([a["mem_sample"][0], a["mem_prompt"][0]]),
        "wall": wall,
        "gains": np.stack([a[x][0].reshape(KB, P).T for x in ("norm_mix_g", "norm_xa_g", "norm_mem_g", "norm_ffn_g")], 1),
        "cos": cos, "sin": sin, "qg": a["q_norm_g"], "kg": a["k_norm_g"],
        "ident": np.eye(P, dtype=np.float32),
        "iota": np.broadcast_to(np.arange(TOPK, dtype=np.float32), (P, TOPK)),
        "sg_gain": a["sg_norm_g"], "sgw": a["sg_w"][0].transpose(2, 0, 1), "sgb": a["sg_b"][0].T,
        "ffn_row": a["norm_ffn_g"], "final_row": a["final_norm_g"][None],
        "subk": np.stack([a["peer_k1"][0], a["peer_k2"][0]], 1).transpose(3, 0, 1, 2).reshape(P, 2 * PH, NK),
        "down": a["expert_down"][0], "up": a["expert_up"][0],
    }
    arrays = {k: np.ascontiguousarray(v) for k, v in arrays.items()}
    nc = bacc.Bacc("TRN2", target_bir_lowering=False, num_devices=1)
    A = {k: nc.dram_tensor(f"in_{k}", v.shape, mybir.dt.from_np(v.dtype), kind="ExternalInput").ap()
         for k, v in arrays.items()}
    outs = [nc.dram_tensor(f"out_{n}", (s, D), F32, kind="ExternalOutput").ap()
            for n, s in (("sample", SAMPLE), ("prompt", PROMPT))]
    layer(nc, A, outs)
    r = run(nc, [{f"in_{k}": v for k, v in arrays.items()}], core_ids=[0])
    got = [r.results[0][f"out_{n}"] for n in ("sample", "prompt")]
    return got[1].reshape(1, PROMPT, D), got[0].reshape(1, SAMPLE, D)
```

```python
from contextlib import ExitStack

import numpy as np

import concourse.bass as bass
from concourse import mybir

F32 = mybir.dt.float32
F32R = mybir.dt.float32r
I32 = mybir.dt.int32
BF16 = mybir.dt.bfloat16
U32 = mybir.dt.uint32
ALU = mybir.AluOpType
ACT = mybir.ActivationFunctionType
AX_X = mybir.AxisListType.X

P = 128
D = 1024
KB = D // P
CH = 512
HK = KB // 2
SAMPLE, PROMPT = 512, 256
SEQS = [(0, SAMPLE // P), (SAMPLE // P, PROMPT // P)]
NT = (SAMPLE + PROMPT) // P
TOK = NT * P
NH, NKV, HD = 16, 4, 64
MEM = 256
XH, XD = 4, 256
NSEQ = 2
NM = NSEQ * MEM // P
G_SG = 8
PH, NK, TOPK = 8, 128, 16
NE = PH * TOPK
EPS = 1e-6
LOWEST = -3.4e38
ND = SAMPLE // P
NG = NT - ND
BG = 4
NGRP = NK // BG
WT = 64

W_KV, W_Q, W_U, W_VS, W_GA, W_GS = 0, 1, 3, 5, 7, 9
W_AO, W_SO, W_OUT, W_XKV, W_XQ, W_XO, W_PQ, W_END = 11, 13, 15, 17, 21, 23, 25, 29


class Pool:

    semaphores = None
    shared = {}

    @classmethod
    def begin(cls, ctx):
        cls.semaphores, cls.shared = ctx, {}

    def carried(self, name, increments):
        if name not in Pool.shared:
            Pool.shared[name] = [self.sem(name), 0]
        sem, base = Pool.shared[name]
        Pool.shared[name][1] = base + increments
        return sem, base

    def __init__(self, nc, ctx):
        self.nc, self.ctx = nc, ctx

    def sb(self, name, shape, dt=F32):
        return self.ctx.enter_context(self.nc.sbuf_tensor(name, shape, dt))

    def sem(self, name):
        return Pool.semaphores.enter_context(self.nc.semaphore(name))


class Stream:

    def __init__(self, nc, ctx, tag, wall, chunks):
        self.wall, self.chunks = wall, chunks
        self.n = 2 * len(chunks)
        m = Pool(nc, ctx)
        self.raw = m.sb(f"w_raw_{tag}", [P, 2, HK, CH])
        self.hi = m.sb(f"w_hi_{tag}", [P, 2, HK, CH], F32R)
        self.lo = m.sb(f"w_lo_{tag}", [P, 2, HK, CH], F32R)
        self.loaded = [m.carried(f"w_loaded{i}", 0)[0] for i in range(2)]
        self.hi_done, self.base = m.carried("w_hi_done", self.n)
        self.lo_done, _ = m.carried("w_lo_done", self.n)
        self.used, _ = m.carried("w_used", 0)

    def load(self, sp):
        for h in range(self.n):
            if h >= 2:
                sp.wait_ge(self.lo_done, self.base + h - 1)
            sp.dma_start(self.raw[:, h % 2], self.wall[self.chunks[h // 2], :, h % 2]).then_inc(
                self.loaded[h % 2], 16)

    def split_hi(self, act, h):
        if h >= self.n:
            return
        act.wait_ge(self.loaded[h % 2], 16 * ((self.base + h) // 2 + 1))
        if h >= 2 and h % 2 == 0:
            act.wait_ge(self.used, (self.base + h) // 2)
        act.activation(self.hi[:, h % 2], self.raw[:, h % 2], ACT.Copy).then_inc(self.hi_done, 1)

    def split_lo(self, dve, h):
        if h >= self.n:
            return
        dve.wait_ge(self.hi_done, self.base + h + 1)
        dve.tensor_tensor(self.lo[:, h % 2], self.raw[:, h % 2], self.hi[:, h % 2].bitcast(F32),
                          ALU.subtract).then_inc(self.lo_done, 1)


class Outputs:

    def __init__(self, nc, ctx, tag):
        m = Pool(nc, ctx)
        self.ready = m.sem(f"{tag}_ready")
        self.freed = m.sem(f"{tag}_freed")


def part(T, k, cols):
    if cols.stop <= SAMPLE:
        return T[0][:, k, cols]
    return T[1][:, k, cols.start - SAMPLE:cols.stop - SAMPLE]


def three(pe, out, lhs, rhs, start, stop):
    pe.matmul(out, lhs[0], rhs[0], start=start, stop=False, skip_group_check=True)
    pe.matmul(out, lhs[0], rhs[1], start=False, stop=False, skip_group_check=True)
    return pe.matmul(out, lhs[1], rhs[0], start=False, stop=stop, skip_group_check=True)


def project_tokens(pe, st, h0, nchunks, T, tiles, lin, o, between=None):
    n = len(tiles)
    for c in range(nchunks):
        for half in range(2):
            h = h0 + 2 * c + half
            pe.wait_ge(st.lo_done, st.base + h + 1)
            for i, t in enumerate(tiles):
                if half == 0 and c > 0:
                    pe.wait_ge(o.freed, n * (c - 1) + i + 1)
                for k in range(HK):
                    cols = slice(t * P, (t + 1) * P)
                    kk = half * HK + k
                    last = three(pe, lin[:, i, :], (part(T[0], kk, cols), part(T[1], kk, cols)),
                                 (st.hi[:, h % 2, k, :], st.lo[:, h % 2, k, :]),
                                 start=(kk == 0), stop=(kk == KB - 1))
                if half == 1:
                    last.then_inc(o.ready, 1)
                elif i == n - 1:
                    last.then_inc(st.used, 1)
                if half == 0 and between is not None:
                    between(c, i)


def project_features(pe, st, h0, nchunks, T, groups, lin, o, per, between=None):
    n = len(groups)
    for c in range(nchunks):
        for half in range(2):
            h = h0 + 2 * c + half
            pe.wait_ge(st.lo_done, st.base + h + 1)
            for i, (bank, col, first, cb, cols, need) in enumerate(groups):
                if half == 0 and c > 0:
                    pe.wait_ge(o.freed, n * (c - 1) + need)
                for k in range(HK):
                    kk = half * HK + k
                    fs = slice(cb * P, (cb + 1) * P)
                    last = three(pe, lin[:, bank, col:col + cols.stop - cols.start],
                                 (st.hi[:, h % 2, k, fs], st.lo[:, h % 2, k, fs]),
                                 (part(T[0], kk, cols), part(T[1], kk, cols)),
                                 start=(kk == 0 and first), stop=(kk == KB - 1))
                if half == 1:
                    last.then_inc(o.ready, 1)
                elif i == n - 1:
                    last.then_inc(st.used, 1)
                if between is not None:
                    between(c, half, i)


FEATURES = [(cb, 0, True, cb, slice(0, SAMPLE), cb + 1) for cb in range(4)] + [
    (4 + cb // 2, (cb % 2) * PROMPT, cb % 2 == 0, cb, slice(SAMPLE, TOK), 6 if cb < 2 else 8)
    for cb in range(4)]


class Turn:

    def __init__(self, nc, ctx, tag, src, T, lin, ident, gain, tiles):
        m = Pool(nc, ctx)
        self.src, self.T, self.lin, self.ident, self.gain = src, T, lin, ident, gain
        self.steps = [(k, t0, min(4, tiles - t0)) for k in range(KB) for t0 in range(0, tiles, 4)]
        (self.turned, self.base), (self.hi, _), (self.lo, _) = (
            m.carried(x, len(self.steps)) for x in ("turned", "turn_hi", "turn_lo"))

    def pe(self, pe):
        for n, (k, t0, nt) in enumerate(self.steps):
            if n >= 6:
                pe.wait_ge(self.lo, self.base + n - 5)
            for t in range(nt):
                last = pe.transpose(self.lin[:, n % 6, t * P:(t + 1) * P],
                                    self.src[:, t0 + t, k * P:(k + 1) * P], self.ident[:])
            last.then_inc(self.turned, 1)

    def act(self, act):
        for n, (k, t0, nt) in enumerate(self.steps):
            act.wait_ge(self.turned, self.base + n + 1)
            scale = 1.0 if self.gain is None else self.gain[:, k:k + 1]
            act.activation(part(self.T[0], k, slice(t0 * P, (t0 + nt) * P)), self.lin[:, n % 6, 0:nt * P], ACT.Copy,
                           scale=scale).then_inc(self.hi, 1)

    def dve(self, dve):
        for n, (k, t0, nt) in enumerate(self.steps):
            dve.wait_ge(self.hi, self.base + n + 1)
            scale = 1.0 if self.gain is None else self.gain[:, k:k + 1]
            cols = slice(t0 * P, (t0 + nt) * P)
            dve.scalar_tensor_tensor(out=part(self.T[1], k, cols), in0=self.lin[:, n % 6, 0:nt * P], scalar=scale,
                                     in1=part(self.T[0], k, cols).bitcast(F32), op0=ALU.mult,
                                     op1=ALU.subtract).then_inc(self.lo, 1)

    def wait(self, eng):
        eng.wait_ge(self.lo, self.base + len(self.steps))


class Norm:

    def __init__(self, nc, ctx, tag, src, tiles, junk=None):
        m = Pool(nc, ctx)
        self.src, self.tiles = src, tiles
        self.junk = m.sb(f"{tag}_squares", [P, D])[:] if junk is None else junk
        self.ss, self.ms, self.sd, self.rstd = (m.sb(f"{tag}_{x}", [P, tiles]) for x in ("ss", "ms", "sd", "rstd"))
        (self.summed, self.base), (self.scaled, _) = (m.carried(f"norm_{x}", tiles) for x in ("summed", "scaled"))
        (self.meaned, self.use), (self.rooted, _), (self.inverted, _) = (
            m.carried(f"norm_{x}", 1) for x in ("meaned", "rooted", "inverted"))

    def act(self, act, before=None):
        for t in range(self.tiles):
            if before is not None:
                before(t)
            if t > 0:
                act.wait_ge(self.summed, self.base + t)
            act.activation(self.junk, self.src[:, t, :], ACT.Square,
                           accum_out=self.ss[:, t:t + 1]).then_inc(self.summed, 1)
        act.wait_ge(self.meaned, self.use + 1)
        act.activation(self.sd[:], self.ms[:], ACT.Sqrt).then_inc(self.rooted, 1)

    def dve(self, dve, dst, row=None):
        dve.wait_ge(self.summed, self.base + self.tiles)
        dve.tensor_scalar(self.ms[:], self.ss[:], 1.0 / D, EPS, ALU.mult, ALU.add).then_inc(self.meaned, 1)
        dve.wait_ge(self.rooted, self.use + 1)
        dve.reciprocal(self.rstd[:], self.sd[:]).then_inc(self.inverted, 1)
        dve.wait_ge(self.inverted, self.use + 1)
        for t in range(self.tiles):
            if row is None:
                dve.tensor_scalar(dst[:, t, :], self.src[:, t, :], self.rstd[:, t:t + 1], None,
                                  ALU.mult).then_inc(self.scaled, 1)
            else:
                dve.scalar_tensor_tensor(out=dst[:, t, :], in0=self.src[:, t, :], scalar=self.rstd[:, t:t + 1],
                                         in1=row[:], op0=ALU.mult, op1=ALU.mult).then_inc(self.scaled, 1)

    def wait(self, eng):
        eng.wait_ge(self.scaled, self.base + self.tiles)


def mixer_inputs(nc, m, T, Y, qT, kT, v_sb, lin, tr, A, U, GA, GS, ident):
    with ExitStack() as ctx:
        mm = Pool(nc, ctx)
        st = Stream(nc, ctx, "in", A["wall"], list(range(W_KV, W_AO)))
        rope = mm.sb("rope", [P, 2, CH])
        norm = Norm(nc, ctx, "mix", Y, NT, rope[:].rearrange("p a b -> p (a b)"))
        gains = mm.sb("mix_gain", [P, KB])
        turn = Turn(nc, ctx, "mix", Y, T, lin, ident, gains, NT)
        cos, sin = mm.sb("cos", [P, 4, HD]), mm.sb("sin", [P, 4, HD])
        qg, kg = mm.sb("qg", [P, HD]), mm.sb("kg", [P, HD])
        gcos, gsin = mm.sb("gcos", [P, 2, 4, HD]), mm.sb("gsin", [P, 2, 4, HD])
        sq = mm.sb("sq", [P, 2, CH])
        hss, hms, hsd, hr = (mm.sb(x, [P, 2, 8]) for x in ("hss", "hms", "hsd", "hr"))
        qn, ra, rb = mm.sb("qn", [P, CH]), mm.sb("ra", [P, CH]), mm.sb("rb", [P, CH])
        STG = 2
        stage = mm.sb("stage", [P, STG, CH])
        x_in = [mm.sem(f"x_in{t}") for t in range(NT)]
        small_in, table_done = mm.sem("small_in"), mm.sem("table_done")
        o = Outputs(nc, ctx, "in")
        sq_done, hs_done, ms_done, sd_done, hr_done = (mm.sem(x) for x in ("sq_done", "hs_done", "hms_done", "hsd_done", "hr_done"))
        part, roped, turned, copied = (mm.sem(x) for x in ("rope_part", "roped", "qk_turned", "qk_copied"))
        spilled = [mm.sem(f"spilled{i}") for i in range(STG)]
        NQ = 3 * NT
        NALL = 11 * NT
        spills = [n for n in range(NQ, NALL) if not 5 * NT <= n < 7 * NT]

        def wait_odd(eng, h):
            if h >= 2 and h % 2 == 1 and h < st.n:
                eng.wait_ge(o.ready, NT * (h // 2))

        with nc.Block() as block:
            @block.sync
            def _(sp):
                for t in range(NT):
                    sp.dma_start(Y[:, t, :], A["x"][t * P:(t + 1) * P, :]).then_inc(x_in[t], 16)
                st.load(sp)

            @block.gpsimd
            def _(pool):
                for dst, src in ((ident[:], A["ident"]), (gains[:], A["gains"][:, 0, :]), (cos[:], A["cos"]),
                                 (sin[:], A["sin"]), (qg[:], A["qg"].broadcast_to((P, HD))),
                                 (kg[:], A["kg"].broadcast_to((P, HD)))):
                    pool.dma_start(dst, src).then_inc(small_in, 16)
                for i, n in enumerate(spills):
                    c, t = n // NT, n % NT
                    dst = U if c < 5 else GA if c < 9 else GS
                    pool.wait_ge(o.freed, n + 1)
                    pool.dma_start(dst[t, :, (c + 1) % 2 * CH:((c + 1) % 2 + 1) * CH], stage[:, i % STG, :]).then_inc(
                        spilled[i % STG], 16)
                for i in range(STG):
                    pool.wait_ge(spilled[i], 16 * len(spills[i::STG]))

            @block.tensor
            def _(pe):
                pe.wait_ge(small_in, 96)
                norm.wait(pe)
                turn.pe(pe)
                turn.wait(pe)

                def qk_turn(n):
                    pe.wait_ge(roped, n + 1)
                    if n >= 2:
                        pe.wait_ge(copied, n - 1)
                    for b in range(4):
                        last = pe.transpose(tr[:, n % 2, b * P:(b + 1) * P], rope[:, n % 2, b * P:(b + 1) * P], ident[:])
                    last.then_inc(turned, 1)

                def between(c, i):
                    if 1 <= c <= 3:
                        qk_turn((c - 1) * NT + i)

                project_tokens(pe, st, 0, 11, T, range(NT), lin, o, between)

            @block.scalar
            def _(act):
                norm.act(act, before=lambda t: act.wait_ge(x_in[t], 16))
                st.split_hi(act, 0)
                st.split_hi(act, 1)
                act.wait_ge(small_in, 96)
                turn.act(act)

                def root(n):
                    act.wait_ge(ms_done, n + 1)
                    act.activation(hsd[:, n % 2, :], hms[:, n % 2, :], ACT.Sqrt).then_inc(sd_done, 1)

                def copy(n):
                    c, t = n // NT, n % NT
                    act.wait_ge(turned, n + 1)
                    src = tr[:, n % 2, :].rearrange("p (b f) -> p b f", b=4)
                    dst = (kT[:, :, t * P:(t + 1) * P] if c == 0 else
                           qT[:, 4 * (c - 1):4 * c, t * P:(t + 1) * P])
                    act.activation(dst, src, ACT.Copy).then_inc(copied, 1)

                for c in range(11):
                    if 1 <= c <= 3:
                        for t in range(NT):
                            copy((c - 1) * NT + t)
                    st.split_hi(act, 2 * c + 2)
                    for t in range(NT):
                        n = c * NT + t
                        act.wait_ge(o.ready, n + 1)
                        if n == NQ:
                            act.wait_ge(o.freed, NQ)
                        if n < NQ:
                            w = CH // 2 if c == 0 else CH
                            if c == 0:
                                act.activation(v_sb[:, t, :], lin[:, t, CH // 2:CH], ACT.Copy)
                            act.activation(sq[:, n % 2, 0:w], lin[:, t, 0:w], ACT.Square).then_inc(sq_done, 1)
                            if t >= 1:
                                root(n - 1)
                            if t == NT - 1:
                                root(n)
                        elif 5 <= c < 7:
                            act.activation(Y[:, t, (c - 5) * CH:(c - 4) * CH], lin[:, t, :],
                                           ACT.Gelu_apprx_tanh).then_inc(o.freed, 1)
                        else:
                            i = spills.index(n)
                            if i >= STG:
                                act.wait_ge(spilled[i % STG], 16 * (i // STG))
                            act.activation(stage[:, i % STG, :], lin[:, t, :],
                                           ACT.Gelu_apprx_tanh if c < 5 else ACT.Sigmoid).then_inc(o.freed, 1)
                    wait_odd(act, 2 * c + 3)
                    st.split_hi(act, 2 * c + 3)

            @block.vector
            def _(dve):
                norm.dve(dve, Y)
                st.split_lo(dve, 0)
                st.split_lo(dve, 1)
                dve.wait_ge(small_in, 96)
                turn.dve(dve)
                for j, g in enumerate((kg, qg)):
                    gb = g[:].unsqueeze(1).broadcast_to((P, 4, HD))
                    dve.tensor_tensor(gcos[:, j], cos[:], gb, ALU.mult).then_inc(table_done, 1)
                    gv = g[:].rearrange("p (a b f) -> p a b f", a=2, b=2)
                    sv = sin[:].rearrange("p n (a b f) -> p n a b f", a=2, b=2)
                    ov = gsin[:, j].rearrange("p n (a b f) -> p n a b f", a=2, b=2)
                    for b in range(2):
                        for a in range(2):
                            dve.tensor_tensor(ov[:, :, a, b, :], sv[:, :, a, b, :],
                                              gv[:, a, 1 - b, :].unsqueeze(1).broadcast_to((P, 4, 16)),
                                              ALU.mult).then_inc(table_done, 1)
                dve.wait_ge(table_done, 10)
                nparts = 0

                def rotate(n):
                    nonlocal nparts
                    c, t = n // NT, n % NT
                    nh = 4 if c == 0 else 8
                    w = nh * HD
                    pos = t if t < 4 else t - 4
                    j = 0 if c == 0 else 1
                    dve.wait_ge(sd_done, n + 1)
                    dve.reciprocal(hr[:, n % 2, :], hsd[:, n % 2, :]).then_inc(hr_done, 1)
                    dve.wait_ge(hr_done, n + 1)
                    src = lin[:, t, 0:w].rearrange("p (h f) -> p h f", h=nh)
                    r = hr[:, n % 2, 0:nh].unsqueeze(2).broadcast_to((P, nh, HD))
                    q = qn[:, 0:w].rearrange("p (h f) -> p h f", h=nh)
                    dve.tensor_tensor(q, src, r, ALU.mult).then_inc(o.freed, 1)
                    dve.wait_ge(o.freed, n + 1)
                    cb = gcos[:, j, pos].unsqueeze(1).broadcast_to((P, nh, HD))
                    dve.tensor_tensor(ra[:, 0:w].rearrange("p (h f) -> p h f", h=nh), q, cb, ALU.mult).then_inc(part, 1)
                    qv = qn[:, 0:w].rearrange("p (h a b f) -> p h a b f", h=nh, a=2, b=2)
                    bv = rb[:, 0:w].rearrange("p (h a b f) -> p h a b f", h=nh, a=2, b=2)
                    gv = gsin[:, j, pos].rearrange("p (a b f) -> p a b f", a=2, b=2)
                    for b in range(2):
                        sb = gv[:, :, b, :].unsqueeze(1).broadcast_to((P, nh, 2, 16))
                        dve.tensor_tensor(bv[:, :, :, b, :], qv[:, :, :, 1 - b, :], sb, ALU.mult).then_inc(part, 1)
                    nparts += 3
                    dve.wait_ge(part, nparts)
                    if n >= 2:
                        dve.wait_ge(turned, n - 1)
                    if c == 0:
                        for dup in range(2):
                            dst = rope[:, n % 2, :].rearrange("p (h u f) -> p h u f", h=nh, u=2)[:, :, dup, :]
                            last = dve.tensor_tensor(dst, ra[:, 0:w].rearrange("p (h f) -> p h f", h=nh),
                                                     rb[:, 0:w].rearrange("p (h f) -> p h f", h=nh), ALU.add)
                    else:
                        last = dve.tensor_tensor(rope[:, n % 2, :], ra[:], rb[:], ALU.add)
                    last.then_inc(roped, 1)
                    dve.wait_ge(roped, n + 1)

                for c in range(11):
                    st.split_lo(dve, 2 * c + 2)
                    for t in range(NT):
                        n = c * NT + t
                        if n < NQ:
                            nh = 4 if c == 0 else 8
                            dve.wait_ge(sq_done, n + 1)
                            if n == 0:
                                dve.memset(hss[:], 1.0).then_inc(hs_done, 1)
                                dve.wait_ge(hs_done, 1)
                            dve.tensor_reduce(hss[:, n % 2, 0:nh],
                                              sq[:, n % 2, 0:nh * HD].rearrange("p (h f) -> p h f", h=nh),
                                              AX_X, ALU.add).then_inc(hs_done, 1)
                            dve.wait_ge(hs_done, n + 2)
                            dve.tensor_scalar(hms[:, n % 2, :], hss[:, n % 2, :], 1.0 / HD, EPS, ALU.mult,
                                              ALU.add).then_inc(ms_done, 1)
                            if t >= 1:
                                rotate(n - 1)
                            if t == NT - 1:
                                rotate(n)
                    st.split_lo(dve, 2 * c + 3)



def attention(nc, tag, T, ident, lin, tr, units, heads, outs, width_of, scores_of, scale):
    with ExitStack() as ctx:
        m = Pool(nc, ctx)
        KMAX = max(width_of(u) for u in units)
        probs = m.sb(f"{tag}_probs", [P, 3, KMAX])
        pT = m.sb(f"{tag}_probsT", [P, 2, KMAX // P, SAMPLE])
        mx, nmx, rs, rr = (m.sb(f"{tag}_{x}", [P, 3]) for x in ("mx", "nmx", "rs", "rr"))
        scored, maxed, negated, exped, inverted, normed, turned, copied, summed, out_hi, out_lo = (
            m.sem(f"{tag}_{x}") for x in ("scored", "maxed", "negated", "exped", "inverted", "normed", "turned",
                                          "copied", "summed", "out_hi", "out_lo"))
        N = len(units)
        head_of = {(s, h): i for i, (s, h) in enumerate(heads)}
        last_unit = [max(u for u, x in enumerate(units) if x[:2] == sh) for sh in heads]
        prods_to_head = [sum(p["head"] <= i for p in outs) for i in range(len(heads))]
        banks = [(n + 1, p) for n, p in enumerate(outs) if p["ends"]]
        bank_step = [last_unit[p["head"]] + 5 for _, p in banks]

        with nc.Block() as block:
            @block.tensor
            def _(pe):
                def scores(u):
                    if u >= 3:
                        pe.wait_ge(exped, u - 2)
                    pairs = scores_of(units[u])
                    for i, (a, b) in enumerate(pairs):
                        last = pe.matmul(lin[:, u % 3, 0:width_of(units[u])], a, b, start=(i == 0),
                                         stop=(i == len(pairs) - 1))
                    last.then_inc(scored, 1)

                def turn(u):
                    pe.wait_ge(normed, u + 1)
                    if u >= 3:
                        pe.wait_ge(copied, u - 2)
                    for kb in range(width_of(units[u]) // P):
                        last = pe.transpose(lin[:, 3 + u % 3, kb * P:(kb + 1) * P],
                                            probs[:, u % 3, kb * P:(kb + 1) * P], ident[:])
                    last.then_inc(turned, 1)

                def values(i):
                    pe.wait_ge(copied, last_unit[i] + 1)
                    for p in (p for p in outs if p["head"] == i):
                        if p["opens"] and p["bank"] >= 2:
                            pe.wait_ge(out_lo, p["bank"] - 1)
                        w = p["cols"].stop - p["cols"].start
                        for kb, v in enumerate(p["values"]):
                            last = pe.matmul(tr[p["rows"], p["bank"] % 2, 0:w], v, pT[:, i % 2, kb, 0:w],
                                             start=(kb == 0), stop=(kb == len(p["values"]) - 1))
                        last.then_inc(summed, 1)

                done = 0
                for step in range(N + 4):
                    if step < N:
                        scores(step)
                    if 2 <= step < N + 2:
                        turn(step - 2)
                    while done < len(heads) and last_unit[done] <= step - 3:
                        values(done)
                        done += 1

            @block.scalar
            def _(act):
                def exp(u):
                    w = width_of(units[u])
                    act.wait_ge(negated, u + 1)
                    if u >= 3:
                        act.wait_ge(turned, u - 2)
                    act.activation(probs[:, u % 3, 0:w], lin[:, u % 3, 0:w], ACT.Exp, bias=nmx[:, u % 3:u % 3 + 1],
                                   scale=scale, accum_out=rs[:, u % 3:u % 3 + 1]).then_inc(exped, 1)

                def copy(u):
                    s, h, t = units[u]
                    i = head_of[s, h]
                    kbs = width_of(units[u]) // P
                    act.wait_ge(turned, u + 1)
                    if i >= 2 and t == 0:
                        act.wait_ge(summed, prods_to_head[i - 2])
                    act.activation(pT[:, i % 2, 0:kbs, t * P:(t + 1) * P],
                                   lin[:, 3 + u % 3, 0:kbs * P].rearrange("p (k q) -> p k q", k=kbs),
                                   ACT.Copy).then_inc(copied, 1)

                for step in range(N + 6):
                    if 3 <= step < N + 3:
                        copy(step - 3)
                    if step < N:
                        exp(step)
                    for n, (prods, p) in enumerate(banks):
                        if bank_step[n] == step:
                            act.wait_ge(summed, prods)
                            act.activation(part(T[0], p["block"], p["cols"]),
                                           tr[:, n % 2, 0:p["cols"].stop - p["cols"].start], ACT.Copy).then_inc(out_hi, 1)

            @block.vector
            def _(dve):
                def norm(u):
                    w = width_of(units[u])
                    i = u % 3
                    dve.wait_ge(exped, u + 1)
                    dve.reciprocal(rr[:, i:i + 1], rs[:, i:i + 1]).then_inc(inverted, 1)
                    dve.wait_ge(inverted, u + 1)
                    dve.tensor_scalar(probs[:, i, 0:w], probs[:, i, 0:w], rr[:, i:i + 1], None,
                                      ALU.mult).then_inc(normed, 1)

                for step in range(N + 6):
                    if step < N:
                        w = width_of(units[step])
                        i = step % 3
                        dve.wait_ge(scored, step + 1)
                        dve.reduce_max(mx[:, i:i + 1], lin[:, i, 0:w], AX_X).then_inc(maxed, 1)
                        dve.wait_ge(maxed, step + 1)
                        dve.tensor_scalar(nmx[:, i:i + 1], mx[:, i:i + 1], -scale, None, ALU.mult).then_inc(negated, 1)
                    if 1 <= step < N + 1:
                        norm(step - 1)
                    for n, (prods, p) in enumerate(banks):
                        if bank_step[n] == step:
                            cols = p["cols"]
                            dve.wait_ge(out_hi, n + 1)
                            dve.tensor_tensor(part(T[1], p["block"], cols), tr[:, n % 2, 0:cols.stop - cols.start],
                                              part(T[0], p["block"], cols).bitcast(F32), ALU.subtract).then_inc(out_lo, 1)


def self_attention(nc, T, qT, kT, v_sb, ident, lin, tr):
    heads = [(s, h) for s in range(NSEQ) for h in range(NH)]
    units = [(s, h, t) for s, h in heads for t in range(SEQS[s][1])]
    span = lambda s: slice(SEQS[s][0] * P, sum(SEQS[s]) * P)
    kv_of = lambda h: h // (NH // NKV)

    def scores_of(u):
        s, h, t = u
        t0 = SEQS[s][0]
        rows = slice(h % 2 * HD, (h % 2 + 1) * HD)
        return [(qT[rows, h // 2, (t0 + t) * P:(t0 + t + 1) * P], kT[rows, kv_of(h), span(s)])]

    outs = [{"head": i, "bank": i // 2, "rows": slice(h % 2 * HD, (h % 2 + 1) * HD), "opens": h % 2 == 0,
             "ends": h % 2 == 1, "block": h // 2, "cols": span(s),
             "values": [v_sb[:, t, kv_of(h) * HD:(kv_of(h) + 1) * HD] for t in range(SEQS[s][0], sum(SEQS[s]))]}
            for i, (s, h) in enumerate(heads)]
    attention(nc, "att", T, ident, lin, tr, units, heads, outs, lambda u: SEQS[u[0]][1] * P, scores_of, HD ** -0.5)


def mixer_outputs(nc, T, Y, G, lin, A, U, GA, GS, ident):
    with ExitStack() as ctx:
        m = Pool(nc, ctx)
        st = Stream(nc, ctx, "out", A["wall"], list(range(W_AO, W_XKV)))
        norm = Norm(nc, ctx, "sg", Y, NT)
        sgn = m.sb("sg_gain", [P, D])
        sgw, sgb = m.sb("sgw", [P, G_SG, P]), m.sb("sgb", [P, G_SG])
        RING = 3
        side = m.sb("side", [P, RING, CH])
        ug = m.sb("ug", [P, 2, NT, P])
        tmp = m.sb("tmp", [P, CH])
        turn_s = Turn(nc, ctx, "sgt", Y, T, lin, ident, None, NT)
        turn_g = Turn(nc, ctx, "mixt", G, T, lin, ident, None, NT)
        small_in = m.sem("sg_small_in")
        side_in = [m.sem(f"side_in{i}") for i in range(RING)]
        side_used = m.sem("side_used")
        ug_in = [m.sem(f"ug_in{i}") for i in range(2)]
        o, o2, o3 = (Outputs(nc, ctx, x) for x in ("attn_o", "sg_o", "mix_o"))
        sg_ready, sg_done, tmp_done = m.sem("sg_ready"), m.sem("sg_done"), m.sem("sg_tmp")
        NO = 2 * NT
        SGP = [(g, t0, n) for g in range(G_SG) for t0, n in SEQS]

        with nc.Block() as block:
            @block.sync
            def _(sp):
                st.load(sp)

            @block.gpsimd
            def _(pool):
                for dst, src in ((sgn[:], A["sg_gain"].broadcast_to((P, D))), (sgw[:], A["sgw"]), (sgb[:], A["sgb"])):
                    pool.dma_start(dst, src).then_inc(small_in, 16)
                for g in range(2):
                    pool.dma_start(ug[:, g], U[:, :, g * P:(g + 1) * P].rearrange("t p f -> p t f")).then_inc(ug_in[g], 16)
                for n in range(3 * NO):
                    j, c, t = n // NO, n // NT % 2, n % NT
                    if j == 1 and n % NO == 0:
                        for g in range(2, G_SG):
                            pool.wait_ge(sg_done, 2 * g - 2)
                            pool.dma_start(ug[:, g % 2], U[:, :, g * P:(g + 1) * P].rearrange("t p f -> p t f")).then_inc(
                                ug_in[g % 2], 16)
                    if n >= RING:
                        r = n - RING
                        pool.wait_ge((o.freed, side_used, o3.freed)[r // NO], r % NO + 1)
                    src = (GA[t], GS[t], A["x"][t * P:(t + 1) * P, :])[j]
                    pool.dma_start(side[:, n % RING, :], src[:, c * CH:(c + 1) * CH]).then_inc(side_in[n % RING], 16)

            @block.tensor
            def _(pe):
                project_tokens(pe, st, 0, 2, T, range(NT), lin, o)
                norm.wait(pe)
                pe.wait_ge(small_in, 48)
                pe.wait_ge(o.freed, NO)
                for n, (g, t0, nt) in enumerate(SGP):
                    if n >= 6:
                        pe.wait_ge(sg_done, n - 5)
                    pe.matmul(lin[:, n % 6, 0:nt * P], sgw[:, g, :], Y[:, t0:t0 + nt, g * P:(g + 1) * P], start=True,
                              stop=True).then_inc(sg_ready, 1)
                pe.wait_ge(sg_done, len(SGP))
                turn_s.pe(pe)
                turn_s.wait(pe)
                project_tokens(pe, st, 4, 2, T, range(NT), lin, o2)
                pe.wait_ge(o2.freed, NO)
                turn_g.pe(pe)
                turn_g.wait(pe)
                project_tokens(pe, st, 8, 2, T, range(NT), lin, o3)

            @block.scalar
            def _(act):
                st.split_hi(act, 0)
                st.split_hi(act, 1)
                norm.act(act)
                for j, oo in enumerate((o, o2, o3)):
                    if j == 1:
                        turn_s.act(act)
                    if j == 2:
                        turn_g.act(act)
                    for c in range(2):
                        st.split_hi(act, 4 * j + 2 * c + 2)
                        act.wait_ge(oo.ready, NT * (c + 1))
                        st.split_hi(act, 4 * j + 2 * c + 3)

            @block.vector
            def _(dve):
                st.split_lo(dve, 0)
                st.split_lo(dve, 1)
                dve.wait_ge(small_in, 48)
                norm.dve(dve, Y, sgn)

                def each(j, oo, use):
                    for c in range(2):
                        st.split_lo(dve, 4 * j + 2 * c + 2)
                        for t in range(NT):
                            n = c * NT + t
                            dve.wait_ge(oo.ready, n + 1)
                            s = NO * j + n
                            dve.wait_ge(side_in[s % RING], 16 * (s // RING + 1))
                            use(oo, n, t, slice(c * CH, (c + 1) * CH), side[:, s % RING, :])
                        st.split_lo(dve, 4 * j + 2 * c + 3)

                def gated(oo, n, t, cols, s):
                    dve.tensor_tensor(G[:, t, cols], lin[:, t, :], s, ALU.mult).then_inc(oo.freed, 1)

                def added(oo, n, t, cols, s):
                    dve.tensor_tensor(tmp[:], lin[:, t, :], s, ALU.mult).then_inc(oo.freed, 1)
                    dve.wait_ge(oo.freed, n + 1)
                    dve.tensor_tensor(G[:, t, cols], G[:, t, cols], tmp[:], ALU.add).then_inc(side_used, 1)
                    dve.wait_ge(side_used, n + 1)

                def residual(oo, n, t, cols, s):
                    dve.tensor_tensor(Y[:, t, cols], lin[:, t, :], s, ALU.add).then_inc(oo.freed, 1)

                each(0, o, gated)
                for n, (g, t0, nt) in enumerate(SGP):
                    dve.wait_ge(sg_ready, n + 1)
                    dve.wait_ge(ug_in[g % 2], 16 * (g // 2 + 1))
                    dve.scalar_tensor_tensor(
                        out=Y[:, t0:t0 + nt, g * P:(g + 1) * P], in0=lin[:, n % 6, 0:nt * P].rearrange("p (t f) -> p t f", t=nt),
                        scalar=sgb[:, g:g + 1], in1=ug[:, g % 2, t0:t0 + nt, :], op0=ALU.add, op1=ALU.mult).then_inc(sg_done, 1)
                turn_s.dve(dve)
                each(1, o2, added)
                turn_g.dve(dve)
                each(2, o3, residual)


def cross_inputs(nc, T, Y, G, keysT, vals, lin, A, ident):
    with ExitStack() as ctx:
        m = Pool(nc, ctx)
        st = Stream(nc, ctx, "xin", A["wall"], list(range(W_XKV, W_XO)))
        M = G[:, 0:NM, :]
        norm_m, norm_x = Norm(nc, ctx, "mem", M, NM), Norm(nc, ctx, "xa", Y, NT)
        gains = m.sb("xa_gains", [P, 2, KB])
        turn_m = Turn(nc, ctx, "memt", M, T, lin, ident, gains[:, 1, :], NM)
        turn_x = Turn(nc, ctx, "xat", G, T, lin, ident, gains[:, 0, :], NT)
        qT = G[:].rearrange("p t d -> p (t d)").rearrange("p (b n) -> p b n", b=KB)
        small_in = m.sem("xa_small_in")
        m_in = [m.sem(f"m_in{t}") for t in range(NM)]
        o_k, o_v, o_q = (Outputs(nc, ctx, x) for x in ("xk", "xv", "xq"))
        MEMS = [(cb, 0, True, cb, slice(0, NM * P), cb + 1) for cb in range(4)]

        with nc.Block() as block:
            @block.sync
            def _(sp):
                for t in range(NM):
                    sp.dma_start(M[:, t, :], A["mem"][t * P:(t + 1) * P, :]).then_inc(m_in[t], 16)
                st.load(sp)

            @block.gpsimd
            def _(pool):
                pool.dma_start(gains[:], A["gains"][:, 1:3, :]).then_inc(small_in, 16)

            @block.tensor
            def _(pe):
                norm_m.wait(pe)
                turn_m.pe(pe)
                turn_m.wait(pe)
                project_features(pe, st, 0, 2, T, MEMS, lin, o_k, None)
                pe.wait_ge(o_k.freed, 8)
                project_tokens(pe, st, 4, 2, T, range(NM), lin, o_v)
                pe.wait_ge(o_v.freed, 2 * NM)
                norm_x.wait(pe)
                turn_x.pe(pe)
                turn_x.wait(pe)
                project_features(pe, st, 8, 2, T, FEATURES, lin, o_q, None)

            @block.scalar
            def _(act):
                norm_m.act(act, before=lambda t: act.wait_ge(m_in[t], 16))
                st.split_hi(act, 0)
                st.split_hi(act, 1)
                act.wait_ge(small_in, 16)
                turn_m.act(act)
                for c in range(4):
                    o = o_k if c < 2 else o_v
                    st.split_hi(act, 2 * c + 2)
                    for i in range(4):
                        act.wait_ge(o.ready, 4 * (c % 2) + i + 1)
                        dst = keysT[:, 4 * c + i, :] if c < 2 else vals[:, i, (c - 2) * CH:(c - 1) * CH]
                        act.activation(dst, lin[:, i, :], ACT.Copy).then_inc(o.freed, 1)
                    st.split_hi(act, 2 * c + 3)
                norm_x.act(act)
                turn_x.act(act)
                for c in range(2):
                    st.split_hi(act, 10 + 2 * c)
                    for bank, col, _, cb, cols, need in FEATURES:
                        act.wait_ge(o_q.ready, 8 * c + need)
                        act.activation(qT[:, 4 * c + cb, cols], lin[:, bank, col:col + cols.stop - cols.start],
                                       ACT.Copy).then_inc(o_q.freed, 1)
                    st.split_hi(act, 11 + 2 * c)

            @block.vector
            def _(dve):
                norm_m.dve(dve, M)
                st.split_lo(dve, 0)
                st.split_lo(dve, 1)
                dve.wait_ge(small_in, 16)
                turn_m.dve(dve)
                for h in range(2, 10):
                    st.split_lo(dve, h)
                norm_x.dve(dve, G)
                turn_x.dve(dve)
                for h in range(10, 12):
                    st.split_lo(dve, h)


def cross_attention(nc, T, G, keysT, vals, ident, lin, tr):
    heads = [(s, h) for s in range(NSEQ) for h in range(XH)]
    units = [(s, h, t) for s, h in heads for t in range(SEQS[s][1])]
    qT = G[:].rearrange("p t d -> p (t d)").rearrange("p (b n) -> p b n", b=KB)
    NB = XD // P

    def scores_of(u):
        s, h, t = u
        t += SEQS[s][0]
        return [(qT[:, NB * h + j, t * P:(t + 1) * P], keysT[:, NB * h + j, s * MEM:(s + 1) * MEM]) for j in range(NB)]

    outs = [{"head": i, "bank": NB * i + j, "rows": slice(0, P), "opens": True, "ends": True, "block": NB * h + j,
             "cols": slice(SEQS[s][0] * P, sum(SEQS[s]) * P),
             "values": [vals[:, s * (MEM // P) + kb, (NB * h + j) * P:(NB * h + j + 1) * P] for kb in range(MEM // P)]}
            for i, (s, h) in enumerate(heads) for j in range(NB)]
    attention(nc, "xatt", T, ident, lin, tr, units, heads, outs, lambda u: MEM, scores_of, XD ** -0.5)


def routing(nc, T, Y, G, H, E12, GATE, IDX, lin, tr, A, ident):
    with ExitStack() as ctx:
        m = Pool(nc, ctx)
        st = Stream(nc, ctx, "rt", A["wall"], list(range(W_XO, W_END)))
        qT = m.sb("peer_qT", [P, 4, TOK])
        norm = Norm(nc, ctx, "ffn", Y, NT, qT[:].rearrange("p a b -> p (a b)")[:, 0:D])
        gains, row = m.sb("ffn_gains", [P, KB]), m.sb("ffn_row", [P, D])
        turn = Turn(nc, ctx, "ffnt", G, T, lin, ident, gains, NT)
        subk = m.sb("subk", [P, 2 * PH, NK])
        iota = m.sb("iota", [P, TOPK])
        LOOK = 2 * 2 * TOPK
        place = m.sb("place", [P, TOPK, LOOK], BF16)
        sc = m.sb("sc", [P, 2, 4, NK])
        left = m.sb("left", [P, 4, NK])
        best, ids = m.sb("best", [P, 2, 4, TOPK]), m.sb("ids", [P, 2, 4, TOPK], U32)
        id_b = m.sb("id_b", [P, 3, 4, TOPK], BF16)
        cand, cleft = m.sb("cand", [P, 2, 2, TOPK * TOPK]), m.sb("cleft", [P, 2, TOPK * TOPK])
        pos, part_u = m.sb("pos", [P, 2, TOPK], U32), m.sb("part_u", [P, 2, 2, 2 * TOPK], U32)
        part_b = m.sb("part_b", [P, 2, LOOK], BF16)
        pick = m.sb("pick", [P, 2, TOPK, LOOK], BF16)
        gsum = m.sb("gsum", [P, NT * PH])
        small_in, chain, place_done = m.sem("rt_small_in"), m.sem("rt_chain"), m.sem("rt_place_done")
        halved, paired, ids_read, parts_ready, parts_read, marked, looked_up, adding = (
            m.sem(f"rt_{x}") for x in ("halved", "paired", "ids_read", "parts_ready", "parts_read", "marked",
                                       "looked_up", "adding"))
        o_x, o_q = Outputs(nc, ctx, "xo"), Outputs(nc, ctx, "pq")
        s_ready, s_copied, s_used, g_shift, g_exp, h_done = (
            m.sem(x) for x in ("s_ready", "s_copied", "s_used", "g_shift", "g_exp", "h_done"))
        NPC = 4
        UNITS = NPC * NT

        with nc.Block() as block:
            @block.sync
            def _(sp):
                st.load(sp)

            @block.gpsimd
            def _(pool):
                for dst, src in ((gains[:], A["gains"][:, 3, :]), (row[:], A["ffn_row"].broadcast_to((P, D))),
                                 (subk[:], A["subk"]), (iota[:], A["iota"])):
                    pool.dma_start(dst, src).then_inc(small_in, 16)
                pool.wait_ge(small_in, 64)
                pool.tensor_copy(place[:], iota[:].unsqueeze(2).broadcast_to((P, TOPK, LOOK))).then_inc(place_done, 1)
                sums = 0
                for r in range(UNITS + 2):
                    u = r
                    if u < UNITS:
                        pool.wait_ge(halved, u + 1)
                        v = best[:, u % 2].rearrange("p (h s) a -> p h s a", s=2)
                        pool.tensor_tensor(cand[:, u % 2].rearrange("p h (a b) -> p h a b", a=TOPK),
                                           v[:, :, 0, :].unsqueeze(3).broadcast_to((P, 2, TOPK, TOPK)),
                                           v[:, :, 1, :].unsqueeze(2).broadcast_to((P, 2, TOPK, TOPK)),
                                           ALU.add).then_inc(paired, 1)
                        pool.tensor_copy(id_b[:, u % 3], ids[:, u % 2]).then_inc(ids_read, 1)
                    u = r - 1
                    if 0 <= u < UNITS:
                        pool.wait_ge(parts_ready, u + 1)
                        pool.tensor_copy(part_b[:, u % 2], part_u[:, u % 2].rearrange("p h j -> p (h j)")).then_inc(
                            parts_read, 1)
                    u = r - 2
                    if 0 <= u < UNITS:
                        pool.wait_ge(marked, u + 1)
                        pool.wait_ge(ids_read, u + 1)
                        pv = pick[:, u % 2].rearrange("p a (s j) -> p s a j", s=4)
                        pool.tensor_tensor(pv, pv, id_b[:, u % 3].unsqueeze(3).broadcast_to((P, 4, TOPK, TOPK)),
                                           ALU.mult).then_inc(adding, 1)
                        for half in (8, 4, 2):
                            sums += 1
                            pool.wait_ge(adding, sums)
                            pool.tensor_tensor(pick[:, u % 2, 0:half], pick[:, u % 2, 0:half], pick[:, u % 2, half:2 * half],
                                               ALU.add).then_inc(adding, 1)
                        sums += 1
                        pool.wait_ge(adding, sums)
                        c, t = u // NT, u % NT
                        x = pick[:, u % 2].rearrange("p a (h s j) -> p a h s j", h=2, s=2)
                        pool.tensor_tensor(E12[:, t, :, 2 * c * TOPK:2 * (c + 1) * TOPK].rearrange("p s (h j) -> p h s j", h=2),
                                           x[:, 0], x[:, 1], ALU.add).then_inc(looked_up, 1)

            @block.tensor
            def _(pe):
                project_tokens(pe, st, 0, 2, T, range(NT), lin, o_x)
                norm.wait(pe)
                turn.pe(pe)
                turn.wait(pe)
                pe.wait_ge(small_in, 64)

                def scores(c, t):
                    i = c * NT + t
                    pe.wait_ge(o_q.freed, 8 * (c + 1))
                    if i >= 2:
                        pe.wait_ge(s_copied, i - 1)
                    for j in range(4):
                        last = pe.matmul(tr[:, i % 2, j * NK:(j + 1) * NK], qT[:, j, t * P:(t + 1) * P],
                                         subk[:, 4 * c + j, :], start=True, stop=True)
                    last.then_inc(s_ready, 1)

                def between(c, half, i):
                    if c >= 1 and half == 0 and i < NT:
                        scores(c - 1, i)

                project_features(pe, st, 4, NPC, T, FEATURES, lin, o_q, None, between)
                for t in range(NT):
                    scores(NPC - 1, t)

            @block.scalar
            def _(act):
                st.split_hi(act, 0)
                st.split_hi(act, 1)
                for c in range(2):
                    st.split_hi(act, 2 * c + 2)
                    act.wait_ge(o_x.ready, NT * (c + 1))
                    st.split_hi(act, 2 * c + 3)
                act.wait_ge(o_x.freed, 2 * NT)
                norm.act(act)
                act.wait_ge(small_in, 64)
                turn.act(act)

                def copy(c):
                    for t in range(NT):
                        i = c * NT + t
                        act.wait_ge(s_ready, i + 1)
                        if i >= 2:
                            act.wait_ge(s_used, i - 1)
                        act.activation(sc[:, i % 2].rearrange("p j k -> p (j k)"), tr[:, i % 2, :], ACT.Copy).then_inc(
                            s_copied, 1)

                for c in range(NPC):
                    if c >= 1:
                        copy(c - 1)
                    st.split_hi(act, 6 + 2 * c)
                    for bank, col, _, cb, cols, need in FEATURES:
                        act.wait_ge(o_q.ready, 8 * c + need)
                        if c >= 1:
                            act.wait_ge(s_ready, NT * c)
                        act.activation(qT[:, cb, cols], lin[:, bank, col:col + cols.stop - cols.start],
                                       ACT.Copy).then_inc(o_q.freed, 1)
                    st.split_hi(act, 7 + 2 * c)
                copy(NPC - 1)
                act.wait_ge(g_shift, 1)
                act.activation(GATE[:], GATE[:], ACT.Exp).then_inc(g_exp, 1)

            @block.vector
            def _(dve):
                links = 0

                def link(*instructions):
                    nonlocal links
                    for x in instructions:
                        x.then_inc(chain, 1)
                        links += 1
                    dve.wait_ge(chain, links)

                st.split_lo(dve, 0)
                st.split_lo(dve, 1)
                for c in range(2):
                    st.split_lo(dve, 2 * c + 2)
                    for t in range(NT):
                        dve.wait_ge(o_x.ready, NT * c + t + 1)
                        cols = slice(c * CH, (c + 1) * CH)
                        dve.tensor_tensor(Y[:, t, cols], lin[:, t, :], Y[:, t, cols], ALU.add).then_inc(o_x.freed, 1)
                    st.split_lo(dve, 2 * c + 3)
                norm.dve(dve, G)
                dve.wait_ge(small_in, 64)
                turn.dve(dve)
                for q in range(NG):
                    last = dve.tensor_tensor(H[:, q, :], G[:, ND + q, :], row[:], ALU.mult)
                last.then_inc(h_done, 1)

                def pick_experts(r):
                    rows = []
                    if r < UNITS:
                        dve.wait_ge(s_copied, r + 1)
                        if r >= 2:
                            dve.wait_ge(ids_read, r - 1)
                        rows += [(best[:, r % 2, j, :], ids[:, r % 2, j, :], sc[:, r % 2, j, :], left[:, j, :])
                                 for j in range(4)]
                    ones = len(rows)
                    if 0 <= r - 1 < UNITS:
                        c, t = (r - 1) // NT, (r - 1) % NT
                        rows += [(GATE[:, t, (2 * c + h) * TOPK:(2 * c + h + 1) * TOPK], pos[:, h, :],
                                  cand[:, (r - 1) % 2, h, :], cleft[:, h, :]) for h in range(2)]
                    if rows:
                        for n, (v, i, src, rest) in enumerate(rows):
                            if n == ones:
                                dve.wait_ge(paired, r)
                            last = dve.max(v[:, 0:8], src)
                        link(last)
                        for v, i, src, rest in rows:
                            dve.max_index(i[:, 0:8], v[:, 0:8], src)
                            last = dve.match_replace(rest, v[:, 0:8], src, LOWEST)
                        link(last)
                        for n, (v, i, src, rest) in enumerate(rows):
                            last = dve.max(v[:, 8:16], rest)
                            if n == 0 and r < UNITS:
                                last.then_inc(s_used, 1)
                        link(last)
                        for n, (v, i, src, rest) in enumerate(rows):
                            last = dve.max_index(i[:, 8:16], v[:, 8:16], rest)
                            if n == ones - 1:
                                last.then_inc(halved, 1)
                        if len(rows) > ones:
                            link(last)
                        else:
                            dve.wait_ge(halved, r + 1)
                    if 0 <= r - 1 < UNITS:
                        u = r - 1
                        if u >= 2:
                            dve.wait_ge(parts_read, u - 1)
                        dve.tensor_scalar(part_u[:, u % 2, :, 0:TOPK], pos[:], 4, None, ALU.logical_shift_right)
                        dve.tensor_scalar(part_u[:, u % 2, :, TOPK:], pos[:], TOPK - 1, None, ALU.bitwise_and).then_inc(
                            parts_ready, 1)
                    if 0 <= r - 2 < UNITS:
                        u = r - 2
                        dve.wait_ge(parts_read, u + 1)
                        if u == 0:
                            dve.wait_ge(place_done, 1)
                        if u >= 2:
                            dve.wait_ge(looked_up, u - 1)
                        dve.tensor_tensor(pick[:, u % 2], part_b[:, u % 2].unsqueeze(1).broadcast_to((P, TOPK, LOOK)),
                                          place[:], ALU.is_equal).then_inc(marked, 1)

                for c in range(NPC):
                    if c >= 1:
                        for t in range(NT - 2):
                            pick_experts((c - 1) * NT + t)
                    st.split_lo(dve, 6 + 2 * c)
                    if c >= 1:
                        for t in range(NT - 2, NT):
                            pick_experts((c - 1) * NT + t)
                    st.split_lo(dve, 7 + 2 * c)
                for r in range((NPC - 1) * NT, UNITS + 2):
                    pick_experts(r)
                g = GATE[:].rearrange("p t (h j) -> p (t h) j", j=TOPK)
                dve.tensor_copy(gsum[:], g[:, :, 0]).then_inc(chain, 1)
                links += 1
                dve.wait_ge(chain, links)
                dve.tensor_tensor(g, g, gsum[:].unsqueeze(2).broadcast_to((P, NT * PH, TOPK)), ALU.subtract).then_inc(g_shift, 1)
                dve.wait_ge(g_exp, 1)
                link(dve.tensor_reduce(gsum[:], g, AX_X, ALU.add))
                link(dve.reciprocal(gsum[:], gsum[:]))
                link(dve.tensor_tensor(g, g, gsum[:].unsqueeze(2).broadcast_to((P, NT * PH, TOPK)), ALU.mult))
                dve.wait_ge(looked_up, UNITS)
                link(*[dve.scalar_tensor_tensor(out=IDX[:, :, q], in0=E12[:, ND + q, 0, :], scalar=float(NK),
                                                in1=E12[:, ND + q, 1, :], op0=ALU.mult, op1=ALU.add) for q in range(NG)])
                dve.wait_ge(h_done, 1)


def dense_gates(nc, E12, GATE, WD, lin, tr, A, ident):
    with ExitStack() as ctx:
        m = Pool(nc, ctx)
        keys = m.sb("keys", [P, NK])
        pairs = m.sb("pairs", [P, 3, SAMPLE])
        hot1, hot2 = m.sb("hot1", [P, 8, NK]), m.sb("hot2", [P, 8, NK])
        stage = m.sb("gate_stage", [P, 2, NK, WT])
        QUADS = P // 4
        keys_in, turned, copied = (m.sem(f"dg_{x}") for x in ("keys_in", "turned", "copied"))
        quad_free, quad_ready, bank_free, bank_ready = (
            m.sem(f"dg_{x}") for x in ("quad_free", "quad_ready", "bank_free", "bank_ready"))
        stored = [m.sem(f"dg_stored{i}") for i in range(2)]

        with nc.Block() as block:
            @block.sync
            def _(sp):
                sp.dma_start(keys[:], A["keys"]).then_inc(keys_in, 16)
                with sp.Fori(0, ND) as i:
                    for s in range(2):
                        sp.wait_ge(bank_free, i * QUADS + 4 + 16 * (s + 1))
                        sp.dma_start(WD[bass.ds(i * 2 + s, 1)].rearrange("a p e t -> p (a e t)"),
                                     stage[:, s].rearrange("p e t -> p (e t)")).then_inc(stored[s], 16)
                for s in range(2):
                    sp.wait_ge(stored[s], 16 * ND + 16)

            @block.tensor
            def _(pe):
                for j in range(3):
                    for t in range(ND):
                        src = GATE[:, t, :] if j == 2 else E12[:, t, j, :]
                        last = pe.transpose(lin[:, j, t * P:(t + 1) * P], src, ident[:])
                    last.then_inc(turned, 1)
                pe.wait_ge(copied, 3)
                with pe.Fori(0, ND) as i:
                    for q in range(QUADS):
                        pe.wait_ge(quad_ready, i * QUADS + q + 1)
                        pe.wait_ge(bank_free, i * QUADS + q + 1)
                        for n in range(4):
                            slot = (4 * q + n) % 8
                            last = pe.matmul(lin[:, q % 4, n * NK:(n + 1) * NK], hot2[:, slot, :], hot1[:, slot, :],
                                             start=True, stop=True)
                        last.then_inc(bank_ready, 1)

            @block.scalar
            def _(act):
                for j in range(3):
                    act.wait_ge(turned, j + 1)
                    act.activation(pairs[:, j, :], lin[:, j, :], ACT.Copy).then_inc(copied, 1)
                act.wait_ge(copied, 3)
                act.sem_inc(bank_free, 4)
                act.sem_inc(bank_ready, 2)
                for s in range(2):
                    act.sem_inc(stored[s], 16)
                with act.Fori(0, ND) as i:
                    for q in range(QUADS):
                        s = q // 16
                        if q % 16 == 0:
                            act.wait_ge(stored[s], i * 16 + 16)
                        act.wait_ge(bank_ready, i * QUADS + q + 3)
                        t0 = 4 * (q % 16)
                        act.activation(stage[:, s, :, t0:t0 + 4].rearrange("p e t -> p t e"),
                                       lin[:, q % 4, :].rearrange("p (t e) -> p t e", t=4), ACT.Copy).then_inc(bank_free, 1)

            @block.vector
            def _(dve):
                dve.wait_ge(keys_in, 16)
                dve.wait_ge(copied, 3)
                with dve.Fori(0, ND) as i:
                    for q in range(QUADS):
                        dve.wait_ge(bank_ready, i * QUADS + q + 1)
                        for n in range(4):
                            slot = (4 * q + n) % 8
                            col = i * P + (4 * q + n)
                            dve.tensor_scalar(hot1[:, slot, :], keys[:], pairs[:, 0, bass.ds(col, 1)],
                                              pairs[:, 2, bass.ds(col, 1)], ALU.is_equal, ALU.mult)
                            last = dve.tensor_scalar(hot2[:, slot, :], keys[:], pairs[:, 1, bass.ds(col, 1)], None, ALU.is_equal)
                        last.then_inc(quad_ready, 1)


def experts(nc, T, Y, H, IDX, GATE, WD, lin, tr, A):
    with ExitStack() as ctx:
        m = Pool(nc, ctx)
        raw_d, raw_u = m.sb("raw_d", [P, 2, KB, P]), m.sb("raw_u", [P, 2, D])
        d_hi, d_lo = m.sb("d_hi", [P, 2, KB, P], F32R), m.sb("d_lo", [P, 2, KB, P], F32R)
        u_hi, u_lo = m.sb("u_hi", [P, BG, D], F32R), m.sb("u_lo", [P, BG, D], F32R)
        c_hi, c_lo = m.sb("c_hi", [P, BG, SAMPLE], F32R), m.sb("c_lo", [P, BG, SAMPLE], F32R)
        wd = m.sb("wd", [P, SAMPLE // WT, BG, WT])
        gl = m.sb("gl", [P, 2, SAMPLE])
        rows = m.sb("rows", [P, 8, D])
        now = m.sb("now", [P, 2, 8], I32)
        dots_now = m.sb("dots_now", [P, 16])
        dots = m.sb("dots", [P, NE * NG])
        d_in = [m.sem(f"ex_d_in{i}") for i in range(2)]
        u_in = [m.sem(f"ex_u_in{i}") for i in range(2)]
        w_in = m.sem("ex_w_in")
        d_hid, d_lod, u_hid, u_lod, act_ready, gelued, weighted, c_hid, c_lod, y_ready, y_added = (
            m.sem(f"ex_{x}") for x in ("d_hi", "d_lo", "u_hi", "u_lo", "act_ready", "gelued", "weighted", "c_hi",
                                       "c_lo", "y_ready", "y_added"))
        rows_in = [m.sem(f"ex_row_in{i}") for i in range(8)]
        rows_free, dots_done, coef_gelu, coef_done, now_done = (
            m.sem(f"ex_{x}") for x in ("rows_free", "dots_done", "coef_gelu", "coef_done", "now_done"))
        HALF = NGRP // 2

        def first_group(g):
            return isinstance(g, int) and g == 0

        def groups(eng, body):
            body(0, "down", False)
            with eng.Fori(1, HALF) as g:
                body(g, "down", False)
            between = between_halves.get(eng)
            if between:
                between()
            with eng.Fori(HALF, NGRP - 1) as g:
                body(g, "up", False)
            body(NGRP - 1, "up", True)

        between_halves = {}

        with nc.Block() as block:
            @block.sync
            def _(sp):
                def load_d(g, b):
                    n = g * BG + b
                    if not (isinstance(g, int) and n < 2):
                        sp.wait_ge(d_lod, n - 1)
                    sp.dma_start(raw_d[:, b % 2], A["downT"][n] if isinstance(g, int) else
                                 A["downT"][bass.ds(n, 1)].rearrange("a p k e -> p (a k) e")).then_inc(d_in[b % 2], 16)

                def load_u(g, b):
                    n = g * BG + b
                    if not (isinstance(g, int) and n < 2):
                        sp.wait_ge(u_lod, n - 1)
                    sp.dma_start(raw_u[:, b % 2], A["up"][bass.ds(n * P, P), :]).then_inc(u_in[b % 2], 16)

                def body(g, kind, last):
                    load_d(g, 0)
                    load_d(g, 1)
                    load_u(g, 0)
                    load_u(g, 1)
                    if not first_group(g):
                        sp.wait_ge(weighted, g * BG)
                    sp.dma_start(wd[:].rearrange("p h e t -> p h (e t)"),
                                 WD[:, :, bass.ds(g * BG, BG), :].rearrange("h p e t -> p h (e t)")).then_inc(w_in, 16)
                    load_d(g, 2)
                    load_d(g, 3)
                    load_u(g, 2)
                    load_u(g, 3)

                groups(sp, body)

            @block.gpsimd
            def _(pool):
                def body(g, kind, last):
                    table = A["down"] if kind == "down" else A["up"]
                    first = g * 16 if kind == "down" else g * 16 - NE * NG
                    for j in range(2):
                        pool.wait_ge(rows_free, g * 16 + 8 * j + 1)
                        pool.tensor_copy(now[:, j, :], IDX[:].rearrange("p s q -> p (s q)")[:, bass.ds(first + 8 * j, 8)]).then_inc(
                            now_done, 1)
                        pool.wait_ge(now_done, g * 2 + j + 1)
                        for k in range(8):
                            pool.wait_ge(rows_free, g * 16 + 8 * j + k + 1)
                            pool.nop(nofuse=True)
                            pool.indirect_dma_start(rows[:, k, :], None, table, bass.IndirectOffsetOnAxis(
                                ap=now[:, j, k:k + 1], axis=0)).then_inc(rows_in[k], 16)

                groups(pool, body)

            @block.tensor
            def _(pe):
                def body(g, kind, last):
                    for b in range(BG):
                        pe.wait_ge(d_lod, g * BG + b + 1)
                        if b >= 2:
                            pe.wait_ge(gelued, g * BG + b - 1)
                        for k in range(KB):
                            mm = three(pe, tr[:, b % 2, :], (d_hi[:, b % 2, k, :], d_lo[:, b % 2, k, :]),
                                       (T[0][0][:, k, :], T[1][0][:, k, :]), start=(k == 0), stop=(k == KB - 1))
                        mm.then_inc(act_ready, 1)
                    if not first_group(g):
                        pe.wait_ge(y_added, g * 8)
                    for half in range(2):
                        cols = slice(half * CH, (half + 1) * CH)
                        for b in range(BG):
                            if half == 0:
                                pe.wait_ge(c_lod, g * BG + b + 1)
                                pe.wait_ge(u_lod, g * BG + b + 1)
                            for t in range(ND):
                                if half == 1 and b == 0 and t >= 2:
                                    pe.wait_ge(y_added, g * 8 + t - 1)
                                ts = slice(t * P, (t + 1) * P)
                                mm = three(pe, lin[:, (4 * half + t) % 6, :], (c_hi[:, b, ts], c_lo[:, b, ts]),
                                           (u_hi[:, b, cols], u_lo[:, b, cols]), start=(b == 0), stop=(b == BG - 1))
                                if b == BG - 1:
                                    mm.then_inc(y_ready, 1)

                groups(pe, body)

            @block.scalar
            def _(act):
                def down_hi(g, b):
                    act.wait_ge(d_in[b % 2], g * 32 + (b // 2 + 1) * 16)
                    act.activation(d_hi[:, b % 2], raw_d[:, b % 2], ACT.Copy).then_inc(d_hid, 1)

                def up_hi(g, b):
                    act.wait_ge(u_in[b % 2], g * 32 + (b // 2 + 1) * 16)
                    act.activation(u_hi[:, b], raw_u[:, b % 2], ACT.Copy).then_inc(u_hid, 1)

                def gelu(g, b):
                    act.wait_ge(act_ready, g * BG + b + 1)
                    if b >= 2:
                        act.wait_ge(weighted, g * BG + b - 1)
                    act.activation(gl[:, b % 2, :], tr[:, b % 2, :], ACT.Gelu_apprx_tanh).then_inc(gelued, 1)

                def coef_hi(g, b):
                    act.wait_ge(weighted, g * BG + b + 1)
                    act.activation(c_hi[:, b, :], gl[:, b % 2, :], ACT.Copy).then_inc(c_hid, 1)

                def body(g, kind, last):
                    if not first_group(g):
                        act.wait_ge(y_ready, g * 8)
                    for b in range(BG):
                        if b >= 1:
                            gelu(g, b - 1)
                            if b + 1 < BG:
                                down_hi(g, b + 1)
                        up_hi(g, b)
                        if b >= 1:
                            coef_hi(g, b - 1)
                    gelu(g, BG - 1)
                    coef_hi(g, BG - 1)
                    if not last:
                        down_hi(g + 1, 0)
                        down_hi(g + 1, 1)

                def between():
                    act.wait_ge(dots_done, HALF)
                    act.activation(dots[:], dots[:], ACT.Gelu_apprx_tanh).then_inc(coef_gelu, 1)

                between_halves[act] = between
                down_hi(0, 0)
                down_hi(0, 1)
                groups(act, body)

            @block.vector
            def _(dve):
                dve.memset(dots_now[:], 0.0).then_inc(rows_free, 8)

                def down_lo(g, b):
                    dve.wait_ge(d_hid, g * BG + b + 1)
                    dve.tensor_tensor(d_lo[:, b % 2], raw_d[:, b % 2], d_hi[:, b % 2].bitcast(F32),
                                      ALU.subtract).then_inc(d_lod, 1)

                def up_lo(g, b):
                    dve.wait_ge(u_hid, g * BG + b + 1)
                    dve.tensor_tensor(u_lo[:, b], raw_u[:, b % 2], u_hi[:, b].bitcast(F32),
                                      ALU.subtract).then_inc(u_lod, 1)

                def weigh(g, b):
                    dve.wait_ge(gelued, g * BG + b + 1)
                    if b == 0:
                        dve.wait_ge(w_in, g * 16 + 16)
                    v = gl[:, b % 2, :].rearrange("p (h t) -> p h t", t=WT)
                    dve.tensor_tensor(v, v, wd[:, :, b, :], ALU.mult).then_inc(weighted, 1)

                def coef_lo(g, b):
                    dve.wait_ge(c_hid, g * BG + b + 1)
                    dve.tensor_tensor(c_lo[:, b, :], gl[:, b % 2, :], c_hi[:, b, :].bitcast(F32),
                                      ALU.subtract).then_inc(c_lod, 1)

                def add(g, half, t):
                    cols = slice(half * CH, (half + 1) * CH)
                    dve.wait_ge(y_ready, g * 8 + 4 * half + t + 1)
                    dve.tensor_tensor(Y[:, t, cols], lin[:, (4 * half + t) % 6, :], Y[:, t, cols], ALU.add).then_inc(y_added, 1)

                def row(g, kind, n):
                    j, k = n // 8, n % 8
                    dve.wait_ge(rows_in[k], g * 32 + 16 * (j + 1))
                    q = k % 2
                    if kind == "down":
                        if n == 0 and not first_group(g):
                            dve.wait_ge(dots_done, g)
                        dve.tensor_tensor_reduce(rows[:, k, :], rows[:, k, :], H[:, q, :], 1.0, 0.0, ALU.mult, ALU.add,
                                                 dots_now[:, n:n + 1]).then_inc(rows_free, 1)
                        if n == 15:
                            dve.wait_ge(rows_free, g * 16 + 16 + 8)
                            dve.tensor_copy(dots[:, bass.ds(g * 16, 16)], dots_now[:]).then_inc(dots_done, 1)
                    else:
                        dve.wait_ge(rows_free, g * 16 + n + 7)
                        dve.scalar_tensor_tensor(out=Y[:, ND + q, :], in0=rows[:, k, :],
                                                 scalar=dots[:, bass.ds(g * 16 - NE * NG + n, 1)], in1=Y[:, ND + q, :],
                                                 op0=ALU.mult, op1=ALU.add).then_inc(rows_free, 1)

                def body(g, kind, last):
                    n = 0
                    for b in range(BG):
                        if b >= 1:
                            weigh(g, b - 1)
                            if b + 1 < BG:
                                down_lo(g, b + 1)
                        up_lo(g, b)
                        if b >= 1:
                            coef_lo(g, b - 1)
                        row(g, kind, n)
                        row(g, kind, n + 1)
                        n += 2
                    weigh(g, BG - 1)
                    coef_lo(g, BG - 1)
                    if not last:
                        down_lo(g + 1, 0)
                        down_lo(g + 1, 1)
                    for _ in range(4):
                        row(g, kind, n)
                        n += 1
                    for t in range(ND):
                        add(g, 0, t)
                    for _ in range(4):
                        row(g, kind, n)
                        n += 1
                    for t in range(ND):
                        add(g, 1, t)

                def between():
                    dve.wait_ge(coef_gelu, 1)
                    dve.tensor_tensor(dots[:].rearrange("p (s q) -> p q s", q=NG), dots[:].rearrange("p (s q) -> p q s", q=NG),
                                      GATE[:, ND:, :], ALU.mult).then_inc(coef_done, 1)
                    dve.wait_ge(coef_done, 1)

                between_halves[dve] = between
                down_lo(0, 0)
                down_lo(0, 1)
                groups(dve, body)


def final_norm(nc, Y, A, outs):
    with ExitStack() as ctx:
        m = Pool(nc, ctx)
        norm = Norm(nc, ctx, "final", Y, NT)
        row = m.sb("final_row", [P, D])
        row_in, stored = m.sem("final_row_in"), m.sem("stored")

        with nc.Block() as block:
            @block.sync
            def _(sp):
                sp.dma_start(row[:], A["final_row"].broadcast_to((P, D))).then_inc(row_in, 16)
                for t in range(NT):
                    sp.wait_ge(norm.scaled, norm.base + t + 1)
                    out, tt = (outs[0], t) if t < ND else (outs[1], t - ND)
                    sp.dma_start(out[tt * P:(tt + 1) * P, :], Y[:, t, :]).then_inc(stored, 16)
                sp.wait_ge(stored, 16 * NT)

            @block.scalar
            def _(act):
                norm.act(act)

            @block.vector
            def _(dve):
                dve.wait_ge(row_in, 16)
                norm.dve(dve, Y, row)


def layer(nc, A, outs):
    U, GA, GS = (nc.dram_tensor(x, (NT, P, D), F32).ap() for x in ("u_rows", "attn_gate_rows", "sg_gate_rows"))
    WD = nc.dram_tensor("dense_gates", (SAMPLE // WT, P, NK, WT), F32).ap()
    with ExitStack() as ctx:
        Pool.begin(ctx)
        m = Pool(nc, ctx)
        lin = ctx.enter_context(nc.psum_tensor("lin", [P, 6, CH], F32))
        tr = ctx.enter_context(nc.psum_tensor("tr", [P, 2, CH], F32))
        Y = m.sb("Y", [P, NT, D])
        GATE, IDX, H = m.sb("GATE", [P, NT, NE]), m.sb("IDX", [P, NE, NG], I32), m.sb("H", [P, NG, D])
        T_s = m.sb("Ts_hi", [P, KB, SAMPLE], F32R), m.sb("Ts_lo", [P, KB, SAMPLE], F32R)
        with ExitStack() as c0:
            n = Pool(nc, c0)
            ident, E12 = n.sb("ident", [P, P]), n.sb("E12", [P, NT, 2, NE])
            with ExitStack() as c1:
                n = Pool(nc, c1)
                T_p = n.sb("Tp_hi", [P, KB, PROMPT], F32R), n.sb("Tp_lo", [P, KB, PROMPT], F32R)
                T = (T_s[0], T_p[0]), (T_s[1], T_p[1])
                G = n.sb("G", [P, NT, D])
                with ExitStack() as c2:
                    k = Pool(nc, c2)
                    qT = G[:].rearrange("p t d -> p (t d)").rearrange("p (b n) -> p b n", b=KB)
                    kT, v_sb = k.sb("kT", [P, NKV, TOK]), k.sb("v_sb", [P, NT, NKV * HD])
                    mixer_inputs(nc, m, T, Y, qT, kT, v_sb, lin, tr, A, U, GA, GS, ident)
                    self_attention(nc, T, qT, kT, v_sb, ident, lin, tr)
                mixer_outputs(nc, T, Y, G, lin, A, U, GA, GS, ident)
                with ExitStack() as c2:
                    k = Pool(nc, c2)
                    keysT, vals = k.sb("keysT", [P, KB, NM * P]), k.sb("vals", [P, NM, D])
                    cross_inputs(nc, T, Y, G, keysT, vals, lin, A, ident)
                    cross_attention(nc, T, G, keysT, vals, ident, lin, tr)
                routing(nc, T, Y, G, H, E12, GATE, IDX, lin, tr, A, ident)
            dense_gates(nc, E12, GATE, WD, lin, tr, A, ident)
        experts(nc, T, Y, H, IDX, GATE, WD, lin, tr, A)
        final_norm(nc, Y, A, outs)


def rope_tables():
    nf = HD // 4
    pos = np.arange(SAMPLE)
    inv = (np.float32(10000.0) ** (-np.arange(nf, dtype=np.float32) / np.float32(nf))).astype(np.float32)
    ar = (pos // 64).astype(np.float32)[:, None] * inv
    ac = (pos % 64).astype(np.float32)[:, None] * inv
    cos = np.concatenate([np.cos(ar), np.cos(ar), np.cos(ac), np.cos(ac)], 1)
    sin = np.concatenate([-np.sin(ar), np.sin(ar), -np.sin(ac), np.sin(ac)], 1)
    return [np.ascontiguousarray(a.reshape(4, P, HD).transpose(1, 0, 2)).astype(np.float32) for a in (cos, sin)]


def chunks_of(w):
    return w.reshape(2, HK, P, -1, CH).transpose(3, 2, 0, 1, 4)


def kernel(**inputs):
    import concourse.bacc as bacc
    from concourse.bass_utils import run_bass_kernel_spmd as run

    a = {k: np.asarray(v) for k, v in inputs.items()}
    w_in = chunks_of(a["w_in"][0])
    wall = np.concatenate([w_in[2:3], w_in[0:2], w_in[3:]] + [chunks_of(a[x][0]) for x in (
        "w_attn_o", "w_sg_o", "w_out", "wkv_xa", "wq_xa", "wo_xa", "w_peer_q")])
    assert wall.shape[0] == W_END
    cos, sin = rope_tables()
    arrays = {
        "x": np.concatenate([a["x_sample"][0], a["x_prompt"][0]]),
        "mem": np.concatenate([a["mem_sample"][0], a["mem_prompt"][0]]),
        "wall": wall,
        "gains": np.stack([a[x][0].reshape(KB, P).T for x in ("norm_mix_g", "norm_xa_g", "norm_mem_g", "norm_ffn_g")], 1),
        "cos": cos, "sin": sin, "qg": a["q_norm_g"], "kg": a["k_norm_g"],
        "ident": np.eye(P, dtype=np.float32),
        "iota": np.broadcast_to(np.arange(TOPK, dtype=np.float32), (P, TOPK)),
        "sg_gain": a["sg_norm_g"], "sgw": a["sg_w"][0].transpose(2, 0, 1), "sgb": a["sg_b"][0].T,
        "ffn_row": a["norm_ffn_g"], "final_row": a["final_norm_g"][None],
        "subk": np.stack([a["peer_k1"][0], a["peer_k2"][0]], 1).transpose(3, 0, 1, 2).reshape(P, 2 * PH, NK),
        "keys": np.broadcast_to(np.arange(NK, dtype=np.float32), (P, NK)),
        "downT": a["expert_down"][0].reshape(NK, P, KB, P).transpose(0, 3, 2, 1),
        "down": a["expert_down"][0], "up": a["expert_up"][0],
    }
    arrays = {k: np.ascontiguousarray(v) for k, v in arrays.items()}
    nc = bacc.Bacc("TRN2", target_bir_lowering=False, num_devices=1)
    A = {k: nc.dram_tensor(f"in_{k}", v.shape, mybir.dt.from_np(v.dtype), kind="ExternalInput").ap()
         for k, v in arrays.items()}
    outs = [nc.dram_tensor(f"out_{n}", (s, D), F32, kind="ExternalOutput").ap()
            for n, s in (("sample", SAMPLE), ("prompt", PROMPT))]
    layer(nc, A, outs)
    r = run(nc, [{f"in_{k}": v for k, v in arrays.items()}], core_ids=[0])
    got = [r.results[0][f"out_{n}"] for n in ("sample", "prompt")]
    return got[1].reshape(1, PROMPT, D), got[0].reshape(1, SAMPLE, D)
```

```python
from contextlib import ExitStack

import numpy as np

import concourse.bass as bass
from concourse import mybir

F32 = mybir.dt.float32
F32R = mybir.dt.float32r
I32 = mybir.dt.int32
BF16 = mybir.dt.bfloat16
U32 = mybir.dt.uint32
ALU = mybir.AluOpType
ACT = mybir.ActivationFunctionType
AX_X = mybir.AxisListType.X

P = 128
D = 1024
KB = D // P
CH = 512
HK = KB // 2
SAMPLE, PROMPT = 512, 256
SEQS = [(0, SAMPLE // P), (SAMPLE // P, PROMPT // P)]
NT = (SAMPLE + PROMPT) // P
TOK = NT * P
NH, NKV, HD = 16, 4, 64
MEM = 256
XH, XD = 4, 256
NSEQ = 2
NM = NSEQ * MEM // P
G_SG = 8
PH, NK, TOPK = 8, 128, 16
NE = PH * TOPK
EPS = 1e-6
LOWEST = -3.4e38
ND = SAMPLE // P
NG = NT - ND
BG = 4
NGRP = NK // BG
WT = 64

W_KV, W_Q, W_U, W_VS, W_GA, W_GS = 0, 1, 3, 5, 7, 9
W_AO, W_SO, W_OUT, W_XKV, W_XQ, W_XO, W_PQ, W_END = 11, 13, 15, 17, 21, 23, 25, 29


class Pool:

    semaphores = None
    shared = {}

    @classmethod
    def begin(cls, ctx):
        cls.semaphores, cls.shared = ctx, {}

    def carried(self, name, increments):
        if name not in Pool.shared:
            Pool.shared[name] = [self.sem(name), 0]
        sem, base = Pool.shared[name]
        Pool.shared[name][1] = base + increments
        return sem, base

    def __init__(self, nc, ctx):
        self.nc, self.ctx = nc, ctx

    def sb(self, name, shape, dt=F32):
        return self.ctx.enter_context(self.nc.sbuf_tensor(name, shape, dt))

    def sem(self, name):
        return Pool.semaphores.enter_context(self.nc.semaphore(name))


class Stream:

    def __init__(self, nc, ctx, wall):
        self.wall, self.n = wall, 2 * W_END
        m = Pool(nc, ctx)
        self.raw = m.sb("w_raw", [P, 2, HK, CH])
        self.hi = m.sb("w_hi", [P, 2, HK, CH], F32R)
        self.lo = m.sb("w_lo", [P, 2, HK, CH], F32R)
        self.loaded = [m.sem(f"w_loaded{i}") for i in range(2)]
        self.hi_done, self.lo_done = m.sem("w_hi_done"), m.sem("w_lo_done")
        self.used = m.sem("w_used")

    def load(self, sp, first, end):
        for h in range(first, end):
            if h >= 2:
                sp.wait_ge(self.lo_done, h - 1)
            sp.dma_start(self.raw[:, h % 2], self.wall[h // 2, :, h % 2]).then_inc(self.loaded[h % 2], 16)

    def split_hi(self, act, h):
        if h >= self.n:
            return
        act.wait_ge(self.loaded[h % 2], 16 * (h // 2 + 1))
        if h >= 2 and h % 2 == 0:
            act.wait_ge(self.used, h // 2)
        act.activation(self.hi[:, h % 2], self.raw[:, h % 2], ACT.Copy).then_inc(self.hi_done, 1)

    def split_lo(self, dve, h):
        if h >= self.n:
            return
        dve.wait_ge(self.hi_done, h + 1)
        dve.tensor_tensor(self.lo[:, h % 2], self.raw[:, h % 2], self.hi[:, h % 2].bitcast(F32),
                          ALU.subtract).then_inc(self.lo_done, 1)


class Outputs:

    def __init__(self, nc, ctx, tag):
        m = Pool(nc, ctx)
        self.ready = m.sem(f"{tag}_ready")
        self.freed = m.sem(f"{tag}_freed")


def part(T, k, cols):
    if cols.stop <= SAMPLE:
        return T[0][:, k, cols]
    return T[1][:, k, cols.start - SAMPLE:cols.stop - SAMPLE]


def three(pe, out, lhs, rhs, start, stop):
    pe.matmul(out, lhs[0], rhs[0], start=start, stop=False, skip_group_check=True)
    pe.matmul(out, lhs[0], rhs[1], start=False, stop=False, skip_group_check=True)
    return pe.matmul(out, lhs[1], rhs[0], start=False, stop=stop, skip_group_check=True)


def project_tokens(pe, st, h0, nchunks, T, tiles, lin, o, between=None):
    n = len(tiles)
    for c in range(nchunks):
        for half in range(2):
            h = h0 + 2 * c + half
            pe.wait_ge(st.lo_done, h + 1)
            for i, t in enumerate(tiles):
                if half == 0 and c > 0:
                    pe.wait_ge(o.freed, n * (c - 1) + i + 1)
                for k in range(HK):
                    cols = slice(t * P, (t + 1) * P)
                    kk = half * HK + k
                    last = three(pe, lin[:, i, :], (part(T[0], kk, cols), part(T[1], kk, cols)),
                                 (st.hi[:, h % 2, k, :], st.lo[:, h % 2, k, :]),
                                 start=(kk == 0), stop=(kk == KB - 1))
                if half == 1:
                    last.then_inc(o.ready, 1)
                elif i == n - 1:
                    last.then_inc(st.used, 1)
                if half == 0 and between is not None:
                    between(c, i)


def project_features(pe, st, h0, nchunks, T, groups, lin, o, between=None):
    n = len(groups)
    for c in range(nchunks):
        for half in range(2):
            h = h0 + 2 * c + half
            pe.wait_ge(st.lo_done, h + 1)
            for i, (bank, col, first, cb, cols, need) in enumerate(groups):
                if half == 0 and c > 0:
                    pe.wait_ge(o.freed, n * (c - 1) + need)
                for k in range(HK):
                    kk = half * HK + k
                    fs = slice(cb * P, (cb + 1) * P)
                    last = three(pe, lin[:, bank, col:col + cols.stop - cols.start],
                                 (st.hi[:, h % 2, k, fs], st.lo[:, h % 2, k, fs]),
                                 (part(T[0], kk, cols), part(T[1], kk, cols)),
                                 start=(kk == 0 and first), stop=(kk == KB - 1))
                if half == 1:
                    last.then_inc(o.ready, 1)
                elif i == n - 1:
                    last.then_inc(st.used, 1)
                if between is not None:
                    between(c, half, i)


FEATURES = [(cb, 0, True, cb, slice(0, SAMPLE), cb + 1) for cb in range(4)] + [
    (4 + cb // 2, (cb % 2) * PROMPT, cb % 2 == 0, cb, slice(SAMPLE, TOK), 6 if cb < 2 else 8)
    for cb in range(4)]


class Turn:

    def __init__(self, nc, ctx, tag, src, T, lin, ident, gain, tiles):
        m = Pool(nc, ctx)
        self.src, self.T, self.lin, self.ident, self.gain = src, T, lin, ident, gain
        self.steps = [(k, t0, min(4, tiles - t0)) for t0 in range(0, tiles, 4) for k in range(KB)]
        (self.turned, self.base), (self.hi, _), (self.lo, _) = (
            m.carried(x, len(self.steps)) for x in ("turned", "turn_hi", "turn_lo"))

    def pe(self, pe, before=None):
        for n, (k, t0, nt) in enumerate(self.steps):
            if before is not None:
                before(n, t0 + nt)
            if n >= 6:
                pe.wait_ge(self.lo, self.base + n - 5)
            for t in range(nt):
                last = pe.transpose(self.lin[:, n % 6, t * P:(t + 1) * P],
                                    self.src[:, t0 + t, k * P:(k + 1) * P], self.ident[:])
            last.then_inc(self.turned, 1)

    def act(self, act):
        for n, (k, t0, nt) in enumerate(self.steps):
            act.wait_ge(self.turned, self.base + n + 1)
            scale = 1.0 if self.gain is None else self.gain[:, k:k + 1]
            act.activation(part(self.T[0], k, slice(t0 * P, (t0 + nt) * P)), self.lin[:, n % 6, 0:nt * P], ACT.Copy,
                           scale=scale).then_inc(self.hi, 1)

    def dve(self, dve):
        for n, (k, t0, nt) in enumerate(self.steps):
            dve.wait_ge(self.hi, self.base + n + 1)
            scale = 1.0 if self.gain is None else self.gain[:, k:k + 1]
            cols = slice(t0 * P, (t0 + nt) * P)
            dve.scalar_tensor_tensor(out=part(self.T[1], k, cols), in0=self.lin[:, n % 6, 0:nt * P], scalar=scale,
                                     in1=part(self.T[0], k, cols).bitcast(F32), op0=ALU.mult,
                                     op1=ALU.subtract).then_inc(self.lo, 1)

    def wait(self, eng):
        eng.wait_ge(self.lo, self.base + len(self.steps))


class Norm:

    def __init__(self, nc, ctx, tag, src, tiles, junk=None):
        m = Pool(nc, ctx)
        self.src, self.tiles = src, tiles
        self.junk = m.sb(f"{tag}_squares", [P, D])[:] if junk is None else junk
        self.ss, self.ms, self.sd, self.rstd = (m.sb(f"{tag}_{x}", [P, tiles]) for x in ("ss", "ms", "sd", "rstd"))
        (self.summed, self.base), (self.meaned, _), (self.rooted, _), (self.inverted, _), (self.scaled, _) = (
            m.carried(f"norm_{x}", tiles) for x in ("summed", "meaned", "rooted", "inverted", "scaled"))

    def act(self, act, before=None):
        for t in range(self.tiles + 1):
            if t < self.tiles:
                if before is not None:
                    before(t)
                if t > 0:
                    act.wait_ge(self.summed, self.base + t)
                act.activation(self.junk, self.src[:, t, :], ACT.Square,
                               accum_out=self.ss[:, t:t + 1]).then_inc(self.summed, 1)
            if t > 0:
                act.wait_ge(self.meaned, self.base + t)
                act.activation(self.sd[:, t - 1:t], self.ms[:, t - 1:t], ACT.Sqrt).then_inc(self.rooted, 1)

    def step(self, dve, t, dst, row=None):
        if t < self.tiles:
            dve.wait_ge(self.summed, self.base + t + 1)
            dve.tensor_scalar(self.ms[:, t:t + 1], self.ss[:, t:t + 1], 1.0 / D, EPS, ALU.mult, ALU.add).then_inc(
                self.meaned, 1)
        if t > 0:
            t -= 1
            dve.wait_ge(self.rooted, self.base + t + 1)
            dve.reciprocal(self.rstd[:, t:t + 1], self.sd[:, t:t + 1]).then_inc(self.inverted, 1)
            dve.wait_ge(self.inverted, self.base + t + 1)
            if row is None:
                dve.tensor_scalar(dst[:, t, :], self.src[:, t, :], self.rstd[:, t:t + 1], None,
                                  ALU.mult).then_inc(self.scaled, 1)
            else:
                dve.scalar_tensor_tensor(out=dst[:, t, :], in0=self.src[:, t, :], scalar=self.rstd[:, t:t + 1],
                                         in1=row[:], op0=ALU.mult, op1=ALU.mult).then_inc(self.scaled, 1)

    def dve(self, dve, dst, row=None):
        for t in range(self.tiles + 1):
            self.step(dve, t, dst, row)

    def wait(self, eng):
        eng.wait_ge(self.scaled, self.base + self.tiles)


def mixer_inputs(nc, st, T, Y, qT, kT, v_sb, lin, tr, A, U, GA, GS, ident, gains):
    with ExitStack() as ctx:
        mm = Pool(nc, ctx)
        rope = mm.sb("rope", [P, 2, CH])
        norm = Norm(nc, ctx, "mix", Y, NT, rope[:].rearrange("p a b -> p (a b)"))
        turn = Turn(nc, ctx, "mix", Y, T, lin, ident, gains[:, 0, :], NT)
        cos, sin = mm.sb("cos", [P, 4, HD]), mm.sb("sin", [P, 4, HD])
        qg, kg = mm.sb("qg", [P, HD]), mm.sb("kg", [P, HD])
        gcos, gsin = mm.sb("gcos", [P, 2, 4, HD]), mm.sb("gsin", [P, 2, 4, HD])
        sq = mm.sb("sq", [P, 2, CH])
        hss, hms, hsd, hr = (mm.sb(x, [P, 2, 8]) for x in ("hss", "hms", "hsd", "hr"))
        qn, ra, rb = mm.sb("qn", [P, CH]), mm.sb("ra", [P, CH]), mm.sb("rb", [P, CH])
        STG = 2
        stage = mm.sb("stage", [P, STG, CH])
        x_in = [mm.sem(f"x_in{t}") for t in range(NT)]
        turn_in, small_in, table_done = mm.sem("turn_in"), mm.sem("small_in"), mm.sem("table_done")
        o = Outputs(nc, ctx, "in")
        sq_done, hs_done, ms_done, sd_done, hr_done = (mm.sem(x) for x in ("sq_done", "hs_done", "hms_done", "hsd_done", "hr_done"))
        part, roped, turned, copied = (mm.sem(x) for x in ("rope_part", "roped", "qk_turned", "qk_copied"))
        spilled = [mm.sem(f"spilled{i}") for i in range(STG)]
        NQ = 3 * NT
        NALL = 11 * NT
        spills = [n for n in range(NQ, NALL) if not 5 * NT <= n < 7 * NT]

        def wait_odd(eng, h):
            if h >= 2 and h % 2 == 1 and h < st.n:
                eng.wait_ge(o.ready, NT * (h // 2))

        with nc.Block() as block:
            @block.sync
            def _(sp):
                for t in range(NT):
                    sp.dma_start(Y[:, t, :], A["x"][t * P:(t + 1) * P, :]).then_inc(x_in[t], 16)
                st.load(sp, 0, 2 * W_AO + 2)

            @block.gpsimd
            def _(pool):
                for dst, src in ((ident[:], A["ident"]), (gains[:], A["gains"])):
                    pool.dma_start(dst, src).then_inc(turn_in, 16)
                for dst, src in ((cos[:], A["cos"]),
                                 (sin[:], A["sin"]), (qg[:], A["qg"].broadcast_to((P, HD))),
                                 (kg[:], A["kg"].broadcast_to((P, HD)))):
                    pool.dma_start(dst, src).then_inc(small_in, 16)
                for i, n in enumerate(spills):
                    c, t = n // NT, n % NT
                    dst = U if c < 5 else GA if c < 9 else GS
                    pool.wait_ge(o.freed, n + 1)
                    pool.dma_start(dst[t, :, (c + 1) % 2 * CH:((c + 1) % 2 + 1) * CH], stage[:, i % STG, :]).then_inc(
                        spilled[i % STG], 16)
                for i in range(STG):
                    pool.wait_ge(spilled[i], 16 * len(spills[i::STG]))

            @block.tensor
            def _(pe):
                pe.wait_ge(turn_in, 32)
                turn.pe(pe, lambda n, end: pe.wait_ge(norm.scaled, norm.base + end))
                turn.wait(pe)

                def qk_turn(n):
                    pe.wait_ge(roped, n + 1)
                    if n >= 2:
                        pe.wait_ge(copied, n - 1)
                    for b in range(4):
                        last = pe.transpose(tr[:, n % 2, b * P:(b + 1) * P], rope[:, n % 2, b * P:(b + 1) * P], ident[:])
                    last.then_inc(turned, 1)

                def between(c, i):
                    if 1 <= c <= 3:
                        qk_turn((c - 1) * NT + i)

                project_tokens(pe, st, 0, W_AO, T, range(NT), lin, o, between)

            @block.scalar
            def _(act):
                norm.act(act, before=lambda t: act.wait_ge(x_in[t], 16))
                act.wait_ge(turn_in, 32)
                turn.act(act)
                st.split_hi(act, 0)
                st.split_hi(act, 1)

                def root(n):
                    act.wait_ge(ms_done, n + 1)
                    act.activation(hsd[:, n % 2, :], hms[:, n % 2, :], ACT.Sqrt).then_inc(sd_done, 1)

                def copy(n):
                    c, t = n // NT, n % NT
                    act.wait_ge(turned, n + 1)
                    src = tr[:, n % 2, :].rearrange("p (b f) -> p b f", b=4)
                    dst = (kT[:, :, t * P:(t + 1) * P] if c == 0 else
                           qT[:, 4 * (c - 1):4 * c, t * P:(t + 1) * P])
                    act.activation(dst, src, ACT.Copy).then_inc(copied, 1)

                for c in range(11):
                    if 1 <= c <= 3:
                        for t in range(NT):
                            copy((c - 1) * NT + t)
                    st.split_hi(act, 2 * c + 2)
                    for t in range(NT):
                        n = c * NT + t
                        act.wait_ge(o.ready, n + 1)
                        if n == NQ:
                            act.wait_ge(o.freed, NQ)
                        if n < NQ:
                            w = CH // 2 if c == 0 else CH
                            if c == 0:
                                act.activation(v_sb[:, t, :], lin[:, t, CH // 2:CH], ACT.Copy)
                            act.activation(sq[:, n % 2, 0:w], lin[:, t, 0:w], ACT.Square).then_inc(sq_done, 1)
                            if t >= 1:
                                root(n - 1)
                            if t == NT - 1:
                                root(n)
                        elif 5 <= c < 7:
                            act.activation(Y[:, t, (c - 5) * CH:(c - 4) * CH], lin[:, t, :],
                                           ACT.Gelu_apprx_tanh).then_inc(o.freed, 1)
                        else:
                            i = spills.index(n)
                            if i >= STG:
                                act.wait_ge(spilled[i % STG], 16 * (i // STG))
                            act.activation(stage[:, i % STG, :], lin[:, t, :],
                                           ACT.Gelu_apprx_tanh if c < 5 else ACT.Sigmoid).then_inc(o.freed, 1)
                    wait_odd(act, 2 * c + 3)
                    st.split_hi(act, 2 * c + 3)

            @block.vector
            def _(dve):
                norm.dve(dve, Y)
                dve.wait_ge(turn_in, 32)
                turn.dve(dve)
                st.split_lo(dve, 0)
                st.split_lo(dve, 1)
                dve.wait_ge(small_in, 64)
                for j, g in enumerate((kg, qg)):
                    gb = g[:].unsqueeze(1).broadcast_to((P, 4, HD))
                    dve.tensor_tensor(gcos[:, j], cos[:], gb, ALU.mult).then_inc(table_done, 1)
                    gv = g[:].rearrange("p (a b f) -> p a b f", a=2, b=2)
                    sv = sin[:].rearrange("p n (a b f) -> p n a b f", a=2, b=2)
                    ov = gsin[:, j].rearrange("p n (a b f) -> p n a b f", a=2, b=2)
                    for b in range(2):
                        for a in range(2):
                            dve.tensor_tensor(ov[:, :, a, b, :], sv[:, :, a, b, :],
                                              gv[:, a, 1 - b, :].unsqueeze(1).broadcast_to((P, 4, 16)),
                                              ALU.mult).then_inc(table_done, 1)
                dve.wait_ge(table_done, 10)
                nparts = 0

                def rotate(n):
                    nonlocal nparts
                    c, t = n // NT, n % NT
                    nh = 4 if c == 0 else 8
                    w = nh * HD
                    pos = t if t < 4 else t - 4
                    j = 0 if c == 0 else 1
                    dve.wait_ge(sd_done, n + 1)
                    dve.reciprocal(hr[:, n % 2, :], hsd[:, n % 2, :]).then_inc(hr_done, 1)
                    dve.wait_ge(hr_done, n + 1)
                    src = lin[:, t, 0:w].rearrange("p (h f) -> p h f", h=nh)
                    r = hr[:, n % 2, 0:nh].unsqueeze(2).broadcast_to((P, nh, HD))
                    q = qn[:, 0:w].rearrange("p (h f) -> p h f", h=nh)
                    dve.tensor_tensor(q, src, r, ALU.mult).then_inc(o.freed, 1)
                    dve.wait_ge(o.freed, n + 1)
                    cb = gcos[:, j, pos].unsqueeze(1).broadcast_to((P, nh, HD))
                    dve.tensor_tensor(ra[:, 0:w].rearrange("p (h f) -> p h f", h=nh), q, cb, ALU.mult).then_inc(part, 1)
                    qv = qn[:, 0:w].rearrange("p (h a b f) -> p h a b f", h=nh, a=2, b=2)
                    bv = rb[:, 0:w].rearrange("p (h a b f) -> p h a b f", h=nh, a=2, b=2)
                    gv = gsin[:, j, pos].rearrange("p (a b f) -> p a b f", a=2, b=2)
                    for b in range(2):
                        sb = gv[:, :, b, :].unsqueeze(1).broadcast_to((P, nh, 2, 16))
                        dve.tensor_tensor(bv[:, :, :, b, :], qv[:, :, :, 1 - b, :], sb, ALU.mult).then_inc(part, 1)
                    nparts += 3
                    dve.wait_ge(part, nparts)
                    if n >= 2:
                        dve.wait_ge(turned, n - 1)
                    if c == 0:
                        for dup in range(2):
                            dst = rope[:, n % 2, :].rearrange("p (h u f) -> p h u f", h=nh, u=2)[:, :, dup, :]
                            last = dve.tensor_tensor(dst, ra[:, 0:w].rearrange("p (h f) -> p h f", h=nh),
                                                     rb[:, 0:w].rearrange("p (h f) -> p h f", h=nh), ALU.add)
                    else:
                        last = dve.tensor_tensor(rope[:, n % 2, :], ra[:], rb[:], ALU.add)
                    last.then_inc(roped, 1)
                    dve.wait_ge(roped, n + 1)

                for c in range(11):
                    st.split_lo(dve, 2 * c + 2)
                    for t in range(NT):
                        n = c * NT + t
                        if n < NQ:
                            nh = 4 if c == 0 else 8
                            dve.wait_ge(sq_done, n + 1)
                            if n == 0:
                                dve.memset(hss[:], 1.0).then_inc(hs_done, 1)
                                dve.wait_ge(hs_done, 1)
                            dve.tensor_reduce(hss[:, n % 2, 0:nh],
                                              sq[:, n % 2, 0:nh * HD].rearrange("p (h f) -> p h f", h=nh),
                                              AX_X, ALU.add).then_inc(hs_done, 1)
                            dve.wait_ge(hs_done, n + 2)
                            dve.tensor_scalar(hms[:, n % 2, :], hss[:, n % 2, :], 1.0 / HD, EPS, ALU.mult,
                                              ALU.add).then_inc(ms_done, 1)
                            if t >= 1:
                                rotate(n - 1)
                            if t == NT - 1:
                                rotate(n)
                    st.split_lo(dve, 2 * c + 3)



def attention(nc, tag, T, ident, lin, tr, units, heads, outs, width_of, scores_of, scale):
    with ExitStack() as ctx:
        m = Pool(nc, ctx)
        KMAX = max(width_of(u) for u in units)
        probs = m.sb(f"{tag}_probs", [P, 3, KMAX])
        pT = m.sb(f"{tag}_probsT", [P, 3, KMAX // P, P])
        mx, nmx, rs, rr = (m.sb(f"{tag}_{x}", [P, 3]) for x in ("mx", "nmx", "rs", "rr"))
        scored, maxed, negated, exped, inverted, normed, turned, copied, valued, out_hi, out_lo = (
            m.sem(f"{tag}_{x}") for x in ("scored", "maxed", "negated", "exped", "inverted", "normed", "turned",
                                          "copied", "valued", "out_hi", "out_lo"))
        N = len(units)
        head_of = {(s, h): i for i, (s, h) in enumerate(heads)}
        last_unit = [max(u for u, x in enumerate(units) if x[:2] == sh) for sh in heads]
        banks = [p for p in outs if p["ends"]]
        bank_units = [last_unit[p["head"]] + 1 for p in banks]

        with nc.Block() as block:
            @block.tensor
            def _(pe):
                def scores(u):
                    if u >= 3:
                        pe.wait_ge(exped, u - 2)
                    pairs = scores_of(units[u])
                    for i, (a, b) in enumerate(pairs):
                        last = pe.matmul(lin[:, u % 3, 0:width_of(units[u])], a, b, start=(i == 0),
                                         stop=(i == len(pairs) - 1))
                    last.then_inc(scored, 1)

                def turn(u):
                    pe.wait_ge(normed, u + 1)
                    if u >= 3:
                        pe.wait_ge(copied, u - 2)
                    for kb in range(width_of(units[u]) // P):
                        last = pe.transpose(lin[:, 3 + u % 3, kb * P:(kb + 1) * P],
                                            probs[:, u % 3, kb * P:(kb + 1) * P], ident[:])
                    last.then_inc(turned, 1)

                def values(u):
                    pe.wait_ge(copied, u + 1)
                    h, t = head_of[units[u][:2]], units[u][2]
                    for p in (p for p in outs if p["head"] == h):
                        if t == 0 and p["opens"] and p["bank"] >= 2:
                            pe.wait_ge(out_lo, p["bank"] - 1)
                        for kb, v in enumerate(p["values"]):
                            last = pe.matmul(tr[p["rows"], p["bank"] % 2, t * P:(t + 1) * P], v, pT[:, u % 3, kb, :],
                                             start=(kb == 0), stop=(kb == len(p["values"]) - 1))
                    last.then_inc(valued, 1)

                for step in range(N + 3):
                    if step < N:
                        scores(step)
                    if 2 <= step < N + 2:
                        turn(step - 2)
                    if 3 <= step:
                        values(step - 3)

            @block.scalar
            def _(act):
                def exp(u):
                    w = width_of(units[u])
                    act.wait_ge(negated, u + 1)
                    if u >= 3:
                        act.wait_ge(turned, u - 2)
                    act.activation(probs[:, u % 3, 0:w], lin[:, u % 3, 0:w], ACT.Exp, bias=nmx[:, u % 3:u % 3 + 1],
                                   scale=scale, accum_out=rs[:, u % 3:u % 3 + 1]).then_inc(exped, 1)

                def copy(u):
                    kbs = width_of(units[u]) // P
                    act.wait_ge(turned, u + 1)
                    if u >= 3:
                        act.wait_ge(valued, u - 2)
                    act.activation(pT[:, u % 3, 0:kbs, :],
                                   lin[:, 3 + u % 3, 0:kbs * P].rearrange("p (k q) -> p k q", k=kbs),
                                   ACT.Copy).then_inc(copied, 1)

                for step in range(N + 4):
                    for n, p in enumerate(banks):
                        if step == bank_units[n] + 3:
                            act.wait_ge(valued, bank_units[n])
                            act.activation(part(T[0], p["block"], p["cols"]),
                                           tr[:, n % 2, 0:p["cols"].stop - p["cols"].start], ACT.Copy).then_inc(out_hi, 1)
                    if 3 <= step < N + 3:
                        copy(step - 3)
                    if step < N:
                        exp(step)

            @block.vector
            def _(dve):
                def norm(u):
                    w = width_of(units[u])
                    i = u % 3
                    dve.wait_ge(exped, u + 1)
                    dve.reciprocal(rr[:, i:i + 1], rs[:, i:i + 1]).then_inc(inverted, 1)
                    dve.wait_ge(inverted, u + 1)
                    dve.tensor_scalar(probs[:, i, 0:w], probs[:, i, 0:w], rr[:, i:i + 1], None,
                                      ALU.mult).then_inc(normed, 1)

                for step in range(N + 4):
                    for n, p in enumerate(banks):
                        if step == bank_units[n] + 3:
                            cols = p["cols"]
                            dve.wait_ge(out_hi, n + 1)
                            dve.tensor_tensor(part(T[1], p["block"], cols), tr[:, n % 2, 0:cols.stop - cols.start],
                                              part(T[0], p["block"], cols).bitcast(F32), ALU.subtract).then_inc(out_lo, 1)
                    if step < N:
                        w = width_of(units[step])
                        i = step % 3
                        dve.wait_ge(scored, step + 1)
                        dve.reduce_max(mx[:, i:i + 1], lin[:, i, 0:w], AX_X).then_inc(maxed, 1)
                        dve.wait_ge(maxed, step + 1)
                        dve.tensor_scalar(nmx[:, i:i + 1], mx[:, i:i + 1], -scale, None, ALU.mult).then_inc(negated, 1)
                    if 1 <= step < N + 1:
                        norm(step - 1)


def self_attention(nc, T, qT, kT, v_sb, ident, lin, tr):
    heads = [(s, h) for s in range(NSEQ) for h in range(NH)]
    units = [(s, h, t) for s, h in heads for t in range(SEQS[s][1])]
    span = lambda s: slice(SEQS[s][0] * P, sum(SEQS[s]) * P)
    kv_of = lambda h: h // (NH // NKV)

    def scores_of(u):
        s, h, t = u
        t0 = SEQS[s][0]
        rows = slice(h % 2 * HD, (h % 2 + 1) * HD)
        return [(qT[rows, h // 2, (t0 + t) * P:(t0 + t + 1) * P], kT[rows, kv_of(h), span(s)])]

    outs = [{"head": i, "bank": i // 2, "rows": slice(h % 2 * HD, (h % 2 + 1) * HD), "opens": h % 2 == 0,
             "ends": h % 2 == 1, "block": h // 2, "cols": span(s),
             "values": [v_sb[:, t, kv_of(h) * HD:(kv_of(h) + 1) * HD] for t in range(SEQS[s][0], sum(SEQS[s]))]}
            for i, (s, h) in enumerate(heads)]
    attention(nc, "att", T, ident, lin, tr, units, heads, outs, lambda u: SEQS[u[0]][1] * P, scores_of, HD ** -0.5)


def mixer_outputs(nc, st, T, Y, G, lin, A, U, GA, GS, ident):
    with ExitStack() as ctx:
        m = Pool(nc, ctx)
        norm = Norm(nc, ctx, "sg", Y, NT)
        M = G[:, 0:NM, :]
        norm_m = Norm(nc, ctx, "mem", M, NM, norm.junk)
        m_in = [m.sem(f"m_in{t}") for t in range(NM)]
        sgn = m.sb("sg_gain", [P, D])
        sgw, sgb = m.sb("sgw", [P, G_SG, P]), m.sb("sgb", [P, G_SG])
        RING = 3
        side = m.sb("side", [P, RING, CH])
        ug = m.sb("ug", [P, 2, NT, P])
        tmp = m.sb("tmp", [P, CH])
        turn_s = Turn(nc, ctx, "sgt", Y, T, lin, ident, None, NT)
        turn_g = Turn(nc, ctx, "mixt", G, T, lin, ident, None, NT)
        small_in = m.sem("sg_small_in")
        side_in = [m.sem(f"side_in{i}") for i in range(RING)]
        side_used = m.sem("side_used")
        ug_in = [m.sem(f"ug_in{i}") for i in range(2)]
        o, o2, o3 = (Outputs(nc, ctx, x) for x in ("attn_o", "sg_o", "mix_o"))
        sg_ready, sg_done, tmp_done = m.sem("sg_ready"), m.sem("sg_done"), m.sem("sg_tmp")
        NO = 2 * NT
        SGP = [(g, t0, n) for g in range(G_SG) for t0, n in SEQS]

        with nc.Block() as block:
            @block.sync
            def _(sp):
                st.load(sp, 2 * W_AO + 2, 2 * W_OUT + 2)
                turn_g.wait(sp)
                for t in range(NM):
                    sp.dma_start(M[:, t, :], A["mem"][t * P:(t + 1) * P, :]).then_inc(m_in[t], 16)
                st.load(sp, 2 * W_OUT + 2, 2 * W_XKV + 2)

            @block.gpsimd
            def _(pool):
                for dst, src in ((sgn[:], A["sg_gain"].broadcast_to((P, D))), (sgw[:], A["sgw"]), (sgb[:], A["sgb"])):
                    pool.dma_start(dst, src).then_inc(small_in, 16)
                for g in range(2):
                    pool.dma_start(ug[:, g], U[:, :, g * P:(g + 1) * P].rearrange("t p f -> p t f")).then_inc(ug_in[g], 16)
                for n in range(3 * NO):
                    j, c, t = n // NO, n // NT % 2, n % NT
                    if j == 1 and n % NO == 0:
                        for g in range(2, G_SG):
                            pool.wait_ge(sg_done, 2 * g - 2)
                            pool.dma_start(ug[:, g % 2], U[:, :, g * P:(g + 1) * P].rearrange("t p f -> p t f")).then_inc(
                                ug_in[g % 2], 16)
                    if n >= RING:
                        r = n - RING
                        pool.wait_ge((o.freed, side_used, o3.freed)[r // NO], r % NO + 1)
                    src = (GA[t], GS[t], A["x"][t * P:(t + 1) * P, :])[j]
                    pool.dma_start(side[:, n % RING, :], src[:, c * CH:(c + 1) * CH]).then_inc(side_in[n % RING], 16)

            @block.tensor
            def _(pe):
                project_tokens(pe, st, 2 * W_AO, 2, T, range(NT), lin, o)
                norm.wait(pe)
                pe.wait_ge(small_in, 48)
                pe.wait_ge(o.freed, NO)
                for n, (g, t0, nt) in enumerate(SGP):
                    if n >= 6:
                        pe.wait_ge(sg_done, n - 5)
                    pe.matmul(lin[:, n % 6, 0:nt * P], sgw[:, g, :], Y[:, t0:t0 + nt, g * P:(g + 1) * P], start=True,
                              stop=True).then_inc(sg_ready, 1)
                pe.wait_ge(sg_done, len(SGP))
                turn_s.pe(pe)
                turn_s.wait(pe)
                project_tokens(pe, st, 2 * W_SO, 2, T, range(NT), lin, o2)

                def summed(n, end):
                    pe.wait_ge(side_used, NT + end)
                    if n < NT:
                        pe.wait_ge(o2.freed, NT + n + 1)
                turn_g.pe(pe, summed)
                turn_g.wait(pe)
                project_tokens(pe, st, 2 * W_OUT, 2, T, range(NT), lin, o3)

            @block.scalar
            def _(act):
                norm.act(act)
                for j, oo in enumerate((o, o2, o3)):
                    if j == 1:
                        turn_s.act(act)
                    if j == 2:
                        turn_g.act(act)
                        act.wait_ge(norm.summed, norm.base + NT)
                        norm_m.act(act, before=lambda t: act.wait_ge(m_in[t], 16))
                    for c in range(2):
                        h = 2 * W_AO + 4 * j + 2 * c
                        st.split_hi(act, h + 2)
                        act.wait_ge(oo.ready, NT * (c + 1))
                        st.split_hi(act, h + 3)

            @block.vector
            def _(dve):
                dve.wait_ge(small_in, 48)
                norm.dve(dve, Y, sgn)

                def each(j, oo, use):
                    for c in range(2):
                        h = 2 * W_AO + 4 * j + 2 * c
                        st.split_lo(dve, h + 2)
                        for t in range(NT):
                            n = c * NT + t
                            dve.wait_ge(oo.ready, n + 1)
                            s = NO * j + n
                            dve.wait_ge(side_in[s % RING], 16 * (s // RING + 1))
                            use(oo, n, t, slice(c * CH, (c + 1) * CH), side[:, s % RING, :])
                        st.split_lo(dve, h + 3)

                def gated(oo, n, t, cols, s):
                    dve.tensor_tensor(G[:, t, cols], lin[:, t, :], s, ALU.mult).then_inc(oo.freed, 1)

                def added(oo, n, t, cols, s):
                    dve.tensor_tensor(tmp[:], lin[:, t, :], s, ALU.mult).then_inc(oo.freed, 1)
                    dve.wait_ge(oo.freed, n + 1)
                    dve.tensor_tensor(G[:, t, cols], G[:, t, cols], tmp[:], ALU.add).then_inc(side_used, 1)
                    dve.wait_ge(side_used, n + 1)

                def residual(oo, n, t, cols, s):
                    dve.tensor_tensor(Y[:, t, cols], lin[:, t, :], s, ALU.add).then_inc(oo.freed, 1)

                each(0, o, gated)
                for n, (g, t0, nt) in enumerate(SGP):
                    dve.wait_ge(sg_ready, n + 1)
                    dve.wait_ge(ug_in[g % 2], 16 * (g // 2 + 1))
                    dve.scalar_tensor_tensor(
                        out=Y[:, t0:t0 + nt, g * P:(g + 1) * P], in0=lin[:, n % 6, 0:nt * P].rearrange("p (t f) -> p t f", t=nt),
                        scalar=sgb[:, g:g + 1], in1=ug[:, g % 2, t0:t0 + nt, :], op0=ALU.add, op1=ALU.mult).then_inc(sg_done, 1)
                turn_s.dve(dve)
                each(1, o2, added)
                turn_g.dve(dve)
                norm_m.dve(dve, M)
                each(2, o3, residual)


def cross_inputs(nc, st, T, Y, G, keysT, vals, lin, A, ident, gains):
    with ExitStack() as ctx:
        m = Pool(nc, ctx)
        M = G[:, 0:NM, :]
        norm_x = Norm(nc, ctx, "xa", Y, NT)
        turn_m = Turn(nc, ctx, "memt", M, T, lin, ident, gains[:, 2, :], NM)
        turn_x = Turn(nc, ctx, "xat", G, T, lin, ident, gains[:, 1, :], NT)
        qT = G[:].rearrange("p t d -> p (t d)").rearrange("p (b n) -> p b n", b=KB)
        H0 = 2 * W_XKV
        o_k, o_v, o_q = (Outputs(nc, ctx, x) for x in ("xk", "xv", "xq"))
        MEMS = [(cb, 0, True, cb, slice(0, NM * P), cb + 1) for cb in range(4)]

        with nc.Block() as block:
            @block.sync
            def _(sp):
                st.load(sp, H0 + 2, 2 * W_XO + 2)

            @block.tensor
            def _(pe):
                turn_m.pe(pe)
                turn_m.wait(pe)
                project_features(pe, st, H0, 2, T, MEMS, lin, o_k)
                pe.wait_ge(o_k.freed, 8)
                project_tokens(pe, st, H0 + 4, 2, T, range(NM), lin, o_v)
                pe.wait_ge(o_v.freed, 2 * NM)
                norm_x.wait(pe)
                turn_x.pe(pe)
                turn_x.wait(pe)
                project_features(pe, st, H0 + 8, 2, T, FEATURES, lin, o_q)

            @block.scalar
            def _(act):
                turn_m.act(act)
                norm_x.act(act)
                for c in range(4):
                    o = o_k if c < 2 else o_v
                    st.split_hi(act, H0 + 2 * c + 2)
                    for i in range(4):
                        act.wait_ge(o.ready, 4 * (c % 2) + i + 1)
                        dst = keysT[:, 4 * c + i, :] if c < 2 else vals[:, i, (c - 2) * CH:(c - 1) * CH]
                        act.activation(dst, lin[:, i, :], ACT.Copy).then_inc(o.freed, 1)
                    st.split_hi(act, H0 + 2 * c + 3)
                turn_x.act(act)
                for c in range(2):
                    st.split_hi(act, H0 + 10 + 2 * c)
                    for bank, col, _, cb, cols, need in FEATURES:
                        act.wait_ge(o_q.ready, 8 * c + need)
                        act.activation(qT[:, 4 * c + cb, cols], lin[:, bank, col:col + cols.stop - cols.start],
                                       ACT.Copy).then_inc(o_q.freed, 1)
                    st.split_hi(act, H0 + 11 + 2 * c)

            @block.vector
            def _(dve):
                turn_m.dve(dve)
                norm_x.dve(dve, G)
                for h in range(2, 10):
                    st.split_lo(dve, H0 + h)
                turn_x.dve(dve)
                for h in range(10, 14):
                    st.split_lo(dve, H0 + h)


def cross_attention(nc, T, G, keysT, vals, ident, lin, tr):
    heads = [(s, h) for s in range(NSEQ) for h in range(XH)]
    units = [(s, h, t) for s, h in heads for t in range(SEQS[s][1])]
    qT = G[:].rearrange("p t d -> p (t d)").rearrange("p (b n) -> p b n", b=KB)
    NB = XD // P

    def scores_of(u):
        s, h, t = u
        t += SEQS[s][0]
        return [(qT[:, NB * h + j, t * P:(t + 1) * P], keysT[:, NB * h + j, s * MEM:(s + 1) * MEM]) for j in range(NB)]

    outs = [{"head": i, "bank": NB * i + j, "rows": slice(0, P), "opens": True, "ends": True, "block": NB * h + j,
             "cols": slice(SEQS[s][0] * P, sum(SEQS[s]) * P),
             "values": [vals[:, s * (MEM // P) + kb, (NB * h + j) * P:(NB * h + j + 1) * P] for kb in range(MEM // P)]}
            for i, (s, h) in enumerate(heads) for j in range(NB)]
    attention(nc, "xatt", T, ident, lin, tr, units, heads, outs, lambda u: MEM, scores_of, XD ** -0.5)


def routing(nc, st, T, Y, G, H, E12, GATE, IDX, lin, tr, A, ident, gains):
    with ExitStack() as ctx:
        m = Pool(nc, ctx)
        H0 = 2 * W_XO
        qT = m.sb("peer_qT", [P, 4, TOK])
        norm = Norm(nc, ctx, "ffn", Y, NT, qT[:].rearrange("p a b -> p (a b)")[:, 0:D])
        row = m.sb("ffn_row", [P, D])
        turn = Turn(nc, ctx, "ffnt", G, T, lin, ident, gains[:, 3, :], NT)
        subk = m.sb("subk", [P, 2 * PH, NK])
        iota = m.sb("iota", [P, TOPK])
        LOOK = 2 * 2 * TOPK
        place = m.sb("place", [P, TOPK, LOOK], BF16)
        sc = m.sb("sc", [P, 2, 4, NK])
        left = m.sb("left", [P, 4, NK])
        best, ids = m.sb("best", [P, 2, 4, TOPK]), m.sb("ids", [P, 2, 4, TOPK], U32)
        id_b = m.sb("id_b", [P, 3, 4, TOPK], BF16)
        WIDE = 4
        SPLIT = WIDE * TOPK
        NC = SPLIT + (TOPK - WIDE) * WIDE
        cand, cleft = m.sb("cand", [P, 2, 2, NC]), m.sb("cleft", [P, 2, NC])
        pos, shifted = m.sb("pos", [P, 2, TOPK], U32), m.sb("shifted", [P, 2, 2, TOPK], U32)
        part_b, start = m.sb("part_b", [P, 2, 2, TOPK], BF16), m.sb("start", [P, 2, TOPK])
        pick = m.sb("pick", [P, 2, TOPK, LOOK], BF16)
        gsum = m.sb("gsum", [P, NT * PH])
        small_in, chain, place_done = m.sem("rt_small_in"), m.sem("rt_chain"), m.sem("rt_place_done")
        halved, paired, ids_read, marked, looked_up, adding = (
            m.sem(f"rt_{x}") for x in ("halved", "paired", "ids_read", "marked", "looked_up", "adding"))
        o_x, o_q = Outputs(nc, ctx, "xo"), Outputs(nc, ctx, "pq")
        s_ready, s_copied, s_used, g_shift, g_exp, h_done = (
            m.sem(x) for x in ("s_ready", "s_copied", "s_used", "g_shift", "g_exp", "h_done"))
        NPC = 4
        UNITS = NPC * NT

        with nc.Block() as block:
            @block.sync
            def _(sp):
                st.load(sp, H0 + 2, 2 * W_END)

            @block.gpsimd
            def _(pool):
                for dst, src in ((row[:], A["ffn_row"].broadcast_to((P, D))),
                                 (subk[:], A["subk"]), (iota[:], A["iota"])):
                    pool.dma_start(dst, src).then_inc(small_in, 16)
                pool.wait_ge(small_in, 48)
                pool.tensor_copy(place[:], iota[:].unsqueeze(2).broadcast_to((P, TOPK, LOOK))).then_inc(place_done, 1)
                sums = 0
                for r in range(UNITS + 1):
                    u = r
                    if u < UNITS:
                        pool.wait_ge(halved, u + 1)
                        v = best[:, u % 2].rearrange("p (h s) a -> p h s a", s=2)
                        for cols, aa, bb in ((slice(0, SPLIT), slice(0, WIDE), slice(0, TOPK)),
                                             (slice(SPLIT, NC), slice(WIDE, TOPK), slice(0, WIDE))):
                            shape = (P, 2, aa.stop - aa.start, bb.stop)
                            last = pool.tensor_tensor(cand[:, u % 2, :, cols].rearrange("p h (a b) -> p h a b", b=bb.stop),
                                                      v[:, :, 0, aa].unsqueeze(3).broadcast_to(shape),
                                                      v[:, :, 1, bb].unsqueeze(2).broadcast_to(shape), ALU.add)
                        last.then_inc(paired, 1)
                        pool.tensor_copy(id_b[:, u % 3], ids[:, u % 2]).then_inc(ids_read, 1)
                    u = r - 1
                    if u >= 0:
                        pool.wait_ge(marked, u + 1)
                        pool.wait_ge(ids_read, u + 1)
                        pv = pick[:, u % 2].rearrange("p a (s j) -> p s a j", s=4)
                        pool.tensor_tensor(pv, pv, id_b[:, u % 3].unsqueeze(3).broadcast_to((P, 4, TOPK, TOPK)),
                                           ALU.mult).then_inc(adding, 1)
                        for half in (8, 4, 2):
                            sums += 1
                            pool.wait_ge(adding, sums)
                            pool.tensor_tensor(pick[:, u % 2, 0:half], pick[:, u % 2, 0:half], pick[:, u % 2, half:2 * half],
                                               ALU.add).then_inc(adding, 1)
                        sums += 1
                        pool.wait_ge(adding, sums)
                        c, t = u // NT, u % NT
                        x = pick[:, u % 2].rearrange("p a (h s j) -> p a h s j", h=2, s=2)
                        pool.tensor_tensor(E12[:, t, :, 2 * c * TOPK:2 * (c + 1) * TOPK].rearrange("p s (h j) -> p h s j", h=2),
                                           x[:, 0], x[:, 1], ALU.add).then_inc(looked_up, 1)

            @block.tensor
            def _(pe):
                project_tokens(pe, st, H0, 2, T, range(NT), lin, o_x)

                def normed(n, end):
                    pe.wait_ge(norm.scaled, norm.base + end)
                    if n < NT:
                        pe.wait_ge(o_x.freed, NT + n + 1)
                turn.pe(pe, normed)
                turn.wait(pe)
                pe.wait_ge(small_in, 48)

                def scores(c, t):
                    i = c * NT + t
                    pe.wait_ge(o_q.freed, 8 * (c + 1))
                    if i >= 2:
                        pe.wait_ge(s_copied, i - 1)
                    for j in range(4):
                        last = pe.matmul(tr[:, i % 2, j * NK:(j + 1) * NK], qT[:, j, t * P:(t + 1) * P],
                                         subk[:, 4 * c + j, :], start=True, stop=True)
                    last.then_inc(s_ready, 1)

                def between(c, half, i):
                    if c >= 1 and half == 0 and i < NT:
                        scores(c - 1, i)

                project_features(pe, st, H0 + 4, NPC, T, FEATURES, lin, o_q, between)
                for t in range(NT):
                    scores(NPC - 1, t)

            @block.scalar
            def _(act):
                st.split_hi(act, H0 + 2)
                act.wait_ge(o_x.ready, NT)
                st.split_hi(act, H0 + 3)
                st.split_hi(act, H0 + 4)
                norm.act(act, before=lambda t: act.wait_ge(o_x.freed, NT + t + 1))
                turn.act(act)
                st.split_hi(act, H0 + 5)

                def copy(c):
                    for t in range(NT):
                        i = c * NT + t
                        act.wait_ge(s_ready, i + 1)
                        if i >= 2:
                            act.wait_ge(s_used, i - 1)
                        act.activation(sc[:, i % 2].rearrange("p j k -> p (j k)"), tr[:, i % 2, :], ACT.Copy).then_inc(
                            s_copied, 1)

                for c in range(NPC):
                    if c >= 1:
                        copy(c - 1)
                    st.split_hi(act, H0 + 6 + 2 * c)
                    for bank, col, _, cb, cols, need in FEATURES:
                        act.wait_ge(o_q.ready, 8 * c + need)
                        if c >= 1:
                            act.wait_ge(s_ready, NT * c)
                        act.activation(qT[:, cb, cols], lin[:, bank, col:col + cols.stop - cols.start],
                                       ACT.Copy).then_inc(o_q.freed, 1)
                    st.split_hi(act, H0 + 7 + 2 * c)
                copy(NPC - 1)
                act.wait_ge(g_shift, 1)
                act.activation(GATE[:], GATE[:], ACT.Exp).then_inc(g_exp, 1)

            @block.vector
            def _(dve):
                links = 0

                def link(*instructions):
                    nonlocal links
                    for x in instructions:
                        x.then_inc(chain, 1)
                        links += 1
                    dve.wait_ge(chain, links)

                for c in range(2):
                    st.split_lo(dve, H0 + 2 * c + 2)
                    for t in range(NT):
                        dve.wait_ge(o_x.ready, NT * c + t + 1)
                        cols = slice(c * CH, (c + 1) * CH)
                        dve.tensor_tensor(Y[:, t, cols], lin[:, t, :], Y[:, t, cols], ALU.add).then_inc(o_x.freed, 1)
                        if c == 1 and t >= 1:
                            norm.step(dve, t - 1, G)
                    if c == 0:
                        st.split_lo(dve, H0 + 3)
                norm.step(dve, NT - 1, G)
                norm.step(dve, NT, G)
                turn.dve(dve)
                st.split_lo(dve, H0 + 5)
                dve.wait_ge(small_in, 48)
                for q in range(NG):
                    last = dve.tensor_tensor(H[:, q, :], G[:, ND + q, :], row[:], ALU.mult)
                last.then_inc(h_done, 1)

                def pick_experts(r):
                    rows = []
                    if r < UNITS:
                        dve.wait_ge(s_copied, r + 1)
                        if r >= 2:
                            dve.wait_ge(ids_read, r - 1)
                        rows += [(best[:, r % 2, j, :], ids[:, r % 2, j, :], sc[:, r % 2, j, :], left[:, j, :])
                                 for j in range(4)]
                    ones = len(rows)
                    if r >= 1:
                        c, t = (r - 1) // NT, (r - 1) % NT
                        rows += [(GATE[:, t, (2 * c + h) * TOPK:(2 * c + h + 1) * TOPK], pos[:, h, :],
                                  cand[:, (r - 1) % 2, h, :], cleft[:, h, :]) for h in range(2)]
                    for n, (v, i, src, rest) in enumerate(rows):
                        if n == ones:
                            dve.wait_ge(paired, r)
                        last = dve.max(v[:, 0:8], src)
                    link(last)
                    for v, i, src, rest in rows:
                        dve.max_index(i[:, 0:8], v[:, 0:8], src)
                        last = dve.match_replace(rest, v[:, 0:8], src, LOWEST)
                    link(last)
                    for n, (v, i, src, rest) in enumerate(rows):
                        last = dve.max(v[:, 8:16], rest)
                        if n == 0 and r < UNITS:
                            last.then_inc(s_used, 1)
                    link(last)
                    for n, (v, i, src, rest) in enumerate(rows):
                        last = dve.max_index(i[:, 8:16], v[:, 8:16], rest)
                        if n == ones - 1:
                            last.then_inc(halved, 1)
                    if len(rows) > ones:
                        link(last)
                    else:
                        dve.wait_ge(halved, r + 1)
                    if r >= 1:
                        u = r - 1
                        dve.tensor_scalar(shifted[:, 0], pos[:], 4, None, ALU.logical_shift_right)
                        link(dve.tensor_scalar(shifted[:, 1], pos[:], 2, None, ALU.logical_shift_right))
                        a_, b_ = part_b[:, :, 0, :], part_b[:, :, 1, :]
                        skip = SPLIT - WIDE * WIDE
                        link(dve.scalar_tensor_tensor(out=a_, in0=shifted[:, 1], scalar=float(-skip // WIDE),
                                                      in1=shifted[:, 0], op0=ALU.add, op1=ALU.max))
                        link(dve.tensor_scalar(start[:], a_, float(WIDE), float(skip), ALU.mult, ALU.add))
                        link(dve.scalar_tensor_tensor(out=start[:], in0=a_, scalar=float(TOPK), in1=start[:],
                                                      op0=ALU.mult, op1=ALU.min))
                        link(dve.scalar_tensor_tensor(out=b_, in0=pos[:], scalar=0.0, in1=start[:], op0=ALU.add,
                                                      op1=ALU.subtract))
                        if u == 0:
                            dve.wait_ge(place_done, 1)
                        if u >= 2:
                            dve.wait_ge(looked_up, u - 1)
                        dve.tensor_tensor(pick[:, u % 2], part_b[:].rearrange("p h s j -> p (h s j)").unsqueeze(1).broadcast_to(
                            (P, TOPK, LOOK)), place[:], ALU.is_equal).then_inc(marked, 1)
                        dve.wait_ge(marked, u + 1)

                for c in range(NPC):
                    if c >= 1:
                        for t in range(NT - 2):
                            pick_experts((c - 1) * NT + t)
                    st.split_lo(dve, H0 + 6 + 2 * c)
                    if c >= 1:
                        for t in range(NT - 2, NT):
                            pick_experts((c - 1) * NT + t)
                    st.split_lo(dve, H0 + 7 + 2 * c)
                for r in range((NPC - 1) * NT, UNITS + 1):
                    pick_experts(r)
                g = GATE[:].rearrange("p t (h j) -> p (t h) j", j=TOPK)
                dve.tensor_copy(gsum[:], g[:, :, 0]).then_inc(chain, 1)
                links += 1
                dve.wait_ge(chain, links)
                dve.tensor_tensor(g, g, gsum[:].unsqueeze(2).broadcast_to((P, NT * PH, TOPK)), ALU.subtract).then_inc(g_shift, 1)
                dve.wait_ge(g_exp, 1)
                link(dve.tensor_reduce(gsum[:], g, AX_X, ALU.add))
                link(dve.reciprocal(gsum[:], gsum[:]))
                link(dve.tensor_tensor(g, g, gsum[:].unsqueeze(2).broadcast_to((P, NT * PH, TOPK)), ALU.mult))
                dve.wait_ge(looked_up, UNITS)
                link(*[dve.scalar_tensor_tensor(out=IDX[:, :, q], in0=E12[:, ND + q, 0, :], scalar=float(NK),
                                                in1=E12[:, ND + q, 1, :], op0=ALU.mult, op1=ALU.add) for q in range(NG)])
                dve.wait_ge(h_done, 1)


class ExpertBuffers:

    def __init__(self, nc, ctx):
        m = Pool(nc, ctx)
        shared = m.sb("shared", [P, 2 * NK * WT])
        self.stage = shared[:].rearrange("p (s e t) -> p s e t", s=2, e=NK)
        sizes = {"raw_d": 2 * KB * P, "raw_u": 2 * D, "wd": SAMPLE * BG, "gl": BG * SAMPLE}
        at, views = 0, {}
        for name, n in sizes.items():
            views[name] = shared[:, at:at + n]
            at += n
        assert at <= NK * WT
        self.raw_d = views["raw_d"].rearrange("p (i k e) -> p i k e", i=2, k=KB)
        self.raw_u = views["raw_u"].rearrange("p (i f) -> p i f", i=2)
        self.wd = views["wd"].rearrange("p (h e t) -> p h e t", e=BG, t=WT)
        self.gl = views["gl"].rearrange("p (b n) -> p b n", b=BG)
        self.rows = shared[:, NK * WT:].rearrange("p (k f) -> p k f", f=D)
        self.stored = [m.sem(f"dg_stored{i}") for i in range(2)]
        self.d_in = [m.sem(f"ex_d_in{i}") for i in range(2)]
        self.u_in = [m.sem(f"ex_u_in{i}") for i in range(2)]


def dense_gates(nc, ex, E12, GATE, WD, lin, tr, A, ident):
    with ExitStack() as ctx:
        m = Pool(nc, ctx)
        keys = m.sb("keys", [P, NK])
        pairs = m.sb("pairs", [P, 3, SAMPLE])
        SLOTS = 16
        hot1, hot2 = m.sb("hot1", [P, SLOTS, NK]), m.sb("hot2", [P, SLOTS, NK])
        away = m.sb("away", [P, 2, NK])
        one = m.sb("one", [P, 1])
        now = m.sb("dg_now", [P, P // 4, 2])
        stage, stored = ex.stage, ex.stored
        QUADS = P // 4
        keys_in, one_set, turned, copied = (m.sem(f"dg_{x}") for x in ("keys_in", "one_set", "turned", "copied"))
        hot_dve, hot_act, hot_pool, bank_free, bank_ready, now_in, aways = (
            m.sem(f"dg_{x}") for x in ("hot_dve", "hot_act", "hot_pool", "bank_free", "bank_ready", "now_in", "aways"))

        with nc.Block() as block:
            @block.sync
            def _(sp):
                sp.dma_start(keys[:], A["keys"]).then_inc(keys_in, 16)

                def store(i, s):
                    sp.wait_ge(bank_free, i * QUADS + 4 + 16 * (s + 1))
                    n = i * 2 + s
                    sp.dma_start(WD[bass.ds(n, 1)].rearrange("a p e t -> p (a e t)"),
                                 stage[:, s].rearrange("p e t -> p (e t)")).then_inc(stored[s], 16)

                with sp.Fori(0, ND - 1) as i:
                    store(i, 0)
                    store(i, 1)
                store(ND - 1, 0)
                sp.wait_ge(stored[0], 16 * ND + 16)
                for b in range(2):
                    sp.dma_start(ex.raw_d[:, b], A["downT"][b]).then_inc(ex.d_in[b], 16)
                for b in range(2):
                    sp.dma_start(ex.raw_u[:, b], A["up"][b * P:(b + 1) * P, :]).then_inc(ex.u_in[b], 16)
                store(ND - 1, 1)

            @block.tensor
            def _(pe):
                for j in range(3):
                    for t in range(ND):
                        src = GATE[:, t, :] if j == 2 else E12[:, t, j, :]
                        last = pe.transpose(lin[:, j, t * P:(t + 1) * P], src, ident[:])
                    last.then_inc(turned, 1)
                pe.wait_ge(copied, 3)
                with pe.Fori(0, ND) as i:
                    for q in range(QUADS):
                        pe.wait_ge(hot_dve, i * QUADS + q + 1)
                        if q % 2 == 0:
                            pe.wait_ge(hot_act, i * (QUADS // 2) + q // 2 + 2)
                        pe.wait_ge(hot_pool, i * QUADS + q + 2)
                        pe.wait_ge(bank_free, i * QUADS + q + 1)
                        for n in range(4):
                            slot = (4 * q + n) % SLOTS
                            last = pe.matmul(lin[:, q % 4, n * NK:(n + 1) * NK], hot2[:, slot, :], hot1[:, slot, :],
                                             start=True, stop=True)
                        last.then_inc(bank_ready, 1)

            @block.scalar
            def _(act):
                for j in range(3):
                    act.wait_ge(turned, j + 1)
                    act.activation(pairs[:, j, :], lin[:, j, :], ACT.Copy).then_inc(copied, 1)
                act.wait_ge(copied, 3)
                act.sem_inc(bank_free, 4)
                act.sem_inc(bank_ready, 4)
                for s in range(2):
                    act.sem_inc(stored[s], 16)
                act.wait_ge(keys_in, 16)
                act.wait_ge(one_set, 1)

                def hot(i, r):
                    act.wait_ge(hot_act, i * (QUADS // 2) + r + 1)
                    act.nop(nofuse=True)
                    for x in range(2):
                        last = act.activation(away[:, x, :], keys[:], ACT.Abs, scale=-1.0,
                                              bias=pairs[:, 1, bass.ds(i * P + 8 * r + 4 * x + 1, 1)])
                    last.then_inc(aways, 1)
                    act.wait_ge(bank_ready, i * QUADS + 2 * r + 2)
                    act.wait_ge(aways, i * (QUADS // 2) + r + 1)
                    slot = 8 * r % SLOTS + 1
                    act.activation(hot2[:, slot:slot + 5:4, :], away[:], ACT.Relu, scale=-1.0, bias=one[:]).then_inc(hot_act, 1)

                def copy(i, q):
                    s = q // 16
                    if q % 16 == 0:
                        act.wait_ge(stored[s], i * 16 + 16)
                    act.wait_ge(bank_ready, i * QUADS + q + 5)
                    t0 = 4 * (q % 16)
                    act.activation(stage[:, s, :, t0:t0 + 4].rearrange("p e t -> p t e"),
                                   lin[:, q % 4, :].rearrange("p (t e) -> p t e", t=4), ACT.Copy).then_inc(bank_free, 1)

                act.sem_inc(hot_act, 1)
                with act.Fori(0, ND) as i:
                    hot(i, 0)
                    for r in range(QUADS // 2):
                        if r + 1 < QUADS // 2:
                            hot(i, r + 1)
                        copy(i, 2 * r)
                        copy(i, 2 * r + 1)

            @block.gpsimd
            def _(pool):
                pool.wait_ge(keys_in, 16)
                pool.wait_ge(copied, 3)
                pool.sem_inc(hot_pool, 1)
                with pool.Fori(0, ND) as i:
                    pool.wait_ge(hot_pool, i * QUADS + 1)
                    pool.nop(nofuse=True)
                    pool.tensor_copy(now[:], pairs[:, 1, bass.ds(i * P, P)].rearrange("p (q n) -> p q n", n=4)[:, :, 2:4]).then_inc(
                        now_in, 1)
                    pool.wait_ge(now_in, i + 1)
                    for q in range(QUADS):
                        pool.wait_ge(bank_ready, i * QUADS + q + 1)
                        pool.nop(nofuse=True)
                        for n in range(2, 4):
                            last = pool.tensor_scalar(hot2[:, (4 * q + n) % SLOTS, :], keys[:], now[:, q, n - 2:n - 1], None,
                                                      ALU.is_equal)
                        last.then_inc(hot_pool, 1)

            @block.vector
            def _(dve):
                dve.memset(one[:], 1.0).then_inc(one_set, 1)
                dve.wait_ge(keys_in, 16)
                dve.wait_ge(copied, 3)
                with dve.Fori(0, ND) as i:
                    for q in range(QUADS):
                        dve.wait_ge(bank_ready, i * QUADS + q + 1)
                        for n in range(4):
                            col = i * P + (4 * q + n)
                            last = dve.tensor_scalar(hot1[:, (4 * q + n) % SLOTS, :], keys[:], pairs[:, 0, bass.ds(col, 1)],
                                                     pairs[:, 2, bass.ds(col, 1)], ALU.is_equal, ALU.mult)
                            if n == 0:
                                dve.tensor_scalar(hot2[:, (4 * q) % SLOTS, :], keys[:], pairs[:, 1, bass.ds(col, 1)], None,
                                                  ALU.is_equal)
                        last.then_inc(hot_dve, 1)


def experts(nc, ex, T, Y, H, IDX, GATE, WD, lin, tr, A):
    with ExitStack() as ctx:
        m = Pool(nc, ctx)
        raw_d, raw_u, wd, gl, rows, d_in, u_in = ex.raw_d, ex.raw_u, ex.wd, ex.gl, ex.rows, ex.d_in, ex.u_in
        d_hi, d_lo = m.sb("d_hi", [P, 2, KB, P], F32R), m.sb("d_lo", [P, 2, KB, P], F32R)
        u_hi, u_lo = m.sb("u_hi", [P, BG, D], F32R), m.sb("u_lo", [P, BG, D], F32R)
        c_hi, c_lo = m.sb("c_hi", [P, BG, SAMPLE], F32R), m.sb("c_lo", [P, BG, SAMPLE], F32R)
        now = m.sb("now", [P, 2, 8], I32)
        dots_now = m.sb("dots_now", [P, 16])
        dots = m.sb("dots", [P, NE * NG])
        w_in = m.sem("ex_w_in")
        d_hid, d_lod, u_hid, u_lod, act_ready, gelued, weighted, c_hid, c_lod, y_ready, y_added = (
            m.sem(f"ex_{x}") for x in ("d_hi", "d_lo", "u_hi", "u_lo", "act_ready", "gelued", "weighted", "c_hi",
                                       "c_lo", "y_ready", "y_added"))
        rows_in = [m.sem(f"ex_row_in{i}") for i in range(8)]
        rows_free, dots_done, coef_gelu, coef_done, now_done = (
            m.sem(f"ex_{x}") for x in ("rows_free", "dots_done", "coef_gelu", "coef_done", "now_done"))
        HALF = NGRP // 2

        def first_group(g):
            return isinstance(g, int) and g == 0

        def groups(eng, body):
            body(0, "down", False)
            with eng.Fori(1, HALF) as g:
                body(g, "down", False)
            between = between_halves.get(eng)
            if between:
                between()
            with eng.Fori(HALF, NGRP - 1) as g:
                body(g, "up", False)
            body(NGRP - 1, "up", True)

        between_halves = {}

        with nc.Block() as block:
            @block.sync
            def _(sp):
                def load_d(g, b):
                    n = g * BG + b
                    if not (isinstance(g, int) and n < 2):
                        sp.wait_ge(d_lod, n - 1)
                    sp.dma_start(raw_d[:, b % 2], A["downT"][n] if isinstance(g, int) else
                                 A["downT"][bass.ds(n, 1)].rearrange("a p k e -> p (a k) e")).then_inc(d_in[b % 2], 16)

                def load_u(g, b):
                    n = g * BG + b
                    if not (isinstance(g, int) and n < 2):
                        sp.wait_ge(u_lod, n - 1)
                    sp.dma_start(raw_u[:, b % 2], A["up"][bass.ds(n * P, P), :]).then_inc(u_in[b % 2], 16)

                def body(g, kind, last):
                    if first_group(g):
                        load_d(g, 2)
                        load_d(g, 3)
                        sp.wait_ge(ex.stored[1], 16 * ND + 16)
                    else:
                        load_d(g, 0)
                        load_d(g, 1)
                        load_u(g, 0)
                        load_u(g, 1)
                        sp.wait_ge(weighted, g * BG)
                    sp.dma_start(wd.rearrange("p h e t -> p h (e t)"),
                                 WD[:, :, bass.ds(g * BG, BG), :].rearrange("h p e t -> p h (e t)")).then_inc(w_in, 16)
                    if not first_group(g):
                        load_d(g, 2)
                        load_d(g, 3)
                    load_u(g, 2)
                    load_u(g, 3)

                groups(sp, body)

            @block.gpsimd
            def _(pool):
                pool.wait_ge(w_in, 16)

                def coef_lo(g, b):
                    pool.wait_ge(c_hid, g * BG + b + 1)
                    pool.tensor_tensor(c_lo[:, b, :], gl[:, b, :], c_hi[:, b, :].bitcast(F32), ALU.subtract).then_inc(c_lod, 1)

                def body(g, kind, last):
                    table = A["down"] if kind == "down" else A["up"]
                    first = g * 16 if kind == "down" else g * 16 - NE * NG
                    for j in range(2):
                        pool.wait_ge(rows_free, g * 16 + 8 * j + 1)
                        pool.tensor_copy(now[:, j, :], IDX[:].rearrange("p s q -> p (s q)")[:, bass.ds(first + 8 * j, 8)]).then_inc(
                            now_done, 1)
                        pool.wait_ge(now_done, g * 2 + j + 1)
                        for k in range(8):
                            pool.wait_ge(rows_free, g * 16 + 8 * j + k + 1)
                            pool.nop(nofuse=True)
                            pool.indirect_dma_start(rows[:, k, :], None, table, bass.IndirectOffsetOnAxis(
                                ap=now[:, j, k:k + 1], axis=0)).then_inc(rows_in[k], 16)
                            if j == 1 and k % 2 == 1:
                                coef_lo(g, k // 2)

                groups(pool, body)

            @block.tensor
            def _(pe):
                def body(g, kind, last):
                    for b in range(BG):
                        pe.wait_ge(d_lod, g * BG + b + 1)
                        if b >= 2:
                            pe.wait_ge(gelued, g * BG + b - 1)
                        for k in range(KB):
                            mm = three(pe, tr[:, b % 2, :], (d_hi[:, b % 2, k, :], d_lo[:, b % 2, k, :]),
                                       (T[0][0][:, k, :], T[1][0][:, k, :]), start=(k == 0), stop=(k == KB - 1))
                        mm.then_inc(act_ready, 1)
                    if not first_group(g):
                        pe.wait_ge(y_added, g * 8)
                    for half in range(2):
                        cols = slice(half * CH, (half + 1) * CH)
                        for b in range(BG):
                            if half == 0:
                                pe.wait_ge(c_lod, g * BG + b + 1)
                                pe.wait_ge(u_lod, g * BG + b + 1)
                            for t in range(ND):
                                if half == 1 and b == 0 and t >= 2:
                                    pe.wait_ge(y_added, g * 8 + t - 1)
                                ts = slice(t * P, (t + 1) * P)
                                mm = three(pe, lin[:, (4 * half + t) % 6, :], (c_hi[:, b, ts], c_lo[:, b, ts]),
                                           (u_hi[:, b, cols], u_lo[:, b, cols]), start=(b == 0), stop=(b == BG - 1))
                                if b == BG - 1:
                                    mm.then_inc(y_ready, 1)

                groups(pe, body)

            @block.scalar
            def _(act):
                def down_hi(g, b):
                    act.wait_ge(d_in[b % 2], g * 32 + (b // 2 + 1) * 16)
                    act.activation(d_hi[:, b % 2], raw_d[:, b % 2], ACT.Copy).then_inc(d_hid, 1)

                def up_hi(g, b):
                    act.wait_ge(u_in[b % 2], g * 32 + (b // 2 + 1) * 16)
                    act.activation(u_hi[:, b], raw_u[:, b % 2], ACT.Copy).then_inc(u_hid, 1)

                def gelu(g, b):
                    act.wait_ge(act_ready, g * BG + b + 1)
                    if not first_group(g):
                        act.wait_ge(c_lod, g * BG + b - 3)
                    act.activation(gl[:, b, :], tr[:, b % 2, :], ACT.Gelu_apprx_tanh).then_inc(gelued, 1)

                def coef_hi(g, b):
                    act.wait_ge(weighted, g * BG + b + 1)
                    act.activation(c_hi[:, b, :], gl[:, b, :], ACT.Copy).then_inc(c_hid, 1)

                def body(g, kind, last):
                    if not first_group(g):
                        act.wait_ge(y_ready, g * 8)
                    for b in range(BG):
                        if b >= 1:
                            gelu(g, b - 1)
                            if b + 1 < BG:
                                down_hi(g, b + 1)
                        up_hi(g, b)
                        if b >= 1:
                            coef_hi(g, b - 1)
                    gelu(g, BG - 1)
                    coef_hi(g, BG - 1)
                    if not last:
                        down_hi(g + 1, 0)
                        down_hi(g + 1, 1)

                def between():
                    act.wait_ge(dots_done, HALF)
                    act.activation(dots[:], dots[:], ACT.Gelu_apprx_tanh).then_inc(coef_gelu, 1)

                between_halves[act] = between
                down_hi(0, 0)
                down_hi(0, 1)
                groups(act, body)

            @block.vector
            def _(dve):
                dve.memset(dots_now[:], 0.0).then_inc(rows_free, 8)

                def down_lo(g, b):
                    dve.wait_ge(d_hid, g * BG + b + 1)
                    dve.tensor_tensor(d_lo[:, b % 2], raw_d[:, b % 2], d_hi[:, b % 2].bitcast(F32),
                                      ALU.subtract).then_inc(d_lod, 1)

                def up_lo(g, b):
                    dve.wait_ge(u_hid, g * BG + b + 1)
                    dve.tensor_tensor(u_lo[:, b], raw_u[:, b % 2], u_hi[:, b].bitcast(F32),
                                      ALU.subtract).then_inc(u_lod, 1)

                def weigh(g, b):
                    dve.wait_ge(gelued, g * BG + b + 1)
                    if b == 0:
                        dve.wait_ge(w_in, g * 16 + 16)
                    v = gl[:, b, :].rearrange("p (h t) -> p h t", t=WT)
                    dve.tensor_tensor(v, v, wd[:, :, b, :], ALU.mult).then_inc(weighted, 1)

                def add(g, half, t):
                    cols = slice(half * CH, (half + 1) * CH)
                    dve.wait_ge(y_ready, g * 8 + 4 * half + t + 1)
                    dve.tensor_tensor(Y[:, t, cols], lin[:, (4 * half + t) % 6, :], Y[:, t, cols], ALU.add).then_inc(y_added, 1)

                def row(g, kind, n):
                    j, k = n // 8, n % 8
                    dve.wait_ge(rows_in[k], g * 32 + 16 * (j + 1))
                    q = k % 2
                    if kind == "down":
                        if n == 0 and not first_group(g):
                            dve.wait_ge(dots_done, g)
                        dve.tensor_tensor_reduce(rows[:, k, :], rows[:, k, :], H[:, q, :], 1.0, 0.0, ALU.mult, ALU.add,
                                                 dots_now[:, n:n + 1]).then_inc(rows_free, 1)
                        if n == 15:
                            dve.wait_ge(rows_free, g * 16 + 16 + 8)
                            dve.tensor_copy(dots[:, bass.ds(g * 16, 16)], dots_now[:]).then_inc(dots_done, 1)
                    else:
                        dve.wait_ge(rows_free, g * 16 + n + 7)
                        dve.scalar_tensor_tensor(out=Y[:, ND + q, :], in0=rows[:, k, :],
                                                 scalar=dots[:, bass.ds(g * 16 - NE * NG + n, 1)], in1=Y[:, ND + q, :],
                                                 op0=ALU.mult, op1=ALU.add).then_inc(rows_free, 1)

                def body(g, kind, last):
                    n = 0
                    for b in range(BG):
                        if b >= 1:
                            weigh(g, b - 1)
                            if b + 1 < BG:
                                down_lo(g, b + 1)
                        up_lo(g, b)
                        row(g, kind, n)
                        row(g, kind, n + 1)
                        n += 2
                    weigh(g, BG - 1)
                    if not last:
                        down_lo(g + 1, 0)
                        down_lo(g + 1, 1)
                    for _ in range(4):
                        row(g, kind, n)
                        n += 1
                    for t in range(ND):
                        add(g, 0, t)
                    for _ in range(4):
                        row(g, kind, n)
                        n += 1
                    for t in range(ND):
                        add(g, 1, t)

                def between():
                    dve.wait_ge(coef_gelu, 1)
                    dve.tensor_tensor(dots[:].rearrange("p (s q) -> p q s", q=NG), dots[:].rearrange("p (s q) -> p q s", q=NG),
                                      GATE[:, ND:, :], ALU.mult).then_inc(coef_done, 1)
                    dve.wait_ge(coef_done, 1)

                between_halves[dve] = between
                down_lo(0, 0)
                down_lo(0, 1)
                groups(dve, body)


def final_norm(nc, Y, A, outs):
    with ExitStack() as ctx:
        m = Pool(nc, ctx)
        norm = Norm(nc, ctx, "final", Y, NT)
        row = m.sb("final_row", [P, D])
        row_in, stored = m.sem("final_row_in"), m.sem("stored")

        with nc.Block() as block:
            @block.sync
            def _(sp):
                sp.dma_start(row[:], A["final_row"].broadcast_to((P, D))).then_inc(row_in, 16)
                for t in range(NT):
                    sp.wait_ge(norm.scaled, norm.base + t + 1)
                    out, tt = (outs[0], t) if t < ND else (outs[1], t - ND)
                    sp.dma_start(out[tt * P:(tt + 1) * P, :], Y[:, t, :]).then_inc(stored, 16)
                sp.wait_ge(stored, 16 * NT)

            @block.scalar
            def _(act):
                norm.act(act)

            @block.vector
            def _(dve):
                dve.wait_ge(row_in, 16)
                norm.dve(dve, Y, row)


def layer(nc, A, outs):
    U, GA, GS = (nc.dram_tensor(x, (NT, P, D), F32).ap() for x in ("u_rows", "attn_gate_rows", "sg_gate_rows"))
    WD = nc.dram_tensor("dense_gates", (SAMPLE // WT, P, NK, WT), F32).ap()
    with ExitStack() as ctx:
        Pool.begin(ctx)
        m = Pool(nc, ctx)
        lin = ctx.enter_context(nc.psum_tensor("lin", [P, 6, CH], F32))
        tr = ctx.enter_context(nc.psum_tensor("tr", [P, 2, CH], F32))
        Y = m.sb("Y", [P, NT, D])
        GATE, IDX, H = m.sb("GATE", [P, NT, NE]), m.sb("IDX", [P, NE, NG], I32), m.sb("H", [P, NG, D])
        T_s = m.sb("Ts_hi", [P, KB, SAMPLE], F32R), m.sb("Ts_lo", [P, KB, SAMPLE], F32R)
        ident, E12 = m.sb("ident", [P, P]), m.sb("E12", [P, NT, 2, NE])
        with ExitStack() as c1:
            n = Pool(nc, c1)
            T_p = n.sb("Tp_hi", [P, KB, PROMPT], F32R), n.sb("Tp_lo", [P, KB, PROMPT], F32R)
            T = (T_s[0], T_p[0]), (T_s[1], T_p[1])
            gains = n.sb("gains", [P, 4, KB])
            st = Stream(nc, c1, A["wall"])
            G = n.sb("G", [P, NT, D])
            with ExitStack() as c2:
                k = Pool(nc, c2)
                qT = G[:].rearrange("p t d -> p (t d)").rearrange("p (b n) -> p b n", b=KB)
                kT, v_sb = k.sb("kT", [P, NKV, TOK]), k.sb("v_sb", [P, NT, NKV * HD])
                mixer_inputs(nc, st, T, Y, qT, kT, v_sb, lin, tr, A, U, GA, GS, ident, gains)
                self_attention(nc, T, qT, kT, v_sb, ident, lin, tr)
            mixer_outputs(nc, st, T, Y, G, lin, A, U, GA, GS, ident)
            with ExitStack() as c2:
                k = Pool(nc, c2)
                keysT, vals = k.sb("keysT", [P, KB, NM * P]), k.sb("vals", [P, NM, D])
                cross_inputs(nc, st, T, Y, G, keysT, vals, lin, A, ident, gains)
                cross_attention(nc, T, G, keysT, vals, ident, lin, tr)
            routing(nc, st, T, Y, G, H, E12, GATE, IDX, lin, tr, A, ident, gains)
        ex = ExpertBuffers(nc, ctx)
        dense_gates(nc, ex, E12, GATE, WD, lin, tr, A, ident)
        experts(nc, ex, T, Y, H, IDX, GATE, WD, lin, tr, A)
        final_norm(nc, Y, A, outs)


def rope_tables():
    nf = HD // 4
    pos = np.arange(SAMPLE)
    inv = (np.float32(10000.0) ** (-np.arange(nf, dtype=np.float32) / np.float32(nf))).astype(np.float32)
    ar = (pos // 64).astype(np.float32)[:, None] * inv
    ac = (pos % 64).astype(np.float32)[:, None] * inv
    cos = np.concatenate([np.cos(ar), np.cos(ar), np.cos(ac), np.cos(ac)], 1)
    sin = np.concatenate([-np.sin(ar), np.sin(ar), -np.sin(ac), np.sin(ac)], 1)
    return [np.ascontiguousarray(a.reshape(4, P, HD).transpose(1, 0, 2)).astype(np.float32) for a in (cos, sin)]


def chunks_of(w):
    return w.reshape(2, HK, P, -1, CH).transpose(3, 2, 0, 1, 4)


def kernel(**inputs):
    import concourse.bacc as bacc
    from concourse.bass_utils import run_bass_kernel_spmd as run

    a = {k: np.asarray(v) for k, v in inputs.items()}
    w_in = chunks_of(a["w_in"][0])
    wall = np.concatenate([w_in[2:3], w_in[0:2], w_in[3:]] + [chunks_of(a[x][0]) for x in (
        "w_attn_o", "w_sg_o", "w_out", "wkv_xa", "wq_xa", "wo_xa", "w_peer_q")])
    assert wall.shape[0] == W_END
    cos, sin = rope_tables()
    arrays = {
        "x": np.concatenate([a["x_sample"][0], a["x_prompt"][0]]),
        "mem": np.concatenate([a["mem_sample"][0], a["mem_prompt"][0]]),
        "wall": wall,
        "gains": np.stack([a[x][0].reshape(KB, P).T for x in ("norm_mix_g", "norm_xa_g", "norm_mem_g", "norm_ffn_g")], 1),
        "cos": cos, "sin": sin, "qg": a["q_norm_g"], "kg": a["k_norm_g"],
        "ident": np.eye(P, dtype=np.float32),
        "iota": np.broadcast_to(np.arange(TOPK, dtype=np.float32), (P, TOPK)),
        "sg_gain": a["sg_norm_g"], "sgw": a["sg_w"][0].transpose(2, 0, 1), "sgb": a["sg_b"][0].T,
        "ffn_row": a["norm_ffn_g"], "final_row": a["final_norm_g"][None],
        "subk": np.stack([a["peer_k1"][0], a["peer_k2"][0]], 1).transpose(3, 0, 1, 2).reshape(P, 2 * PH, NK),
        "keys": np.broadcast_to(np.arange(NK, dtype=np.float32), (P, NK)),
        "downT": a["expert_down"][0].reshape(NK, P, KB, P).transpose(0, 3, 2, 1),
        "down": a["expert_down"][0], "up": a["expert_up"][0],
    }
    arrays = {k: np.ascontiguousarray(v) for k, v in arrays.items()}
    nc = bacc.Bacc("TRN2", target_bir_lowering=False, num_devices=1)
    A = {k: nc.dram_tensor(f"in_{k}", v.shape, mybir.dt.from_np(v.dtype), kind="ExternalInput").ap()
         for k, v in arrays.items()}
    outs = [nc.dram_tensor(f"out_{n}", (s, D), F32, kind="ExternalOutput").ap()
            for n, s in (("sample", SAMPLE), ("prompt", PROMPT))]
    layer(nc, A, outs)
    r = run(nc, [{f"in_{k}": v for k, v in arrays.items()}], core_ids=[0])
    got = [r.results[0][f"out_{n}"] for n in ("sample", "prompt")]
    return got[1].reshape(1, PROMPT, D), got[0].reshape(1, SAMPLE, D)
```
